# Optimizing a Trainium2 kernel written in Bass

```python
import jax, jax.numpy as jnp
from jax import lax
import numpy as np

D_MODEL = 1024
BATCH = 1
SEQ = 256
DEPTH = 2
DEC_BATCH = 1
DEC_SEQ = 256
PAST_LEN = 128

SSD_EXPAND = 2
D_INNER = SSD_EXPAND * D_MODEL
SSD_HEAD_DIM = 64
SSD_HEADS = D_INNER // SSD_HEAD_DIM
SSD_GROUPS = 8
SSD_STATE = 128
SSD_CHUNK = 128
D_CONV = 5
GN = SSD_GROUPS * SSD_STATE
CONV_DIM = D_INNER + 2 * GN
ATTN_HEAD_DIM = 64
HEADS_PER_GROUP = 8
DILATION_GROUPS = ((128, 1), (512, 4), (2048, 16))
ATTN_HEADS = HEADS_PER_GROUP * len(DILATION_GROUPS)
ATTN_WIDTH = ATTN_HEADS * ATTN_HEAD_DIM
ATTN_OUT_WIDTH = HEADS_PER_GROUP * ATTN_HEAD_DIM
REL_BUCKETS = 32
REL_MAX_DISTANCE = 1024
PEER_HEADS = 8
PEER_N_KEYS = 128
PEER_EXPERTS = PEER_N_KEYS * PEER_N_KEYS
PEER_KEY_DIM = 256
PEER_HALF = PEER_KEY_DIM // 2
PEER_TOPK = 16
PEER_TOKEN_BLOCK = 128
RMS_EPS = 1e-6

OFF_XBC = D_INNER
OFF_DT = OFF_XBC + CONV_DIM
OFF_Q = OFF_DT + 2 * SSD_HEADS
OFF_K = OFF_Q + ATTN_WIDTH
OFF_V = OFF_K + ATTN_WIDTH
OFF_GATE = OFF_V + ATTN_WIDTH
IN_COLS = OFF_GATE + 2 * D_MODEL

kernel_name = 'hybrid_ssd_dilated_attn_peer_encoder'

def rms_norm(x, w):
    xf = x.astype(jnp.float32)
    y = xf * lax.rsqrt(jnp.mean(xf * xf, axis=-1, keepdims=True) + RMS_EPS)
    return (y * w.astype(jnp.float32)).astype(x.dtype)

def t5_bucket(rel):
    half = REL_BUCKETS // 2
    max_exact = half // 2
    n = np.abs(rel)
    large = max_exact + (np.log(np.maximum(n, 1) / max_exact) / np.log(REL_MAX_DISTANCE / max_exact) * (half - max_exact)).astype(np.int32)
    large = np.minimum(large, half - 1)
    return np.where(rel > 0, half, 0) + np.where(n < max_exact, n, large)

def ssd_chunked(x, dt, A, B, C):
    b, L, H, P = x.shape
    G, N = B.shape[2], B.shape[3]
    R = H // G
    Q = SSD_CHUNK
    c = L // Q
    xg = (x * dt[..., None]).reshape(b, c, Q, G, R, P)
    Acs = jnp.cumsum((dt * A).reshape(b, c, Q, G, R), axis=2)
    Bc = B.reshape(b, c, Q, G, N)
    Cc = C.reshape(b, c, Q, G, N)
    tril = np.tril(np.ones((Q, Q), dtype=bool))[:, :, None, None]
    seg = jnp.exp(jnp.where(tril, Acs[:, :, :, None] - Acs[:, :, None, :], -jnp.inf))
    CB = jnp.einsum('bclgn,bcsgn->bclsg', Cc, Bc)
    y_diag = jnp.einsum('bclsgr,bcsgrp->bclgrp', CB[..., None] * seg, xg)
    decay_states = jnp.exp(Acs[:, :, -1:] - Acs)
    states = jnp.einsum('bclgn,bclgr,bclgrp->bcgrpn', Bc, decay_states, xg)
    chunk_decay = jnp.exp(Acs[:, :, -1])

    def step(h, inp):
        st, dec = inp
        return h * dec[..., None, None] + st, h

    h0 = jnp.zeros((b, G, R, P, N), jnp.float32)
    _, prev = lax.scan(step, h0, (jnp.moveaxis(states, 1, 0), jnp.moveaxis(chunk_decay, 1, 0)))
    prev = jnp.moveaxis(prev, 0, 1)
    y_off = jnp.einsum('bclgn,bcgrpn,bclgr->bclgrp', Cc, prev, jnp.exp(Acs))
    return (y_diag + y_off).reshape(b, L, H, P)

def ssd_branch(z, xbc, dt_raw, conv_w, conv_b, A_log, dt_bias, D_skip, norm_w):
    b, L, _ = xbc.shape
    pad = D_CONV // 2
    xbc = lax.conv_general_dilated(xbc, conv_w[:, None, :], window_strides=(1,), padding=[(pad, pad)],
                                   dimension_numbers=('NWC', 'WIO', 'NWC'), feature_group_count=CONV_DIM) + conv_b
    xbc = jax.nn.silu(xbc).astype(jnp.float32)
    xs = xbc[..., :D_INNER].reshape(b, L, SSD_HEADS, SSD_HEAD_DIM)
    Bm = xbc[..., D_INNER:D_INNER + GN].reshape(b, L, SSD_GROUPS, SSD_STATE)
    Cm = xbc[..., D_INNER + GN:].reshape(b, L, SSD_GROUPS, SSD_STATE)
    dt = jax.nn.softplus(dt_raw.astype(jnp.float32).reshape(b, L, 2, SSD_HEADS) + dt_bias.astype(jnp.float32))
    A = -jnp.exp(A_log.astype(jnp.float32))
    y_f = ssd_chunked(xs, dt[:, :, 0], A[0], Bm, Cm)
    flip = lambda t: jnp.flip(t, axis=1)
    y_b = flip(ssd_chunked(flip(xs), flip(dt[:, :, 1]), A[1], flip(Bm), flip(Cm)))
    y = y_f + y_b + D_skip.astype(jnp.float32)[:, None] * xs
    y = y.reshape(b, L, D_INNER) * jax.nn.silu(z.astype(jnp.float32))
    return rms_norm(y, norm_w).astype(z.dtype)

def dilated_window_attention(q, k, v, bias_table, window, dilation):
    b, L, h, e = q.shape
    span = (window // 2) // dilation
    W = span
    M = L // dilation
    nb = -(-M // W)
    Mp = nb * W

    def to_sub(t):
        t = t.reshape(b, M, dilation, h, e).transpose(0, 2, 1, 3, 4)
        return jnp.pad(t, ((0, 0), (0, 0), (0, Mp - M), (0, 0), (0, 0)))

    def windows(t):
        t = jnp.pad(t, ((0, 0), (0, 0), (W, W), (0, 0), (0, 0))).reshape(b, dilation, nb + 2, W, h, e)
        return jnp.concatenate([t[:, :, :-2], t[:, :, 1:-1], t[:, :, 2:]], axis=3)

    qs = to_sub(q).reshape(b, dilation, nb, W, h, e)
    ks = windows(to_sub(k))
    vs = windows(to_sub(v))
    i = np.arange(W)[:, None]
    j = np.arange(3 * W)[None, :]
    rel_sub = j - W - i
    bias = jnp.transpose(bias_table[t5_bucket(rel_sub * dilation)], (2, 0, 1)).astype(jnp.float32)
    blk = np.arange(nb)[:, None, None]
    m_k = (blk - 1) * W + j[None]
    valid = (np.abs(rel_sub)[None] <= span) & (m_k >= 0) & (m_k < M)
    s = jnp.einsum('bdnqhe,bdnkhe->bdnhqk', qs, ks).astype(jnp.float32) * (e ** -0.5) + bias[None, None, None]
    s = jnp.where(valid[None, None, :, None], s, -1e30)
    m = jnp.max(s, axis=-1, keepdims=True)
    p = jnp.exp(s - m)
    den = jnp.sum(p, axis=-1, keepdims=True)
    o = jnp.einsum('bdnhqk,bdnkhe->bdnqhe', (p / den).astype(v.dtype), vs)
    lse = (m + jnp.log(den))[..., 0].transpose(0, 1, 2, 4, 3)
    o = o.reshape(b, dilation, Mp, h, e)[:, :, :M].transpose(0, 2, 1, 3, 4).reshape(b, L, h, e)
    lse = lse.reshape(b, dilation, Mp, h)[:, :, :M].transpose(0, 2, 1, 3).reshape(b, L, h)
    return o, lse

def attention_branch(q, k, v, rel_bias):
    b, L = q.shape[0], q.shape[1]
    q = q.reshape(b, L, ATTN_HEADS, ATTN_HEAD_DIM)
    k = k.reshape(b, L, ATTN_HEADS, ATTN_HEAD_DIM)
    v = v.reshape(b, L, ATTN_HEADS, ATTN_HEAD_DIM)
    outs, lses = [], []
    for gi, (win, dil) in enumerate(DILATION_GROUPS):
        hs = slice(gi * HEADS_PER_GROUP, (gi + 1) * HEADS_PER_GROUP)
        o, lse = dilated_window_attention(q[:, :, hs], k[:, :, hs], v[:, :, hs], rel_bias[:, hs], win, dil)
        outs.append(o)
        lses.append(lse)
    wts = jax.nn.softmax(jnp.stack(lses), axis=0)
    o = jnp.sum(wts[..., None] * jnp.stack(outs).astype(jnp.float32), axis=0)
    return o.reshape(b, L, ATTN_OUT_WIDTH).astype(q.dtype)

def peer_ffn(xn, w_query, sub_keys, expert_u, expert_v):
    b, L, D = xn.shape
    T = b * L
    xt = xn.reshape(T, D)
    q = (xt @ w_query).reshape(T, PEER_HEADS, 2, PEER_HALF)
    s = jnp.einsum('thsk,snk->thsn', q, sub_keys).astype(jnp.float32)
    sv, si = lax.top_k(s, PEER_TOPK)
    cand = (sv[:, :, 0, :, None] + sv[:, :, 1, None, :]).reshape(T, PEER_HEADS, PEER_TOPK * PEER_TOPK)
    cv, ci = lax.top_k(cand, PEER_TOPK)
    i1 = jnp.take_along_axis(si[:, :, 0], ci // PEER_TOPK, axis=-1)
    i2 = jnp.take_along_axis(si[:, :, 1], ci % PEER_TOPK, axis=-1)
    idx = i1 * PEER_N_KEYS + i2
    g = jax.nn.softmax(cv, axis=-1)
    nblk = T // PEER_TOKEN_BLOCK

    def block(args):
        xb, ib, gb = args
        hid = jax.nn.gelu(jnp.einsum('td,thkd->thk', xb, expert_u[ib]).astype(jnp.float32), approximate=False)
        return jnp.einsum('thk,thkd->td', (gb * hid).astype(xb.dtype), expert_v[ib])

    out = lax.map(block, (xt.reshape(nblk, PEER_TOKEN_BLOCK, D),
                          idx.reshape(nblk, PEER_TOKEN_BLOCK, PEER_HEADS, PEER_TOPK),
                          g.reshape(nblk, PEER_TOKEN_BLOCK, PEER_HEADS, PEER_TOPK)))
    return out.reshape(b, L, D)

def trunk(x, rel_bias, norm1_w, w_in, conv_w, conv_b, A_log, dt_bias, D_skip, ssd_norm_w,
          w_ssd_out, w_attn_out, w_out, norm2_w, w_query, sub_keys, expert_u, expert_v, final_norm_w):
    b, L, _ = x.shape
    for l in range(DEPTH):
        hn = rms_norm(x, norm1_w[l])
        proj = hn @ w_in[l]
        y_ssd = ssd_branch(proj[..., :OFF_XBC], proj[..., OFF_XBC:OFF_DT], proj[..., OFF_DT:OFF_Q],
                           conv_w[l], conv_b[l], A_log[l], dt_bias[l], D_skip[l], ssd_norm_w[l])
        y_att = attention_branch(proj[..., OFF_Q:OFF_K], proj[..., OFF_K:OFF_V], proj[..., OFF_V:OFF_GATE], rel_bias)
        gates = jax.nn.sigmoid(proj[..., OFF_GATE:].astype(jnp.float32)).reshape(b, L, 2, D_MODEL)
        merged = gates[:, :, 0] * (y_ssd @ w_ssd_out[l]) + gates[:, :, 1] * (y_att @ w_attn_out[l])
        x = x + merged.astype(x.dtype) @ w_out[l]
        x = x + peer_ffn(rms_norm(x, norm2_w[l]), w_query[l], sub_keys[l], expert_u[l], expert_v[l])
    return rms_norm(x, final_norm_w)

def setup_inputs(seed: int = 0) -> dict:
    key = jax.random.key(seed)
    ks = jax.random.split(key, 24)
    f32 = jnp.float32
    nrm = lambda k, shape, scale: jax.random.normal(k, shape, f32) * scale
    dt0 = jnp.exp(jax.random.uniform(ks[7], (DEPTH, 2, SSD_HEADS), f32, np.log(1e-3), np.log(1e-1)))
    return {
        'x_prompt': nrm(ks[0], (BATCH, SEQ, D_MODEL), 1.0),
        'x_sample': nrm(ks[1], (DEC_BATCH, DEC_SEQ, D_MODEL), 1.0),
        'rel_bias': nrm(ks[2], (REL_BUCKETS, ATTN_HEADS), 0.5),
        'norm1_w': 1.0 + nrm(ks[3], (DEPTH, D_MODEL), 0.05),
        'w_in': nrm(ks[4], (DEPTH, D_MODEL, IN_COLS), D_MODEL ** -0.5),
        'conv_w': nrm(ks[5], (DEPTH, D_CONV, CONV_DIM), D_CONV ** -0.5),
        'conv_b': nrm(ks[6], (DEPTH, CONV_DIM), 0.01),
        'A_log': jnp.log(jax.random.uniform(ks[8], (DEPTH, 2, SSD_HEADS), f32, 1.0, 16.0)),
        'dt_bias': dt0 + jnp.log(-jnp.expm1(-dt0)),
        'D_skip': 1.0 + nrm(ks[9], (DEPTH, SSD_HEADS), 0.1),
        'ssd_norm_w': 1.0 + nrm(ks[10], (DEPTH, D_INNER), 0.05),
        'w_ssd_out': nrm(ks[11], (DEPTH, D_INNER, D_MODEL), D_INNER ** -0.5),
        'w_attn_out': nrm(ks[12], (DEPTH, ATTN_OUT_WIDTH, D_MODEL), ATTN_OUT_WIDTH ** -0.5),
        'w_out': nrm(ks[13], (DEPTH, D_MODEL, D_MODEL), D_MODEL ** -0.5),
        'norm2_w': 1.0 + nrm(ks[14], (DEPTH, D_MODEL), 0.05),
        'w_query': nrm(ks[15], (DEPTH, D_MODEL, PEER_HEADS * PEER_KEY_DIM), D_MODEL ** -0.5),
        'sub_keys': nrm(ks[16], (DEPTH, 2, PEER_N_KEYS, PEER_HALF), PEER_HALF ** -0.5),
        'expert_u': nrm(ks[17], (DEPTH, PEER_EXPERTS, D_MODEL), D_MODEL ** -0.5),
        'expert_v': nrm(ks[18], (DEPTH, PEER_EXPERTS, D_MODEL), PEER_HEADS ** -0.5),
        'final_norm_w': 1.0 + nrm(ks[19], (D_MODEL,), 0.05),
    }

def reference(x_prompt, x_sample, rel_bias, norm1_w, w_in, conv_w, conv_b, A_log, dt_bias, D_skip,
              ssd_norm_w, w_ssd_out, w_attn_out, w_out, norm2_w, w_query, sub_keys, expert_u, expert_v,
              final_norm_w):
    y_prompt = trunk(x_prompt, rel_bias, norm1_w, w_in, conv_w, conv_b, A_log, dt_bias, D_skip, ssd_norm_w,
                     w_ssd_out, w_attn_out, w_out, norm2_w, w_query, sub_keys, expert_u, expert_v, final_norm_w)
    y_sample = trunk(x_sample, rel_bias, norm1_w, w_in, conv_w, conv_b, A_log, dt_bias, D_skip, ssd_norm_w,
                     w_ssd_out, w_attn_out, w_out, norm2_w, w_query, sub_keys, expert_u, expert_v, final_norm_w)
    return (y_prompt, y_sample)


_drawn_inputs = setup_inputs


def setup_inputs(seed=0):
    import zlib

    import numpy as np

    out = dict(_drawn_inputs(seed))
    spreads = {}
    factors = {}
    for name, (base, spread) in spreads.items():
        noise = np.random.default_rng([zlib.crc32(name.encode()), seed]).standard_normal(out[name].shape)
        drawn = base * np.exp(spread * noise) if base else spread * noise
        out[name] = __import__('jax').numpy.asarray(drawn.astype(out[name].dtype))
    for name, factor in factors.items():
        out[name] = (out[name] * factor).astype(out[name].dtype)
    return out
```

```python
from contextlib import ExitStack

import numpy as np
import concourse.bass as bass
from concourse import mybir

F32 = mybir.dt.float32
F32R = mybir.dt.float32r
BF16 = mybir.dt.bfloat16
U32 = mybir.dt.uint32
ALU = mybir.AluOpType
ACT = mybir.ActivationFunctionType
AX = mybir.AxisListType.X

P = 128
D = 1024
KD = D // P
SEQ = 256
NSEQ = 2
T = NSEQ * SEQ
NT = T // P
DEPTH = 2
D_INNER = 2048
GROUPS = 8
RH = 4
HD = 64
SSD_HEADS = 32
CONV = 5
CONV_DIM = D_INNER + 2 * GROUPS * P
ATTN_WIDTH = 1536
NG = 3
WINDOWS = ((128, 1), (512, 4), (2048, 16))
REL_BUCKETS = 32
REL_MAX = 1024
PH = 8
TOPK = 16
EXPERT_TILES = 128
EPS = 1e-6
OFF_XBC = D_INNER
OFF_DT = OFF_XBC + CONV_DIM
OFF_Q = OFF_DT + 2 * SSD_HEADS
OFF_K = OFF_Q + ATTN_WIDTH
OFF_V = OFF_K + ATTN_WIDTH
OFF_GATE = OFF_V + ATTN_WIDTH
NEG = -1e30

UNIT = KD * P
SLOTS = 9
CREDIT = 16
STRIPES = 8
BLOCKS = 4
PHASES = (("ssd", GROUPS, (0, 1, 2, 3, 4, 5)), ("att", 4, (0, 1, 2, 3, 4, 5, 6, 7, 8)), ("mrg", 8, (0, 1, 2, 3, 4)),
          ("out", 1, (0, 1, 2, 3, 4, 5, 6, 7)), ("qry", PH // 2, (0, 1, 2, 3)),
          ("peer", STRIPES * BLOCKS, (0, 1, 2, 0, 3, 4, 5, 6)))
NAMES = [q[0] for q in PHASES]
UNITS = sum(i * len(n) for _, i, n in PHASES)
BASE = {}
LOADS = {}
_u = 0
_per_slot = [0] * SLOTS
for _name, _i, _n in PHASES:
    BASE[_name] = _u
    LOADS[_name] = list(_per_slot)
    _u += _i * len(_n)
    for _j in _n:
        _per_slot[_j] += _i
SLOT_LOADS = list(_per_slot)


def last_user(name, j):
    k = NAMES.index(name)
    slot = PHASES[k][2][j]
    for jj in range(j - 1, -1, -1):
        if PHASES[k][2][jj] == slot:
            return BASE[name] + jj
    for back in range(1, len(PHASES) + 1):
        pn, it, slots = PHASES[(k - back) % len(PHASES)]
        for jj in range(len(slots) - 1, -1, -1):
            if slots[jj] == slot:
                return BASE[pn] + (it - 1) * len(slots) + jj - (UNITS if k - back < 0 else 0)
    raise ValueError(name)


SPLIT_QRY = 2 * PH
SPLIT_PEER = (0, 1, 2, 4, 3, 5, 6, 7)
SPLITS = SPLIT_QRY + STRIPES * BLOCKS * len(SPLIT_PEER)
LOAD_PEER = (0, 1, 2, 4, 5, 3, 6, 7)


PW_N1, PW_N2, PW_CONV = 0, 8, 16
PW_DTB = PW_CONV + GROUPS * 32
PW_ALOG = PW_DTB + 64
PW_KEYS = PW_ALOG + 64
PW_WDT = PW_KEYS + 256
PW = PW_WDT + KD * 64

C_ID, C_LE, C_GE, C_ONE, C_MF, C_MB, C_I16, C_IOTA = 0, 128, 256, 384, 512, 768, 1024, 1040
CW = C_IOTA + 144
RW = 2 * SEQ


def t5_bucket(rel):
    half = REL_BUCKETS // 2
    exact = half // 2
    n = np.abs(rel)
    large = exact + (np.log(np.maximum(n, 1) / exact) / np.log(REL_MAX / exact) * (half - exact)).astype(np.int32)
    large = np.minimum(large, half - 1)
    return np.where(rel > 0, half, 0) + np.where(n < exact, n, large)


def constants():
    c = np.zeros((P, CW), np.float32)
    i = np.arange(P)
    c[:, C_ID:C_ID + P] = np.eye(P)
    c[:, C_LE:C_LE + P] = i[:, None] <= i[None, :]
    c[:, C_GE:C_GE + P] = i[:, None] >= i[None, :]
    c[:, C_ONE:C_ONE + P] = 1.0
    c[:, C_MF:C_MF + P] = np.where(i[None, :] >= i[:, None], 0.0, NEG)
    c[:, C_MB + P:C_MB + 2 * P] = np.where(i[None, :] <= i[:, None], 0.0, NEG)
    c[:, C_I16:C_I16 + 16] = np.arange(16)
    c[:, C_IOTA:C_IOTA + 144] = np.arange(144)
    return c


def bias_constants():
    d = np.arange(RW) - (SEQ - 1)
    hot = (t5_bucket(d)[None, :] == np.arange(REL_BUCKETS)[:, None]).astype(np.float32)
    mask = np.full((NG * 8, RW), NEG, np.float32)
    for g, (win, dil) in enumerate(WINDOWS):
        ok = (d % dil == 0) & (np.abs(d // dil) <= (win // 2) // dil)
        mask[g * 8:(g + 1) * 8, ok] = 0.0
    out = np.zeros((56, RW), np.float32)
    out[0:32] = hot
    out[32:56] = mask
    return out


class Count:

    def __init__(self, sem, per_layer, before=0):
        self.sem, self.per_layer, self.before = sem, per_layer, before

    def at(self, layer, n):
        return layer * self.per_layer + (n + self.before)


def spread(ap, axis, n):
    s = ap.unsqueeze(axis)
    shape = list(s.shape)
    shape[axis] = n
    return s.broadcast_to(shape)


def build(nc, x_prompt, x_sample, consts, biases, rel, par, w_ssd, w_att, w_mrg, w_out, w_qry, w_u, w_v,
          w_final, y_prompt, y_sample):
    with ExitStack() as ctx:
        at_byte = {}

        def sb(name, shape, dt=F32):
            t = ctx.enter_context(nc.sbuf_tensor(name, shape, dt))
            at_byte[name] = nc.sbuf_base - int(np.prod(shape[1:])) * (2 if dt is BF16 else 4)
            return t

        def part(name, ap):
            shape = list(ap.shape)
            return nc.alloc_sbuf_tensor_at(name, shape, F32R, offset=at_byte[ap.tensor.name] + 4 * ap.offset)

        def sem(name):
            return ctx.enter_context(nc.semaphore(name))

        def count(name, per_layer, before=0):
            return Count(sem(name), per_layer, before)

        a_dram = nc.dram_tensor("a_rows", [2, SSD_HEADS, T], F32).ap()
        r_dram = nc.dram_tensor("bias_rows", [NG * 8, RW], F32).ap()
        bias_dram = nc.dram_tensor("bias_tiles", [4, 2, P, 6, SEQ], F32).ap()

        bank = [ctx.enter_context(nc.psum_tensor(f"bank{i}", [P, 512], F32)) for i in range(4)]
        routes = ctx.enter_context(nc.psum_tensor("banks4to7", [P, 4, 512], F32))

        def pb(i):
            return bank[i][:, :] if i < 4 else routes[:, i - 4, :]

        x = sb("x", [P, NT, D])
        hT = sb("hT", [P, KD, T])
        ring = [sb(f"ring{j}", [P, UNIT]) for j in range(SLOTS)]
        pr = sb("pr", [P, PW])
        cst = sb("cst", [P, CW])
        iota_b = sb("iota_b", [P, 144, 16], BF16)
        stat = sb("stat", [P, 64])
        yT = sb("yT", [P, 16, T])
        late = sb("late", [P, 5 * T])
        rstdB = late[:, 0:T]
        oT = late[:, T:].rearrange("p (h t) -> p h t", h=4)
        ident = cst[:, C_ID:C_ID + P]
        le = cst[:, C_LE:C_LE + P]
        ge = cst[:, C_GE:C_GE + P]
        ones = cst[:, C_ONE:C_ONE + P]

        WORDS = 21300
        arena = sb("arena", [P, WORDS])
        used = [0]

        def cut(*shape, dt=F32):
            n = 1
            for s in shape:
                n *= s
            words = n if dt in (F32, U32) else (n + 1) // 2
            o = used[0]
            used[0] += words
            assert used[0] <= WORDS, used[0]
            v = arena[:, o:o + words]
            if dt is not F32:
                v = v.bitcast(dt)
            if len(shape) > 1:
                names = " ".join(f"d{i}" for i in range(len(shape)))
                v = v.rearrange(f"p ({names}) -> p {names}", **{f"d{i}": s for i, s in enumerate(shape)})
            return v

        rel_w, hot_rel, mask_rel = cut(NG * 8), cut(RW), cut(RW)
        used[0] = 0
        xn = [cut(D), cut(D)]
        junk = cut(D)
        decays = used[0]
        used[0] = 0
        xtok = cut(NT, 2 * P)
        xdt = [cut(NT, 2 * P) for _ in range(2)]
        used[0] = decays
        dtv = cut(NT, 64)
        negA = cut(NT, 64)
        keep = used[0]
        dr0, dax, du, dw, dln, dd, dz, da = (cut(NT, 64) for _ in range(8))
        aexp = cut(64)
        aT = cut(2, T)
        used[0] = keep
        aBC = cut(2, RH, T)
        E = cut(8, 768)
        cx = [cut(T) for _ in range(4)]
        zs = [cut(T) for _ in range(2)]
        y3 = [cut(T) for _ in range(2)]
        sq = [cut(T) for _ in range(2)]
        gneg = cut(NT, 2, RH)
        gdt = cut(NT, 2, RH)
        gp = cut(32)
        sqsum = cut(T)
        used[0] = 0
        qk = [cut(T) for _ in range(6)]
        vtok = [cut(NT, P) for _ in range(3)]
        BM = cut(2, 6, SEQ)
        Pm = cut(8, NG, SEQ)
        mx, nm, den, wg, fw = (cut(8, NG) for _ in range(5))
        m1, s1, r1 = (cut(8) for _ in range(3))
        top = used[0]
        PTt = cut(4, NG, 2, SEQ)
        used[0] = top
        vraw = [cut(T) for _ in range(3)]
        used[0] = 0
        mT = cut(8, T)
        sg = [cut(T) for _ in range(4)]
        t1 = cut(T)
        t2 = cut(T)
        used[0] = 0
        hTh = cut(KD, T)
        xn2 = [cut(D), cut(D)]
        junk2 = cut(D)
        used[0] = KD * T
        qT = [cut(T) for _ in range(4)]
        sc = [cut(2, NT, P) for _ in range(2)]
        sc2 = cut(2, NT, P)
        v16 = cut(2, NT, TOPK)
        x16 = cut(2, NT, TOPK, dt=U32)
        f16 = cut(2, NT, TOPK)
        cand = cut(NT, 256)
        cand2 = cut(NT, 256)
        cvh = cut(NT, TOPK)
        ci = cut(NT * TOPK, dt=U32)
        pij = cut(2, NT * TOPK, dt=U32)
        pf = cut(2, NT * TOPK)
        hot = cut(NT, TOPK, 16)
        idh = cut(2, NT * TOPK)
        CV = cut(NT, PH, TOPK)
        ID = [cut(NT, PH, TOPK) for _ in range(2)]
        Ge = cut(NT, PH, TOPK)
        gsum = cut(32)
        grec = cut(32)
        gr = [cut(T) for _ in range(2)]
        assert used[0] <= 28 * T + 2 * D
        used[0] = KD * T
        Gs = [yT, cut(16, T)]
        gh = [cut(T) for _ in range(4)]
        ghh = [cut(T) for _ in range(4)]
        hi_u = [ring[8][:, :], ring[7][:, :]]
        hi_v = [late[:, 0:UNIT], late[:, UNIT:2 * UNIT], pr[:, 0:UNIT], cut(UNIT)]
        hi_u = [part(f"hi_u{n}", a) for n, a in enumerate(hi_u)]
        hi_v = [part(f"hi_v{n}", a) for n, a in enumerate(hi_v)]
        hi_q = [hi_u[0], hi_v[0]]
        lo = [part(f"lo{n}", ring[n][:, :]) for n in range(7)]
        hT_hi, hT_lo = part("hT_hi", hTh), part("hT_lo", hT[:, :, :])
        gh_h = [part(f"gh_hi{n}", a) for n, a in enumerate(ghh)]
        gh_l = [part(f"gh_lo{n}", a) for n, a in enumerate(gh)]
        idT = [late[:, 2 * UNIT + q * (T // 2):2 * UNIT + (q + 1) * (T // 2)].bitcast(BF16) for q in range(2)]
        gP = cut(3, T, dt=BF16)
        Bh = [cut(P, 16, dt=BF16) for _ in range(2)]
        eq = [cut(16, 16, dt=BF16) for _ in range(2)]
        A3 = [cut(3, 16, 16, dt=BF16) for _ in range(2)]
        used[0] = 0
        fin = [cut(D) for _ in range(2)]
        fjunk = cut(D)
        wfin = cut(D)

        w_in = [sem(f"w_in{j}") for j in range(SLOTS)]
        slot_free = Count(sem("slot_free"), UNITS, CREDIT)
        cst_in, x_in, rel_in, row_out, bias_out = (sem(n) for n in ("cst_in", "x_in", "rel_in", "row_out", "bias_out"))
        iota_ok, rel_mm, row_ok = sem("iota_ok"), sem("rel_mm"), sem("row_ok")
        par_in = count("par_in", 16)
        n_ss, n_ms, n_sqrt, n_rs, n_xn, n_tr, hT_ok = (count(n, k) for n, k in (
            ("n_ss", 8), ("n_ms", 2), ("n_sqrt", 2), ("n_rs", 2), ("n_xn", 8), ("n_tr", 16), ("hT_ok", 16)))
        dt_mm, dt_ax, dt_u, dt_w, dt_ln, dt_a, dt_cs, dt_T = (count(n, k) for n, k in (
            ("dt_mm", 1), ("dt_ax", 1), ("dt_u", 2), ("dt_w", 1), ("dt_ln", 1), ("dt_a", 1), ("dt_cs", 1), ("dt_T", 3)))
        dt_v = count("dt_v", 9)
        aT_out = count("aT_out", 16)
        bc_in = count("bc_in", 16 * GROUPS)
        g_cp = count("g_cp", 3 * GROUPS)
        arg, ex = count("arg", 8 * GROUPS), count("ex", 8 * GROUPS)
        c_mm, c_acc, c_tap, c_ok, c_s = (count(n, k * GROUPS) for n, k in (
            ("c_mm", 4), ("c_acc", 4), ("c_tap", 12), ("c_ok", 4), ("c_s", 4)))
        z_mm, z_s = count("z_mm", 2 * GROUPS), count("z_s", 2 * GROUPS, 2)
        xt_mm, xt_ok, xd_ok = (count(n, 2 * GROUPS) for n in ("xt_mm", "xt_ok", "xd_ok"))
        cb_mm, m_ok = count("cb_mm", 2 * GROUPS), count("m_ok", 8 * GROUPS)
        y_mm, y_v, y3_ok, sq_ok, y_ok = (count(n, 2 * GROUPS, b) for n, b in (
            ("y_mm", 0), ("y_v", 2), ("y3_ok", 0), ("sq_ok", 0), ("y_ok", 2)))
        sq_sum = count("sq_sum", 1 + 2 * GROUPS, 2)
        r_mm, r_ms, r_sq, r_ok = (count(n, 1) for n in ("r_mm", "r_ms", "r_sq", "r_ok"))
        bm_in = count("bm_in", 16 * 4)
        p_mm, p_evA, p_evV = count("p_mm", 36), count("p_evA", 20), count("p_evV", 16)
        vt_mm, vt_ok = count("vt_mm", 12), count("vt_ok", 12)
        s_mm, s_v, s_nm, p_x = (count(n, 32) for n in ("s_mm", "s_v", "s_nm", "p_x"))
        a_v, a_w = count("a_v", 4 * 6), count("a_w", 4)
        p_f = count("p_f", 32)
        t_mm, t_evA, t_evV = count("t_mm", 48), count("t_evA", 24), count("t_evV", 24)
        o_mm, o_ok = count("o_mm", 4), count("o_ok", 4, 1)
        ga_mm, gb_mm, pa_mm, pb_mm = (count(n, 8) for n in ("ga_mm", "gb_mm", "pa_mm", "pb_mm"))
        sg_ok = count("sg_ok", 16)
        m_v, mT_ok = count("m_v", 24), count("mT_ok", 8, 2)
        out_mm, x_mid = count("out_mm", 8), count("x_mid", 8)
        q_mm, q_ev, q_s, q_sv = (count(n, 16) for n in ("q_mm", "q_ev", "q_s", "q_sv"))
        TK = 16
        k_v, k_done = count("k_v", TK * PH), count("k_done", PH, 2)
        g_v, g_e, g_ok, gt_mm, gt_ok = (count(n, k) for n, k in (
            ("g_v", 3), ("g_e", 1), ("g_ok", 1), ("gt_mm", 3), ("gt_ok", 7)))
        g_fence = count("g_fence", 1)
        CH = (STRIPES + 1) * BLOCKS * 8
        h_eq, h_ok, h_mm, G_ok = (count(n, CH) for n in ("h_eq", "h_ok", "h_mm", "G_ok"))
        u_mm, u_ge, gh_m, gh_hi, gh_ok = (count(n, EXPERT_TILES, b) for n, b in (
            ("u_mm", 0), ("u_ge", 2), ("gh_m", 0), ("gh_hi", 0), ("gh_ok", 0)))
        w_hi, w_lo = count("w_hi", SPLITS), count("w_lo", SPLITS)
        hh_ok, hl_ok = count("hh_ok", 8), count("hl_ok", 8)
        v_mm, v_add = count("v_mm", 256), count("v_add", 256, 2)
        f_w, f_ss, f_v, f_sq, f_x, f_ok, f_out = (sem(n) for n in ("f_w", "f_ss", "f_v", "f_sq", "f_x", "f_ok", "f_out"))

        block = ctx.enter_context(nc.Block())

        def wait(e, c, layer, n):
            e.wait_ge(c.sem, c.at(layer, n))

        def wait_alone(e, c, layer, n):
            value = c.at(layer, n)
            e.compute_val(value)
            e.wait_ge(cst_in, 16)
            e.wait_ge(c.sem, value)

        def h_piece(h, n):
            return h[:, 4 * (n % 2):4 * (n % 2) + 4, (n // 2) * P:(n // 2 + 1) * P]

        def loaded(e, l, name, i, j):
            slots = PHASES[NAMES.index(name)][2]
            s = slots[j]
            first, each = LOADS[name][s], slots.count(s)
            e.wait_ge(w_in[s], (l * SLOT_LOADS[s] + i * each + (first + slots[:j].count(s) + 1)) * 16)

        def qry_split(h2, n):
            return h2 * 4 + n

        def peer_split(blk, n):
            return blk * 8 + (SPLIT_QRY + SPLIT_PEER.index(n))

        @block.sync
        def _(sp):
            sp.dma_start(cst[:, :], consts).then_inc(cst_in, 16)
            sp.dma_start(x[:, 0:2, :], x_prompt.rearrange("b (t p) d -> p (b t) d", p=P)).then_inc(x_in, 16)
            sp.dma_start(x[:, 2:4, :], x_sample.rearrange("b (t p) d -> p (b t) d", p=P)).then_inc(x_in, 16)

            def load(src, j, free_at):
                sp.compute_val(src.offset)
                if free_at is not None:
                    sp.compute_val(free_at)
                    sp.wait_ge(cst_in, 16)
                    sp.wait_ge(slot_free.sem, free_at)
                sp.dma_start(ring[j][:, :], src).then_inc(w_in[j], 16)

            def phase(l, name, unit, order=None):
                _, iters, slots = PHASES[NAMES.index(name)]
                n = len(slots)
                order = order or range(n)
                for j in order:
                    u = last_user(name, j)
                    load(unit(0, j), slots[j], slot_free.at(l, u + 1) if u >= -CREDIT else None)
                if iters > 1:
                    with sp.Fori(1, iters) as i:
                        for j in order:
                            earlier = [jj for jj in range(j) if slots[jj] == slots[j]]
                            if earlier:
                                u = i * n + (BASE[name] + earlier[-1])
                            else:
                                last = max(jj for jj in range(n) if slots[jj] == slots[j])
                                u = (i - 1) * n + (BASE[name] + last)
                            load(unit(i, j), slots[j], slot_free.at(l, u + 1))

            with sp.Fori(0, DEPTH) as l:
                phase(l, "ssd", lambda i, j: w_ssd[l, i, j])
                phase(l, "att", lambda i, j: w_att[l, i, j])
                phase(l, "mrg", lambda i, j: w_mrg[l, i, j])
                phase(l, "out", lambda i, j: w_out[l, j])
                phase(l, "qry", lambda i, j: w_qry[l, i, j])
                phase(l, "peer", lambda i, j: w_u[l, i, j] if j < 4 else w_v[l, i, j - 4], LOAD_PEER)
            yp = y_prompt.rearrange("b (t p) d -> p (b t) d", p=P)
            ys = y_sample.rearrange("b (t p) d -> p (b t) d", p=P)
            for tt in range(NT):
                sp.wait_ge(f_ok, tt + 1)
                dst = yp[:, tt, :] if tt < 2 else ys[:, tt - 2, :]
                sp.dma_start(dst, fin[tt % 2]).then_inc(f_out, 16)
                sp.wait_ge(f_out, 16 * (tt + 1))

        @block.gpsimd
        def _(pool):
            pool.wait_ge(row_ok, 1)
            pool.dma_start(r_dram, oT[0:NG * 8, 0, :]).then_inc(row_out, 16)
            pool.wait_ge(row_out, 16)
            for hp in range(4):
                for qt in range(2):
                    for j in range(2):
                        src = bass.AP(tensor=r_dram.tensor, offset=(2 * hp + j) * RW + (SEQ - 1) - qt * P,
                                      ap=[[8 * RW, NG], [-1, P], [1, SEQ]])
                        dst = bias_dram[hp, qt, :, 3 * j:3 * j + 3, :].rearrange("q g k -> g q k")
                        pool.dma_start(dst, src).then_inc(bias_out, 16)
                        pool.wait_ge(bias_out, 16 * (4 * hp + 2 * qt + j + 1))
            pool.dma_start(pr[:, :], par[0]).then_inc(par_in.sem, 16)
            with pool.Fori(0, DEPTH) as l:
                wait_alone(pool, dt_T, l, 3)
                pool.dma_start(a_dram.rearrange("d h t -> h d t"), aT[0:SSD_HEADS]).then_inc(aT_out.sem, 16)
                nc.gpsimd.memset(sqsum, 0.0).then_inc(sq_sum.sem, 1)

                def spread_rows(g):
                    return (aBC, spread(a_dram[:, bass.ds(g * RH, RH), :].rearrange("d h t -> d (h t)"), 0, P))

                dst, src = spread_rows(0)
                wait_alone(pool, aT_out, l, 16)
                pool.dma_start(dst.rearrange("p d h t -> p d (h t)"), src).then_inc(bc_in.sem, 16)

                def add_squares(g):
                    for i in range(2):
                        wait(pool, sq_ok, l, g * 2 + (i + 1))
                        wait(pool, sq_sum, l, g * 2 + (i + 1))
                        nc.gpsimd.tensor_tensor(sqsum, sqsum, sq[i], ALU.add).then_inc(sq_sum.sem, 1)

                with pool.Fori(1, GROUPS) as g:
                    dst, src = spread_rows(g)
                    pool.compute_val(src.offset)
                    wait_alone(pool, arg, l, g * 8)
                    pool.dma_start(dst.rearrange("p d h t -> p d (h t)"), src).then_inc(bc_in.sem, 16)
                    add_squares(g - 1)
                add_squares(GROUPS - 1)

                def bias_tiles(hp):
                    return BM.rearrange("p q h k -> p q (h k)"), bias_dram[hp].rearrange("q p h k -> p q (h k)")

                wait_alone(pool, r_ok, l, 1)
                dst, src = bias_tiles(0)
                pool.dma_start(dst, src).then_inc(bm_in.sem, 16)
                with pool.Fori(1, 4) as hp:
                    dst, src = bias_tiles(hp)
                    pool.compute_val(src.offset)
                    wait_alone(pool, s_v, l, hp * 8)
                    pool.dma_start(dst, src).then_inc(bm_in.sem, 16)

                def low(n, slot, hi):
                    wait(pool, w_hi, l, n + 1)
                    nc.gpsimd.tensor_tensor(lo[slot][:, :], ring[slot][:, :], hi[:, :], ALU.subtract).then_inc(w_lo.sem, 1)

                with pool.Fori(0, PH // 2) as h2:
                    for n in range(4):
                        low(qry_split(h2, n), n, hi_q[n % 2])
                with pool.Fori(0, STRIPES * BLOCKS) as blk:
                    for n in SPLIT_PEER:
                        low(peer_split(blk, n), PHASES[-1][2][n], hi_u[n % 2] if n < 4 else hi_v[n - 4])
                src = par[l + 1]
                pool.compute_val(src.offset)
                wait_alone(pool, v_mm, l, 256)
                pool.dma_start(pr[:, :], src).then_inc(par_in.sem, 16)
            pool.wait_ge(par_in.sem, 16 * (DEPTH + 1))
            pool.wait_ge(v_add.sem, v_add.at(DEPTH, 0))
            pool.dma_start(wfin, w_final.partition_broadcast(P)).then_inc(f_w, 16)
            pool.wait_ge(f_w, 16)

        @block.tensor
        def _(pe):
            pe.sem_inc(slot_free.sem, CREDIT - 1)
            pe.wait_ge(cst_in, 16)
            pe.wait_ge(rel_in, 48)
            pe.matmul(pb(0)[0:NG * 8, :], rel_w[0:REL_BUCKETS], hot_rel[0:REL_BUCKETS], start=True, stop=True).then_inc(rel_mm, 1)

            def project(l, name, i, j, out, rhs, n=KD, start=True, stop=True, k0=0):
                loaded(pe, l, name, i, j)
                for k in range(n):
                    mm = pe.matmul(out, ring[j][:, k * P:(k + 1) * P], rhs[:, k0 + k, :],
                                   start=start and k == 0, stop=stop and k == n - 1)
                    if k == 0:
                        mm.then_inc(slot_free.sem, 1)
                return mm

            def product3(out, a, b, start, stop):
                return [pe.matmul(out, a[p], b[q], start=start and n == 0, stop=stop and n == 2)
                        for n, (p, q) in enumerate(((0, 0), (0, 1), (1, 0)))]

            def project3(l, split, slot, hi, out):
                wait(pe, w_lo, l, split + 1)
                for k in range(KD):
                    cols = slice(k * P, (k + 1) * P)
                    mm = product3(out, (hi[:, cols], lo[slot][:, cols]), (hT_hi[:, k, :], hT_lo[:, k, :]), k == 0, k == KD - 1)
                    if k == 0:
                        mm[0].then_inc(slot_free.sem, 1)
                return mm[-1]

            def norm(l, w):
                for tt in range(NT):
                    wait(pe, n_xn, l, 4 * w + tt + 1)
                    if tt >= 2:
                        wait(pe, hT_ok, l, 8 * w + 2 * (tt - 1))
                    for half in range(2):
                        out = pb(2 * (tt % 2) + half)
                        for k in range(4):
                            kk = 4 * half + k
                            mm = pe.transpose(out[:, k * P:(k + 1) * P], (xn, xn2)[w][tt % 2][:, kk * P:(kk + 1) * P], ident)
                        mm.then_inc(n_tr.sem, 1)

            with pe.Fori(0, DEPTH) as l:
                norm(l, 0)
                wait(pe, hT_ok, l, 8)
                wait(pe, par_in, l, 16)
                for tt in range(NT):
                    for k in range(KD):
                        mm = pe.matmul(pb(4)[:, tt * 64:(tt + 1) * 64], hT[:, k, tt * P:(tt + 1) * P],
                                       pr[:, PW_WDT + 64 * k:PW_WDT + 64 * (k + 1)], start=(k == 0), stop=(k == KD - 1))
                mm.then_inc(dt_mm.sem, 1)
                wait(pe, dt_a, l, 1)
                for s in range(NSEQ):
                    for d, tri in ((0, le), (1, ge)):
                        first, second = (2 * s, 2 * s + 1) if d == 0 else (2 * s + 1, 2 * s)
                        cols = slice(32 * d, 32 * d + 32)
                        for tt, parts in ((first, [(tri, first)]), (second, [(ones, first), (tri, second)])):
                            for n, (m, src) in enumerate(parts):
                                pe.matmul(pb(5)[:, tt * 64 + 32 * d:tt * 64 + 32 * d + 32], m, da[:, src, cols],
                                          start=(n == 0), stop=(n == len(parts) - 1))
                            for n, (m, src) in enumerate(parts):
                                mm = pe.matmul(pb(6 + d)[0:32, tt * P:(tt + 1) * P], da[:, src, cols], m,
                                               start=(n == 0), stop=(n == len(parts) - 1))
                mm.then_inc(dt_cs.sem, 1)
                wait_alone(pe, dt_T, l, 3)

                with pe.Fori(0, GROUPS) as g:
                    for j in range(4):
                        if j == 2:
                            wait(pe, y_v, l, g * 2)
                        project(l, "ssd", g, j, pb(j), hT).then_inc(c_mm.sem, 1)
                    for i in range(2):
                        wait(pe, z_s, l, g * 2 + i - 1)
                        project(l, "ssd", g, 4 + i, pb(4 + i), hT).then_inc(z_mm.sem, 1)
                    for s in range(NSEQ):
                        wait(pe, c_s, l, g * 4 + 2)
                        for si in range(2):
                            mm = pe.matmul(pb(s)[:, si * SEQ:(si + 1) * SEQ],
                                           cx[0][:, s * SEQ + si * P:s * SEQ + (si + 1) * P],
                                           cx[1][:, s * SEQ:(s + 1) * SEQ], start=True, stop=True)
                        mm.then_inc(cb_mm.sem, 1)
                    for i in range(2):
                        wait(pe, c_s, l, g * 4 + (3 + i))
                        for tt in range(NT):
                            mm = pe.transpose(pb(6 + i)[:, tt * P:(tt + 1) * P],
                                              cx[2 + i][:, tt * P:(tt + 1) * P], ident)
                        mm.then_inc(xt_mm.sem, 1)
                    wait(pe, xd_ok, l, g * 2 + 2)
                    for n in range(8):
                        r, s = 2 * (n // 4) + (n % 4) // 2, n % 2
                        wait(pe, m_ok, l, g * 8 + (n + 1))
                        out = pb(2 + r // 2)[64 * (r % 2):64 * (r % 2) + 64, :]
                        o = s * SEQ
                        xs = slice(r * HD, (r + 1) * HD)
                        parts = [(0, 0, 0, 256, 0), (1, 1, 256, 256, 0), (1, 0, 512, 128, 0), (0, 1, 640, 128, 128)]
                        for q, (d, si, c0, w, l0) in enumerate(parts):
                            mm = pe.matmul(out[:, o + l0:o + l0 + w], xdt[d][:, 2 * s + si, xs],
                                           E[:, n, c0:c0 + w], start=(q == 0), stop=(q == 3))
                        if n % 4 == 3:
                            mm.then_inc(y_mm.sem, 1)
                wait(pe, sq_sum, l, 1 + 2 * GROUPS)
                wait(pe, z_s, l, 2 * GROUPS)
                pe.matmul(pb(4), ones, sqsum, start=True, stop=True).then_inc(r_mm.sem, 1)
                wait_alone(pe, y_v, l, 2 * GROUPS)
                wait_alone(pe, r_ok, l, 1)

                with pe.Fori(0, 4) as hp:
                    wait(pe, o_ok, l, hp)
                    for u in range(9):
                        if u >= 4:
                            if u % 2 == 0:
                                wait(pe, p_evA, l, hp * 5 + (u - 4) // 2 + 1)
                            else:
                                wait(pe, p_evV, l, hp * 4 + (u - 4) // 2 + 1)
                        project(l, "att", hp, u, pb(u % 4), hT).then_inc(p_mm.sem, 1)
                    wait(pe, p_evA, l, hp * 5 + 5)
                    wait(pe, p_evV, l, hp * 4 + 4)
                    for g in range(NG):
                        for tt in range(NT):
                            mm = pe.transpose(pb(4 + g)[:, tt * P:(tt + 1) * P], vraw[g][:, tt * P:(tt + 1) * P], ident)
                        mm.then_inc(vt_mm.sem, 1)
                    for c in range(8):
                        j, s, qt = c // 4, (c // 2) % 2, c % 2
                        if c >= 2:
                            wait(pe, s_v, l, hp * 8 + (c - 1))
                        hd = slice(64 * j, 64 * j + 64)
                        for g in range(NG):
                            mm = pe.matmul(pb(2 * (c % 2) + g // 2)[:, (g % 2) * SEQ:(g % 2 + 1) * SEQ],
                                           qk[2 * g][hd, s * SEQ + qt * P:s * SEQ + (qt + 1) * P],
                                           qk[2 * g + 1][hd, s * SEQ:(s + 1) * SEQ], start=True, stop=True)
                        mm.then_inc(s_mm.sem, 1)
                    wait(pe, vt_ok, l, hp * 3 + 3)
                    for n in range(12):
                        js, m = n // 3, n % 3
                        if m == 0:
                            wait(pe, p_f, l, hp * 8 + (2 * js + 2))
                        if n >= 4:
                            if n % 2 == 0:
                                wait(pe, t_evA, l, hp * 6 + (n - 4) // 2 + 1)
                            else:
                                wait(pe, t_evV, l, hp * 6 + (n - 4) // 2 + 1)
                        for q in range(4):
                            gk, qt = 2 * m + q // 2, q % 2
                            g, kt = gk // 2, gk % 2
                            mm = pe.transpose(pb(4 + n % 4)[:, q * P:(q + 1) * P],
                                              Pm[:, 2 * js + qt, g, kt * P:(kt + 1) * P], ident)
                        mm.then_inc(t_mm.sem, 1)
                    wait(pe, t_evA, l, hp * 6 + 6)
                    wait(pe, t_evV, l, hp * 6 + 6)
                    for js in range(4):
                        j, s = js // 2, js % 2
                        for q in range(6):
                            g, kt = q // 2, q % 2
                            mm = pe.matmul(pb(0)[64 * j:64 * j + 64, s * SEQ:(s + 1) * SEQ],
                                           vtok[g][:, 2 * s + kt, 64 * j:64 * j + 64], PTt[:, js, g, kt, :],
                                           start=(q == 0), stop=(q == 5))
                    mm.then_inc(o_mm.sem, 1)

                wait(pe, y_ok, l, 2 * GROUPS)
                wait_alone(pe, o_ok, l, 4)
                with pe.Fori(0, 4) as c2:
                    for h in range(2):
                        c, b = c2 * 2 + h, 4 * h
                        wait(pe, mT_ok, l, c - 1)
                        project(l, "mrg", c, 0, pb(b), hT).then_inc(ga_mm.sem, 1)
                        project(l, "mrg", c, 1, pb(b + 1), hT).then_inc(gb_mm.sem, 1)
                        project(l, "mrg", c, 2, pb(b + 2), yT, stop=False)
                        project(l, "mrg", c, 3, pb(b + 2), yT, start=False, k0=8).then_inc(pa_mm.sem, 1)
                        project(l, "mrg", c, 4, pb(b + 3), oT, n=4).then_inc(pb_mm.sem, 1)

                wait(pe, mT_ok, l, 8)
                for n in range(8):
                    tt, nh = n // 2, n % 2
                    for k in range(KD):
                        if n == 0:
                            loaded(pe, l, "out", 0, k)
                        mm = pe.matmul(pb(n), mT[:, k, tt * P:(tt + 1) * P], ring[k][:, nh * 512:(nh + 1) * 512],
                                       start=(k == 0), stop=(k == KD - 1))
                        if (n == 0 and k == 0) or (n == 7 and k < KD - 1):
                            mm.then_inc(slot_free.sem, 1)
                    mm.then_inc(out_mm.sem, 1)
                wait(pe, x_mid, l, 8)

                norm(l, 1)
                wait_alone(pe, hl_ok, l, 8)
                with pe.Fori(0, PH // 2) as h2:
                    for hh in range(2):
                        h = h2 * 2 + hh
                        for s in range(2):
                            wait_q = 2 * hh + s
                            project3(l, qry_split(h2, wait_q), wait_q, hi_q[s], pb(wait_q)).then_inc(q_mm.sem, 1)
                        for s in range(2):
                            wait(pe, q_ev, l, h * 2 + (s + 1))
                            for tt in range(NT):
                                mm = pe.matmul(pb(4 + 2 * hh + s)[:, tt * P:(tt + 1) * P],
                                               qT[2 * hh + s][:, tt * P:(tt + 1) * P],
                                               pr[:, PW_KEYS + s * P:PW_KEYS + (s + 1) * P], start=True, stop=True)
                            mm.then_inc(q_s.sem, 1)
                    wait(pe, q_sv, l, h2 * 4 + 4)
                wait(pe, g_ok, l, 1)
                for n, src in enumerate((ID[0], ID[1], Ge)):
                    for tt in range(NT):
                        mm = pe.transpose(pb(n)[:, tt * P:(tt + 1) * P], src[:, tt].rearrange("p h k -> p (h k)"), ident)
                    mm.then_inc(gt_mm.sem, 1)
                wait_alone(pe, gt_ok, l, 7)

                def outer(l, base, c):
                    wait(pe, h_ok, l, base + (c + 1))
                    for t in range(16):
                        mm = pe.matmul(routes[:, 2 * (c % 2) + t // 8, 64 * (t % 8):64 * (t % 8) + 48],
                                       Bh[c % 2][:, :, t], A3[c % 2][:, :, :, t], start=True, stop=True)
                    mm.then_inc(h_mm.sem, 1)

                with pe.Fori(0, BLOCKS) as b:
                    for c in range(8):
                        outer(l, b * 8, c)
                with pe.Fori(0, STRIPES // 2) as sp2:
                    for par2 in range(2):
                        with pe.Fori(0, BLOCKS) as b:
                            blk = sp2 * (2 * BLOCKS) + par2 * BLOCKS + b
                            base = blk * 8 + BLOCKS * 8
                            for j in range(4):
                                wait(pe, u_ge, l, blk * 4 + j - 1)
                                project3(l, peer_split(blk, j), (0, 1, 2, 0)[j], hi_u[j % 2], pb(j % 2)).then_inc(u_mm.sem, 1)
                                outer(l, base, j)

                            def values(n, j):
                                tt, nh = n // 2, n % 2
                                tok, cols = slice(tt * P, (tt + 1) * P), slice(nh * 512, (nh + 1) * 512)
                                return product3(pb(2 + n % 2), (gh_h[j][:, tok], gh_l[j][:, tok]),
                                                (hi_v[j][:, cols], lo[3 + j][:, cols]), j == 0, j == 3)

                            for n in range(2):
                                wait(pe, v_add, l, blk * 8 + n - 1)
                                for j in range(3):
                                    if n == 0:
                                        wait(pe, w_lo, l, peer_split(blk, 4 + j) + 1)
                                        wait(pe, gh_ok, l, blk * 4 + (j + 1))
                                    mm = values(n, j)
                                    if n == 0 and j == 0:
                                        mm[0].then_inc(slot_free.sem, 1)
                            wait(pe, w_lo, l, peer_split(blk, 7) + 1)
                            wait(pe, gh_ok, l, blk * 4 + 4)
                            for n in range(8):
                                if n < 2:
                                    mm = values(n, 3)
                                else:
                                    wait(pe, v_add, l, blk * 8 + n - 1)
                                    for j in range(4):
                                        mm = values(n, j)
                                        if n == 7 and j < 3:
                                            mm[-1].then_inc(slot_free.sem, 1)
                                mm[-1].then_inc(v_mm.sem, 1)
                                if n % 2:
                                    outer(l, base, 4 + n // 2)

        @block.scalar
        def _(act):
            act.dma_start(rel_w[0:REL_BUCKETS], rel).then_inc(rel_in, 16)
            act.dma_start(hot_rel[0:REL_BUCKETS], biases[0:32]).then_inc(rel_in, 16)
            act.dma_start(mask_rel[0:NG * 8], biases[32:56]).then_inc(rel_in, 16)
            act.wait_ge(rel_in, 48)

            def norm(l, w):
                if w == 0:
                    wait(act, v_add, l, 0)
                else:
                    wait(act, x_mid, l, 8)
                for tt in range(NT):
                    if tt:
                        wait(act, n_ss, l, 4 * w + tt)
                    act.activation((junk, junk2)[w], x[:, tt, :], ACT.Square, accum_out=stat[:, tt:tt + 1]).then_inc(n_ss.sem, 1)
                wait(act, n_ms, l, w + 1)
                act.activation(stat[:, 8:12], stat[:, 4:8], ACT.Sqrt).then_inc(n_sqrt.sem, 1)

            act.wait_ge(x_in, 32)
            with act.Fori(0, DEPTH) as l:
                norm(l, 0)
                wait(act, par_in, l, 16)
                act.activation(aexp, pr[:, PW_ALOG:PW_ALOG + 64], ACT.Exp).then_inc(dt_u.sem, 1)
                wait(act, dt_ax, l, 1)
                act.activation(du, dax, ACT.Exp, scale=-1.0).then_inc(dt_u.sem, 1)
                wait(act, dt_w, l, 1)
                act.activation(dln, dw, ACT.Ln).then_inc(dt_ln.sem, 1)

                with act.Fori(0, GROUPS) as g:
                    for n in range(8):
                        wait(act, arg, l, g * 8 + (n + 1))
                        act.activation(E[:, n, :], E[:, n, :], ACT.Exp).then_inc(ex.sem, 1)

                    def centre(j):
                        wait(act, c_mm, l, g * 4 + (j + 1))
                        act.activation(cx[j], pb(j), ACT.Identity, bias=gp[:, 8 * j + 5:8 * j + 6],
                                       scale=gp[:, 8 * j + 2:8 * j + 3]).then_inc(c_acc.sem, 1)

                    def silu(j):
                        wait(act, c_ok, l, g * 4 + (j + 1))
                        act.activation(cx[j], cx[j], ACT.Silu).then_inc(c_s.sem, 1)

                    def silu_z(i):
                        wait(act, z_mm, l, g * 2 + (i + 1))
                        act.activation(zs[i], pb(4 + i), ACT.Silu).then_inc(z_s.sem, 1)

                    wait(act, g_cp, l, g * 3 + 3)
                    centre(0)
                    centre(1)
                    silu(0)
                    centre(2)
                    silu(1)
                    centre(3)
                    silu(2)
                    silu_z(0)
                    silu(3)
                    silu_z(1)
                    for i in range(2):
                        wait(act, xt_mm, l, g * 2 + (i + 1))
                        act.activation(xtok[:, :, i * P:(i + 1) * P], pb(6 + i).rearrange("p (t c) -> p t c", t=NT),
                                       ACT.Copy).then_inc(xt_ok.sem, 1)
                    for i in range(2):
                        wait(act, y3_ok, l, g * 2 + (i + 1))
                        wait(act, sq_sum, l, g * 2 + i)
                        act.activation(sq[i], y3[i], ACT.Square).then_inc(sq_ok.sem, 1)
                        act.activation(yT[:, g * 2 + i, :], y3[i], ACT.Copy,
                                       scale=gp[:, 8 * (2 + i) + 7:8 * (2 + i) + 8]).then_inc(y_ok.sem, 1)
                wait(act, r_ms, l, 1)
                act.activation(sqsum, sqsum, ACT.Sqrt).then_inc(r_sq.sem, 1)
                wait_alone(act, r_ok, l, 1)

                with act.Fori(0, 4) as hp:
                    for u in range(0, 9, 2):
                        dst = qk[u] if u < 6 else vraw[u - 6]
                        wait(act, p_mm, l, hp * 9 + (u + 1))
                        act.activation(dst, pb(u % 4), ACT.Copy, scale=HD ** -0.5 if u < 6 else 1.0).then_inc(p_evA.sem, 1)
                    for g in range(NG):
                        wait(act, vt_mm, l, hp * 3 + (g + 1))
                        act.activation(vtok[g], pb(4 + g).rearrange("p (t c) -> p t c", t=NT),
                                       ACT.Copy).then_inc(vt_ok.sem, 1)
                    for c in range(8):
                        wait(act, s_nm, l, hp * 8 + (c + 1))
                        for g in range(NG):
                            ins = act.activation(Pm[:, c, g, :], Pm[:, c, g, :], ACT.Exp, bias=nm[:, c, g:g + 1],
                                                 accum_out=den[:, c, g:g + 1])
                        ins.then_inc(p_x.sem, 1)
                    wait(act, a_v, l, hp * 6 + 2)
                    act.activation(wg, wg, ACT.Exp).then_inc(a_w.sem, 1)
                    for n in range(0, 12, 2):
                        wait(act, t_mm, l, hp * 12 + (n + 1))
                        js, m = n // 3, n % 3
                        act.activation(PTt[:, js].rearrange("p g k q -> p (g k q)")[:, m * 512:(m + 1) * 512],
                                       pb(4 + n % 4), ACT.Copy).then_inc(t_evA.sem, 1)
                    wait(act, o_mm, l, hp + 1)
                    act.activation(oT[:, hp, :], pb(0), ACT.Copy).then_inc(o_ok.sem, 1)

                with act.Fori(0, 4) as c2:
                    for h in range(2):
                        c, b = c2 * 2 + h, 4 * h
                        wait(act, mT_ok, l, c - 1)
                        wait(act, ga_mm, l, c + 1)
                        act.activation(sg[2 * h], pb(b), ACT.Sigmoid).then_inc(sg_ok.sem, 1)
                        wait(act, gb_mm, l, c + 1)
                        act.activation(sg[2 * h + 1], pb(b + 1), ACT.Sigmoid).then_inc(sg_ok.sem, 1)

                norm(l, 1)
                for n in range(8):
                    wait(act, hT_ok, l, 8 + (n + 1))
                    act.activation(h_piece(hT_hi, n), h_piece(hT, n), ACT.Copy).then_inc(hh_ok.sem, 1)

                def high(name, i, j, slot, hi):
                    loaded(act, l, name, i, j)
                    act.activation(hi[:, :], ring[slot][:, :], ACT.Copy).then_inc(w_hi.sem, 1)

                with act.Fori(0, PH // 2) as h2:
                    def high_q(n):
                        high("qry", h2, n, n, hi_q[n % 2])

                    def query(n):
                        wait(act, q_mm, l, h2 * 4 + (n + 1))
                        act.activation(qT[n], pb(n), ACT.Copy).then_inc(q_ev.sem, 1)

                    def scores(hh):
                        wait(act, k_done, l, h2 * 2 + hh - 1)
                        for s in range(2):
                            wait(act, q_s, l, h2 * 4 + (2 * hh + s + 1))
                            act.activation(sc[hh][:, s], pb(4 + 2 * hh + s).rearrange("p (t n) -> p t n", t=NT),
                                           ACT.Copy).then_inc(q_sv.sem, 1)

                    high_q(0)
                    high_q(1)
                    query(0)
                    high_q(2)
                    query(1)
                    high_q(3)
                    scores(0)
                    query(2)
                    query(3)
                    scores(1)
                wait(act, g_v, l, 1)
                act.activation(Ge, Ge, ACT.Exp).then_inc(g_e.sem, 1)
                wait(act, gt_mm, l, 3)

                with act.Fori(0, STRIPES * BLOCKS) as blk:
                    def high_p(n):
                        high("peer", blk, n, PHASES[-1][2][n], hi_u[n % 2] if n < 4 else hi_v[n - 4])

                    def gelu(j):
                        wait(act, u_mm, l, blk * 4 + (j + 1))
                        act.activation(gh[j], pb(j % 2), ACT.Gelu).then_inc(u_ge.sem, 1)

                    def routed_high(j):
                        wait(act, gh_m, l, blk * 4 + (j + 1))
                        act.activation(gh_h[j][:, :], gh[j], ACT.Copy).then_inc(gh_hi.sem, 1)

                    high_p(0)
                    high_p(1)
                    gelu(0)
                    high_p(2)
                    high_p(4)
                    gelu(1)
                    high_p(3)
                    routed_high(0)
                    high_p(5)
                    gelu(2)
                    routed_high(1)
                    high_p(6)
                    high_p(7)
                    gelu(3)
                    routed_high(2)
                    routed_high(3)

            act.wait_ge(v_add.sem, v_add.at(DEPTH, 0))
            for tt in range(NT):
                if tt:
                    act.wait_ge(f_ss, tt)
                act.activation(fjunk, x[:, tt, :], ACT.Square, accum_out=stat[:, tt:tt + 1]).then_inc(f_ss, 1)
            act.wait_ge(f_v, 1)
            act.activation(stat[:, 8:12], stat[:, 4:8], ACT.Sqrt).then_inc(f_sq, 1)

        @block.vector
        def _(v):
            v.sem_inc(z_s.sem, 2)
            v.sem_inc(y_v.sem, 2)
            v.sem_inc(y_ok.sem, 2)
            v.sem_inc(sq_sum.sem, 2)
            v.sem_inc(o_ok.sem, 1)
            v.sem_inc(mT_ok.sem, 2)
            v.sem_inc(k_done.sem, 2)
            v.sem_inc(u_ge.sem, 2)
            v.wait_ge(cst_in, 16)
            v.tensor_copy(iota_b[:, :, :], spread(cst[:, C_IOTA:C_IOTA + 144], 2, 16)).then_inc(iota_ok, 1)
            v.wait_ge(rel_in, 48)
            v.wait_ge(rel_mm, 1)
            v.tensor_tensor(oT[0:NG * 8, 0, :], pb(0)[0:NG * 8, :], mask_rel[0:NG * 8], ALU.add).then_inc(row_ok, 1)
            v.wait_ge(iota_ok, 1)
            v.wait_ge(row_out, 16)
            v.wait_ge(x_in, 32)
            v.memset(stat[:, 60:61], 0.0).then_inc(v_add.sem, 2)

            def norm(l, w):
                wait(v, n_ss, l, 4 * w + 4)
                v.tensor_scalar(stat[:, 4:8], stat[:, 0:4], 1.0 / D, EPS, ALU.mult, ALU.add).then_inc(n_ms.sem, 1)
                wait(v, n_sqrt, l, w + 1)
                v.reciprocal(stat[:, 12:16], stat[:, 8:12]).then_inc(n_rs.sem, 1)
                wait(v, n_rs, l, w + 1)
                wait(v, par_in, l, 16)

                def scale(tt):
                    if tt >= 2:
                        wait(v, n_tr, l, 8 * w + 2 * (tt - 1))
                    v.tensor_scalar((xn, xn2)[w][tt % 2], x[:, tt, :], stat[:, 12 + tt:13 + tt], None, ALU.mult).then_inc(n_xn.sem, 1)

                def store(tt):
                    for half in range(2):
                        wait(v, n_tr, l, 8 * w + 2 * tt + half + 1)
                        o = (PW_N1, PW_N2)[w] + 4 * half
                        v.tensor_tensor(hT[:, 4 * half:4 * half + 4, tt * P:(tt + 1) * P],
                                        pb(2 * (tt % 2) + half).rearrange("p (k t) -> p k t", k=4),
                                        spread(pr[:, o:o + 4], 2, P), ALU.mult).then_inc(hT_ok.sem, 1)

                scale(0)
                scale(1)
                store(0)
                scale(2)
                store(1)
                scale(3)
                store(2)
                store(3)

            with v.Fori(0, DEPTH) as l:
                norm(l, 0)
                step = [0]

                def link(ins):
                    step[0] += 1
                    ins.then_inc(dt_v.sem, 1)
                    wait(v, dt_v, l, step[0])

                wait(v, dt_mm, l, 1)
                link(v.tensor_tensor(dr0, pb(4)[:, 0:256].rearrange("p (t h) -> p t h", t=NT),
                                     spread(pr[:, PW_DTB:PW_DTB + 64], 1, NT), ALU.add))
                v.scalar_tensor_tensor(out=dax, in0=dr0, scalar=-1.0, in1=dr0, op0=ALU.mult, op1=ALU.max).then_inc(dt_ax.sem, 1)
                wait(v, dt_u, l, 2)
                v.tensor_scalar(dw, du, 1.0, None, ALU.add).then_inc(dt_w.sem, 1)
                wait(v, dt_w, l, 1)
                link(v.tensor_scalar(dd, dw, -1.0, None, ALU.add))
                link(v.tensor_scalar(dz, dd, 0.0, None, ALU.is_equal))
                link(v.tensor_tensor(dd, dd, dz, ALU.add))
                link(v.reciprocal(dd, dd))
                wait(v, dt_ln, l, 1)
                link(v.tensor_tensor(dd, dd, dln, ALU.mult))
                link(v.tensor_tensor(dd, dd, dz, ALU.add))
                link(v.tensor_tensor(dd, dd, du, ALU.mult))
                link(v.scalar_tensor_tensor(out=dtv, in0=dr0, scalar=0.0, in1=dd, op0=ALU.max, op1=ALU.add))
                v.scalar_tensor_tensor(out=da, in0=dtv, scalar=-1.0, in1=spread(aexp, 1, NT),
                                       op0=ALU.mult, op1=ALU.mult).then_inc(dt_a.sem, 1)
                wait(v, dt_cs, l, 1)
                v.tensor_scalar(negA, pb(5)[:, 0:256].rearrange("p (t h) -> p t h", t=NT), -1.0, None,
                                ALU.mult).then_inc(dt_T.sem, 1)
                for d in range(2):
                    v.tensor_copy(aT[0:32, d, :], pb(6 + d)[0:32, :]).then_inc(dt_T.sem, 1)
                wait_alone(v, dt_T, l, 3)

                with v.Fori(0, GROUPS) as g:
                    wait(v, y_ok, l, g * 2)
                    v.tensor_copy(gneg, negA.rearrange("p t (d h) -> p t d h", d=2)[:, :, :, bass.ds(g * RH, RH)]).then_inc(g_cp.sem, 1)
                    v.tensor_copy(gdt, dtv.rearrange("p t (d h) -> p t d h", d=2)[:, :, :, bass.ds(g * RH, RH)]).then_inc(g_cp.sem, 1)
                    v.tensor_copy(gp, pr[:, bass.ds(g * 32 + PW_CONV, 32)]).then_inc(g_cp.sem, 1)
                    wait(v, g_cp, l, g * 3 + 3)
                    wait(v, bc_in, l, g * 16 + 16)
                    for n in range(8):
                        r, s = 2 * (n // 4) + (n % 4) // 2, n % 2
                        parts = [(0, 0, 0, 256, 0, C_MF), (1, 1, 256, 256, 0, C_MB), (1, 0, 512, 128, 0, C_MB + P),
                                 (0, 1, 640, 128, 128, C_MF)]
                        for d, si, c0, w, l0, m in parts:
                            ins = v.scalar_tensor_tensor(
                                out=E[:, n, c0:c0 + w], in0=aBC[:, d, r, s * SEQ + l0:s * SEQ + l0 + w],
                                scalar=gneg[:, 2 * s + si, d, r:r + 1], in1=cst[:, m:m + w], op0=ALU.add, op1=ALU.add)
                        ins.then_inc(arg.sem, 1)
                    for j in range(4):
                        wait(v, c_acc, l, g * 4 + (j + 1))
                        for q, k in enumerate((0, 1, 3, 4)):
                            o = k - CONV // 2
                            lo, w = max(0, -o), SEQ - abs(o)
                            acc = cx[j].rearrange("p (s t) -> p s t", s=NSEQ)[:, :, lo:lo + w]
                            src = pb(j).rearrange("p (s t) -> p s t", s=NSEQ)[:, :, lo + o:lo + o + w]
                            ins = v.scalar_tensor_tensor(out=acc, in0=src, scalar=gp[:, 8 * j + k:8 * j + k + 1], in1=acc,
                                                         op0=ALU.mult, op1=ALU.add)
                            if q < 3:
                                ins.then_inc(c_tap.sem, 1)
                                wait(v, c_tap, l, g * 12 + (3 * j + q + 1))
                            else:
                                ins.then_inc(c_ok.sem, 1)
                    wait(v, xt_ok, l, g * 2 + 2)
                    for d in range(2):
                        v.tensor_tensor(xdt[d].rearrange("p t (r e) -> p t r e", r=RH),
                                        xtok.rearrange("p t (r e) -> p t r e", r=RH),
                                        spread(gdt[:, :, d, :], 3, HD), ALU.mult).then_inc(xd_ok.sem, 1)
                    for n in range(8):
                        s = n % 2
                        wait(v, cb_mm, l, g * 2 + 2)
                        wait(v, ex, l, g * 8 + (n + 1))
                        v.tensor_tensor(E[:, n, 0:512], E[:, n, 0:512], pb(s), ALU.mult)
                        two = pb(s)[:, 0:512].rearrange("p (a b) -> p a b", b=P)[:, 0:4:3, :]
                        v.tensor_tensor(E[:, n, 512:768].rearrange("p (a b) -> p a b", b=P),
                                        E[:, n, 512:768].rearrange("p (a b) -> p a b", b=P), two, ALU.mult).then_inc(m_ok.sem, 1)
                    for i in range(2):
                        wait(v, y_mm, l, g * 2 + (i + 1))
                        q = 8 * (2 + i) + 6
                        v.scalar_tensor_tensor(out=y3[i], in0=cx[2 + i], scalar=gp[:, q:q + 1], in1=pb(2 + i),
                                               op0=ALU.mult, op1=ALU.add).then_inc(y_v.sem, 1)
                        wait(v, y_v, l, g * 2 + (i + 1))
                        wait(v, z_s, l, g * 2 + (i + 1))
                        v.tensor_tensor(y3[i], y3[i], zs[i], ALU.mult).then_inc(y3_ok.sem, 1)
                wait(v, r_mm, l, 1)
                v.tensor_scalar(sqsum, pb(4), 1.0 / D_INNER, EPS, ALU.mult, ALU.add).then_inc(r_ms.sem, 1)
                wait(v, r_sq, l, 1)
                wait(v, y_ok, l, 2 * GROUPS)
                v.reciprocal(rstdB, sqsum).then_inc(r_ok.sem, 1)

                with v.Fori(0, 4) as hp:
                    for u in range(1, 9, 2):
                        dst = qk[u] if u < 6 else vraw[u - 6]
                        wait(v, p_mm, l, hp * 9 + (u + 1))
                        v.tensor_copy(dst, pb(u % 4)).then_inc(p_evV.sem, 1)
                    wait(v, bm_in, l, hp * 16 + 16)
                    for c in range(8):
                        j, qt = c // 4, c % 2
                        wait_alone(v, s_mm, l, hp * 8 + (c + 1))
                        for g in range(NG):
                            ins = v.tensor_tensor_reduce(
                                Pm[:, c, g, :], pb(2 * (c % 2) + g // 2)[:, (g % 2) * SEQ:(g % 2 + 1) * SEQ],
                                BM[:, qt, 3 * j + g, :], 1.0, -3e38, ALU.add, ALU.max, mx[:, c, g:g + 1])
                        ins.then_inc(s_v.sem, 1)
                        wait(v, s_v, l, hp * 8 + (c + 1))
                        v.tensor_scalar(nm[:, c, :], mx[:, c, :], -1.0, None, ALU.mult).then_inc(s_nm.sem, 1)
                    st = [0]

                    def link(ins):
                        st[0] += 1
                        ins.then_inc(a_v.sem, 1)
                        wait(v, a_v, l, hp * 6 + st[0])

                    link(v.tensor_reduce(m1, mx, AX, ALU.max))
                    link(v.tensor_tensor(wg, mx, spread(m1, 2, NG), ALU.subtract))
                    wait(v, a_w, l, hp + 1)
                    wait(v, p_x, l, hp * 8 + 8)
                    link(v.tensor_tensor(fw, wg, den, ALU.mult))
                    link(v.tensor_reduce(s1, fw, AX, ALU.add))
                    link(v.reciprocal(r1, s1))
                    link(v.tensor_tensor(fw, wg, spread(r1, 2, NG), ALU.mult))
                    assert st[0] == 6
                    for c in range(8):
                        for g in range(NG):
                            ins = v.tensor_scalar(Pm[:, c, g, :], Pm[:, c, g, :], fw[:, c, g:g + 1], None, ALU.mult)
                        ins.then_inc(p_f.sem, 1)
                    for n in range(1, 12, 2):
                        wait(v, t_mm, l, hp * 12 + (n + 1))
                        js, m = n // 3, n % 3
                        v.tensor_copy(PTt[:, js].rearrange("p g k q -> p (g k q)")[:, m * 512:(m + 1) * 512],
                                      pb(4 + n % 4)).then_inc(t_evV.sem, 1)

                with v.Fori(0, 4) as c2:
                    for h in range(2):
                        c, b = c2 * 2 + h, 4 * h
                        wait(v, mT_ok, l, c)
                        wait(v, pa_mm, l, c + 1)
                        v.tensor_tensor(t1, pb(b + 2), rstdB, ALU.mult).then_inc(m_v.sem, 1)
                        wait(v, m_v, l, c * 3 + 1)
                        wait(v, sg_ok, l, c * 2 + 2)
                        v.tensor_tensor(t1, t1, sg[2 * h], ALU.mult).then_inc(m_v.sem, 1)
                        wait(v, pb_mm, l, c + 1)
                        v.tensor_tensor(t2, pb(b + 3), sg[2 * h + 1], ALU.mult).then_inc(m_v.sem, 1)
                        wait(v, m_v, l, c * 3 + 3)
                        v.tensor_tensor(mT[:, c, :], t1, t2, ALU.add).then_inc(mT_ok.sem, 1)

                for n in range(8):
                    tt, nh = n // 2, n % 2
                    xo = x[:, tt, nh * 512:(nh + 1) * 512]
                    wait(v, out_mm, l, n + 1)
                    v.tensor_tensor(xo, xo, pb(n), ALU.add).then_inc(x_mid.sem, 1)

                norm(l, 1)
                for n in range(8):
                    wait(v, hh_ok, l, n + 1)
                    v.tensor_tensor(h_piece(hT_lo, n), h_piece(hT, n), h_piece(hT_hi, n), ALU.subtract).then_inc(hl_ok.sem, 1)
                with v.Fori(0, PH // 2) as h2:
                    for hh in range(2):
                        h = h2 * 2 + hh
                        st = [0]

                        def link(ins):
                            st[0] += 1
                            ins.then_inc(k_v.sem, 1)
                            wait_alone(v, k_v, l, h * TK + st[0])

                        def top16(src, tmp, val, idx, n):
                            for i in range(n):
                                ins = v.max(val(i)[:, 0:8], src(i))
                            link(ins)
                            for i in range(n):
                                v.max_index(idx(i)[:, 0:8], val(i)[:, 0:8], src(i))
                                ins = v.match_replace(out=tmp(i), in_to_replace=val(i)[:, 0:8], in_values=src(i), imm_value=-3e38)
                            link(ins)
                            for i in range(n):
                                ins = v.max(val(i)[:, 8:16], tmp(i))
                            link(ins)
                            for i in range(n):
                                ins = v.max_index(idx(i)[:, 8:16], val(i)[:, 8:16], tmp(i))
                            link(ins)

                        wait_alone(v, q_sv, l, h * 2 + 2)
                        top16(lambda i: sc[hh][:, i // NT, i % NT, :], lambda i: sc2[:, i // NT, i % NT, :],
                              lambda i: v16[:, i // NT, i % NT, :], lambda i: x16[:, i // NT, i % NT, :], 2 * NT)
                        v.tensor_copy(f16, x16)
                        link(v.tensor_tensor(cand.rearrange("p t (i j) -> p t i j", i=16), spread(v16[:, 0], 3, 16),
                                             spread(v16[:, 1], 2, 16), ALU.add))
                        top16(lambda i: cand[:, i, :], lambda i: cand2[:, i, :], lambda i: cvh[:, i, :],
                              lambda i: ci.rearrange("p (t k) -> p t k", t=NT)[:, i, :], NT)
                        v.tensor_scalar(pij[:, 0, :], ci, 4, None, ALU.logical_shift_right)
                        link(v.tensor_scalar(pij[:, 1, :], ci, 15, None, ALU.bitwise_and))
                        link(v.tensor_copy(pf, pij))
                        for q in range(2):
                            flat = hot.rearrange("p t k j -> p (t k) j")
                            link(v.tensor_tensor(flat, spread(pf[:, q, :], 2, 16),
                                                 spread(cst[:, C_I16:C_I16 + 16], 1, NT * TOPK), ALU.is_equal))
                            link(v.tensor_tensor(hot, hot, spread(f16[:, q], 2, TOPK), ALU.mult))
                            ins = v.tensor_reduce(idh[:, q, :], flat, AX, ALU.add)
                            if q == 0:
                                link(ins)
                            else:
                                ins.then_inc(k_done.sem, 1)
                        assert st[0] == TK, st[0]
                        wait(v, k_done, l, h + 1)
                        v.tensor_copy(CV[:, :, h, :], cvh)
                        for q in range(2):
                            v.tensor_copy(ID[q][:, :, h, :], idh[:, q].rearrange("p (t k) -> p t k", t=NT))
                wait(v, k_done, l, PH)
                flat = [a.rearrange("p t h k -> p (t h) k") for a in (CV, Ge)]
                v.memset(gsum, 0.0).then_inc(g_fence.sem, 1)
                wait(v, g_fence, l, 1)
                v.tensor_tensor(flat[1], flat[0], spread(flat[0][:, :, 0], 2, TOPK), ALU.subtract).then_inc(g_v.sem, 1)
                wait(v, g_e, l, 1)
                v.tensor_reduce(gsum, flat[1], AX, ALU.add).then_inc(g_v.sem, 1)
                wait(v, g_v, l, 2)
                v.reciprocal(grec, gsum).then_inc(g_v.sem, 1)
                wait(v, g_v, l, 3)
                v.tensor_tensor(flat[1], flat[1], spread(grec, 2, TOPK), ALU.mult).then_inc(g_ok.sem, 1)
                for q in range(2):
                    wait(v, gt_mm, l, q + 1)
                    v.tensor_copy(idT[q], pb(q)).then_inc(gt_ok.sem, 1)
                wait(v, gt_mm, l, 3)
                v.tensor_copy(gP[:, 0, :], pb(2)).then_inc(gt_ok.sem, 1)
                wait(v, gt_ok, l, 3)
                v.tensor_tensor(gr[0], pb(2), gP[:, 0, :], ALU.subtract).then_inc(gt_ok.sem, 1)
                wait(v, gt_ok, l, 4)
                v.tensor_copy(gP[:, 1, :], gr[0]).then_inc(gt_ok.sem, 1)
                wait(v, gt_ok, l, 5)
                v.tensor_tensor(gr[1], gr[0], gP[:, 1, :], ALU.subtract).then_inc(gt_ok.sem, 1)
                wait(v, gt_ok, l, 6)
                v.tensor_copy(gP[:, 2, :], gr[1]).then_inc(gt_ok.sem, 1)
                wait_alone(v, gt_ok, l, 7)

                def one_hots(l, base, stripe, tok, c):
                    n0 = base + (c + 1)
                    o = tok + 16 * c
                    v.tensor_tensor(eq[c % 2], spread(idT[0][:, bass.ds(o, 16)], 1, 16),
                                    iota_b[:, bass.ds(stripe * 16, 16), :], ALU.is_equal).then_inc(h_eq.sem, 1)
                    v.tensor_tensor(Bh[c % 2], spread(idT[1][:, bass.ds(o, 16)], 1, P), iota_b[:, 0:P, :], ALU.is_equal)
                    wait(v, h_eq, l, n0)
                    v.tensor_tensor(A3[c % 2], spread(eq[c % 2], 1, 3), spread(gP[:, :, bass.ds(o, 16)], 2, 16),
                                    ALU.mult).then_inc(h_ok.sem, 1)

                def collect(l, base, G, tok, c):
                    wait(v, h_mm, l, base + (c + 1))
                    src = routes[:, 2 * (c % 2):2 * (c % 2) + 2, :].rearrange("p a (t x) -> p (a t) x", x=64)
                    src = src[:, :, 0:48].rearrange("p t (q n) -> p n t q", q=3)
                    v.tensor_reduce(G[:, :, bass.ds(tok + 16 * c, 16)], src, AX, ALU.add).then_inc(G_ok.sem, 1)

                with v.Fori(0, BLOCKS) as b:
                    for c in range(0, 8, 2):
                        one_hots(l, b * 8, 0, b * P, c)
                        one_hots(l, b * 8, 0, b * P, c + 1)
                        collect(l, b * 8, Gs[0], b * P, c)
                        collect(l, b * 8, Gs[0], b * P, c + 1)
                with v.Fori(0, STRIPES // 2) as sp2:
                    for par2 in range(2):
                        with v.Fori(0, BLOCKS) as b:
                            stripe = sp2 * 2 + par2
                            blk = sp2 * (2 * BLOCKS) + par2 * BLOCKS + b
                            base = blk * 8 + BLOCKS * 8
                            G, G_next = Gs[par2], Gs[1 - par2]

                            def routed(j):
                                wait(v, u_ge, l, blk * 4 + (j + 1))
                                wait(v, G_ok, l, stripe * (8 * BLOCKS) + 8 * BLOCKS)
                                v.tensor_tensor(gh[j], gh[j], G[:, b * 4 + j, :], ALU.mult).then_inc(gh_m.sem, 1)

                            def routed_low(j):
                                wait(v, gh_hi, l, blk * 4 + (j + 1))
                                v.tensor_tensor(gh_l[j][:, :], gh[j], gh_h[j][:, :], ALU.subtract).then_inc(gh_ok.sem, 1)

                            for j in range(4):
                                one_hots(l, base, stripe + 1, b * P, j)
                                if j:
                                    collect(l, base, G_next, b * P, j - 1)
                                routed(j)
                                if j:
                                    routed_low(j - 1)
                            routed_low(3)
                            for n in range(8):
                                tt, nh = n // 2, n % 2
                                xo = x[:, tt, nh * 512:(nh + 1) * 512]
                                if n % 2 == 0:
                                    collect(l, base, G_next, b * P, 3 + n // 2)
                                    one_hots(l, base, stripe + 1, b * P, 4 + n // 2)
                                wait(v, v_mm, l, blk * 8 + (n + 1))
                                v.tensor_tensor(xo, xo, pb(2 + n % 2), ALU.add).then_inc(v_add.sem, 1)
                            collect(l, base, G_next, b * P, 7)

            v.wait_ge(f_w, 16)
            v.wait_ge(f_ss, 4)
            v.tensor_scalar(stat[:, 4:8], stat[:, 0:4], 1.0 / D, EPS, ALU.mult, ALU.add).then_inc(f_v, 1)
            v.wait_ge(f_sq, 1)
            v.reciprocal(stat[:, 12:16], stat[:, 8:12]).then_inc(f_v, 1)
            v.wait_ge(f_v, 2)
            for tt in range(NT):
                if tt >= 2:
                    v.wait_ge(f_out, 16 * (tt - 1))
                v.scalar_tensor_tensor(out=fin[tt % 2], in0=x[:, tt, :], scalar=stat[:, 12 + tt:13 + tt], in1=wfin,
                                       op0=ALU.mult, op1=ALU.mult).then_inc(f_ok, 1)


def unit_tiles(w, cols):
    k = w.shape[0] // P
    r = w.reshape(k, P, -1)
    return np.stack([np.ascontiguousarray(r[:, :, c:c + P].transpose(1, 0, 2)).reshape(P, k * P) for c in cols])


def lay_out(i):
    w_in = i["w_in"]
    w_ssd, w_att, w_mrg, w_qry, w_u, par = [], [], [], [], [], []
    for l in range(DEPTH):
        w = w_in[l]
        r = range(GROUPS)
        cols = [[OFF_XBC + D_INNER + g * P, OFF_XBC + D_INNER + (GROUPS + g) * P, OFF_XBC + 2 * g * P,
                 OFF_XBC + (2 * g + 1) * P, 2 * g * P, (2 * g + 1) * P] for g in r]
        w_ssd.append(np.stack([unit_tiles(w, c) for c in cols]))
        cols = [[o + g * 512 + hp * P for g in range(NG) for o in (OFF_Q, OFF_K)]
                + [OFF_V + g * 512 + hp * P for g in range(NG)] for hp in range(4)]
        w_att.append(np.stack([unit_tiles(w, c) for c in cols]))
        m = np.zeros((8, 5, P, UNIT), np.float32)
        for c in range(8):
            m[c, 0:2] = unit_tiles(w, [OFF_GATE + c * P, OFF_GATE + D + c * P])
            m[c, 2] = unit_tiles(i["w_ssd_out"][l][:D], [c * P])[0]
            m[c, 3] = unit_tiles(i["w_ssd_out"][l][D:], [c * P])[0]
            m[c, 4, :, 0:512] = unit_tiles(i["w_attn_out"][l], [c * P])[0]
        w_mrg.append(m)
        w_qry.append(unit_tiles(i["w_query"][l], [n * P for n in range(2 * PH)]).reshape(PH // 2, 4, P, UNIT))
        u = i["expert_u"][l].reshape(EXPERT_TILES, P, KD, P)
        w_u.append(u.transpose(0, 3, 2, 1).reshape(STRIPES * BLOCKS, 4, P, UNIT))
        q = np.zeros((P, PW), np.float32)
        q[:, PW_N1:PW_N1 + KD] = i["norm1_w"][l].reshape(KD, P).T
        q[:, PW_N2:PW_N2 + KD] = i["norm2_w"][l].reshape(KD, P).T
        skip = np.repeat(i["D_skip"][l], HD)
        for g in r:
            for t, ch in enumerate((D_INNER + g * P, D_INNER + (GROUPS + g) * P, 2 * g * P, (2 * g + 1) * P)):
                o = PW_CONV + g * 32 + t * 8
                q[:, o:o + CONV] = i["conv_w"][l][:, ch:ch + P].T
                q[:, o + 5] = i["conv_b"][l][ch:ch + P]
                if t >= 2:
                    q[:, o + 6] = skip[ch:ch + P]
                    q[:, o + 7] = i["ssd_norm_w"][l][ch:ch + P]
        q[:, PW_DTB:PW_DTB + 64] = i["dt_bias"][l].reshape(1, 64)
        q[:, PW_ALOG:PW_ALOG + 64] = i["A_log"][l].reshape(1, 64)
        q[:, PW_KEYS:PW_KEYS + 256] = i["sub_keys"][l].transpose(2, 0, 1).reshape(P, 256)
        q[:, PW_WDT:PW] = w[:, OFF_DT:OFF_Q].reshape(KD, P, 64).transpose(1, 0, 2).reshape(P, KD * 64)
        par.append(q)
    par.append(par[0])
    return {
        "x_prompt": i["x_prompt"], "x_sample": i["x_sample"], "consts": constants(), "biases": bias_constants(),
        "rel": i["rel_bias"], "par": np.stack(par), "w_ssd": np.stack(w_ssd), "w_att": np.stack(w_att),
        "w_mrg": np.stack(w_mrg), "w_out": i["w_out"].reshape(DEPTH, KD, P, D), "w_qry": np.stack(w_qry),
        "w_u": np.stack(w_u), "w_v": i["expert_v"].reshape(DEPTH, STRIPES * BLOCKS, 4, P, D),
        "w_final": i["final_norm_w"],
    }


def kernel(**inputs):
    import numpy as _np
    import concourse.bacc as _bacc
    from concourse.bass_utils import run_bass_kernel_spmd as _run

    nc = _bacc.Bacc("TRN2", target_bir_lowering=False, num_devices=1)
    arrays, args = {}, {}
    for name, a in lay_out({k: _np.asarray(v) for k, v in inputs.items()}).items():
        a = _np.ascontiguousarray(a)
        arrays[f"in_{name}"] = a
        args[name] = nc.dram_tensor(f"in_{name}", a.shape, F32, kind="ExternalInput").ap()
    for name in ("y_prompt", "y_sample"):
        args[name] = nc.dram_tensor(f"out_{name}", (1, SEQ, D), F32, kind="ExternalOutput").ap()
    build(nc, **args)
    r = _run(nc, [arrays], core_ids=[0])
    return tuple(r.results[0][f"out_{n}"] for n in ("y_prompt", "y_sample"))
```

```python
from contextlib import ExitStack

import numpy as np
import concourse.bass as bass
from concourse import mybir

F32 = mybir.dt.float32
F32R = mybir.dt.float32r
BF16 = mybir.dt.bfloat16
U32 = mybir.dt.uint32
ALU = mybir.AluOpType
ACT = mybir.ActivationFunctionType
AX = mybir.AxisListType.X

P = 128
D = 1024
KD = D // P
SEQ = 256
NSEQ = 2
T = NSEQ * SEQ
NT = T // P
DEPTH = 2
D_INNER = 2048
GROUPS = 8
RH = 4
HD = 64
SSD_HEADS = 32
CONV = 5
CONV_DIM = D_INNER + 2 * GROUPS * P
ATTN_WIDTH = 1536
NG = 3
WINDOWS = ((128, 1), (512, 4), (2048, 16))
REL_BUCKETS = 32
REL_MAX = 1024
PH = 8
TOPK = 16
EXPERT_TILES = 128
EPS = 1e-6
OFF_XBC = D_INNER
OFF_DT = OFF_XBC + CONV_DIM
OFF_Q = OFF_DT + 2 * SSD_HEADS
OFF_K = OFF_Q + ATTN_WIDTH
OFF_V = OFF_K + ATTN_WIDTH
OFF_GATE = OFF_V + ATTN_WIDTH
NEG = -1e30

UNIT = KD * P
SLOTS = 7
CREDIT = 16
STRIPES = 8
BLOCKS = 4
PHASES = (("ssd", GROUPS, (0, 1, 2, 3, 4, 5)), ("att", 4, (0, 1, 2, 3, 4, 5, 6, 2, 3)), ("mrg", 8, (0, 1, 2, 3, 4)),
          ("out", 1, (0, 1, 2, 3, 4, 5, 6, 2)), ("qry", PH // 2, (0, 1, 2, 3)),
          ("peer", STRIPES * BLOCKS, (0, 1, 2, 0, 3, 4, 5, 6)))
NAMES = [q[0] for q in PHASES]
UNITS = sum(i * len(n) for _, i, n in PHASES)
BASE = {}
LOADS = {}
_u = 0
_per_slot = [0] * SLOTS
for _name, _i, _n in PHASES:
    BASE[_name] = _u
    LOADS[_name] = list(_per_slot)
    _u += _i * len(_n)
    for _j in _n:
        _per_slot[_j] += _i
SLOT_LOADS = list(_per_slot)


def last_user(name, j):
    k = NAMES.index(name)
    slot = PHASES[k][2][j]
    for jj in range(j - 1, -1, -1):
        if PHASES[k][2][jj] == slot:
            return BASE[name] + jj
    for back in range(1, len(PHASES) + 1):
        pn, it, slots = PHASES[(k - back) % len(PHASES)]
        for jj in range(len(slots) - 1, -1, -1):
            if slots[jj] == slot:
                return BASE[pn] + (it - 1) * len(slots) + jj - (UNITS if k - back < 0 else 0)
    raise ValueError(name)


SPLIT = {}
_u = 0
for _name, _i, _n in PHASES:
    SPLIT[_name] = _u
    _u += _i * (4 if _name == "mrg" else len(_n))
SPLITS = _u
SPLIT_PEER = (0, 1, 2, 4, 3, 5, 6, 7)
LOAD_PEER = (0, 1, 2, 4, 5, 3, 6, 7)


PW_N1, PW_N2, PW_CONV = 0, 8, 16
PW_DTB = PW_CONV + GROUPS * 32
PW_ALOG = PW_DTB + 64
PW_KEYS = PW_ALOG + 64
PW_WDT = PW_KEYS + 256
PW = PW_WDT + KD * 64

C_ID, C_LE, C_GE, C_ONE, C_MF, C_MB, C_I16, C_IOTA = 0, 128, 256, 384, 512, 768, 1024, 1040
CW = C_IOTA + 144
RW = 2 * SEQ


def t5_bucket(rel):
    half = REL_BUCKETS // 2
    exact = half // 2
    n = np.abs(rel)
    large = exact + (np.log(np.maximum(n, 1) / exact) / np.log(REL_MAX / exact) * (half - exact)).astype(np.int32)
    large = np.minimum(large, half - 1)
    return np.where(rel > 0, half, 0) + np.where(n < exact, n, large)


def constants():
    c = np.zeros((P, CW), np.float32)
    i = np.arange(P)
    c[:, C_ID:C_ID + P] = np.eye(P)
    c[:, C_LE:C_LE + P] = i[:, None] <= i[None, :]
    c[:, C_GE:C_GE + P] = i[:, None] >= i[None, :]
    c[:, C_ONE:C_ONE + P] = 1.0
    c[:, C_MF:C_MF + P] = np.where(i[None, :] >= i[:, None], 0.0, NEG)
    c[:, C_MB + P:C_MB + 2 * P] = np.where(i[None, :] <= i[:, None], 0.0, NEG)
    c[:, C_I16:C_I16 + 16] = np.arange(16)
    c[:, C_IOTA:C_IOTA + 144] = np.arange(144)
    return c


def bias_constants():
    d = np.arange(RW) - (SEQ - 1)
    hot = (t5_bucket(d)[None, :] == np.arange(REL_BUCKETS)[:, None]).astype(np.float32)
    mask = np.full((NG * 8, RW), NEG, np.float32)
    for g, (win, dil) in enumerate(WINDOWS):
        ok = (d % dil == 0) & (np.abs(d // dil) <= (win // 2) // dil)
        mask[g * 8:(g + 1) * 8, ok] = 0.0
    out = np.zeros((56, RW), np.float32)
    out[0:32] = hot
    out[32:56] = mask
    return out


class Count:

    def __init__(self, sem, per_layer, before=0):
        self.sem, self.per_layer, self.before = sem, per_layer, before

    def at(self, layer, n):
        return layer * self.per_layer + (n + self.before)


def spread(ap, axis, n):
    s = ap.unsqueeze(axis)
    shape = list(s.shape)
    shape[axis] = n
    return s.broadcast_to(shape)


def build(nc, x_prompt, x_sample, consts, biases, rel, par, w_ssd, w_att, w_mrg, w_out, w_qry, w_u, w_v,
          w_final, y_prompt, y_sample):
    with ExitStack() as ctx:
        at_byte = {}

        def sb(name, shape, dt=F32):
            t = ctx.enter_context(nc.sbuf_tensor(name, shape, dt))
            at_byte[name] = nc.sbuf_base - int(np.prod(shape[1:])) * (2 if dt is BF16 else 4)
            return t

        def part(name, ap):
            shape = list(ap.shape)
            return nc.alloc_sbuf_tensor_at(name, shape, F32R, offset=at_byte[ap.tensor.name] + 4 * ap.offset)

        def sem(name):
            return ctx.enter_context(nc.semaphore(name))

        def count(name, per_layer, before=0):
            return Count(sem(name), per_layer, before)

        a_dram = nc.dram_tensor("a_rows", [2, SSD_HEADS, T], F32).ap()
        r_dram = nc.dram_tensor("bias_rows", [NG * 8, RW], F32).ap()
        bias_dram = nc.dram_tensor("bias_tiles", [4, 2, P, 6, SEQ], F32).ap()

        bank = [ctx.enter_context(nc.psum_tensor(f"bank{i}", [P, 512], F32)) for i in range(4)]
        routes = ctx.enter_context(nc.psum_tensor("banks4to7", [P, 4, 512], F32))

        def pb(i):
            return bank[i][:, :] if i < 4 else routes[:, i - 4, :]

        x = sb("x", [P, NT, D])
        hT = sb("hT", [P, KD, T])
        ring = [sb(f"ring{j}", [P, UNIT]) for j in range(SLOTS)]
        spare = [sb(f"spare{j}", [P, UNIT]) for j in range(2)]
        pr = sb("pr", [P, PW])
        cst = sb("cst", [P, CW])
        iota_b = sb("iota_b", [P, 144, 16], BF16)
        stat = sb("stat", [P, 64])
        yT = sb("yT", [P, 16, T])
        late = sb("late", [P, 5 * T])
        rstdB = late[:, 0:T]
        oT = late[:, T:].rearrange("p (h t) -> p h t", h=4)
        ident = cst[:, C_ID:C_ID + P]
        le = cst[:, C_LE:C_LE + P]
        ge = cst[:, C_GE:C_GE + P]
        ones = cst[:, C_ONE:C_ONE + P]

        WORDS = 21300
        arena = sb("arena", [P, WORDS])
        used = [0]

        def cut(*shape, dt=F32):
            n = 1
            for s in shape:
                n *= s
            words = n if dt in (F32, U32) else (n + 1) // 2
            o = used[0]
            used[0] += words
            assert used[0] <= WORDS, used[0]
            v = arena[:, o:o + words]
            if dt is not F32:
                v = v.bitcast(dt)
            if len(shape) > 1:
                names = " ".join(f"d{i}" for i in range(len(shape)))
                v = v.rearrange(f"p ({names}) -> p {names}", **{f"d{i}": s for i, s in enumerate(shape)})
            return v

        rel_w, hot_rel, mask_rel = cut(NG * 8), cut(RW), cut(RW)
        used[0] = 0
        hTh = cut(KD, T)
        after_h = used[0]
        xn = [cut(D), cut(D)]
        junk = cut(D)
        decays = used[0]
        used[0] = after_h
        xtok = cut(NT, 2 * P)
        xdt = [cut(NT, 2 * P) for _ in range(2)]
        used[0] = decays
        dtv = cut(NT, 64)
        negA = cut(NT, 64)
        keep = used[0]
        dr0, dax, du, dw, dln, dd, dz, da = (cut(NT, 64) for _ in range(8))
        aexp = cut(64)
        aT = cut(2, T)
        used[0] = keep
        aBC = cut(2, RH, T)
        E = cut(8, 768)
        cx = [cut(T) for _ in range(4)]
        zs = [oT[:, i, :] for i in range(2)]
        y3 = [oT[:, 2 + i, :] for i in range(2)]
        sq = [cut(T) for _ in range(2)]
        gneg = cut(NT, 2, RH)
        gdt = cut(NT, 2, RH)
        gp = cut(32)
        sqsum = rstdB
        used[0] = after_h
        qk = [cut(T) for _ in range(6)]
        vtok = [cut(NT, P) for _ in range(3)]
        BM = cut(2, 6, SEQ)
        Pm = cut(8, NG, SEQ)
        mx, nm, den, wg, fw = (cut(8, NG) for _ in range(5))
        m1, s1, r1 = (cut(8) for _ in range(3))
        top = used[0]
        PTt = [cut(NG * 2 * SEQ) for _ in range(2)]
        used[0] = top
        vraw = [cut(T) for _ in range(3)]
        used[0] = after_h
        mT = cut(8, T)
        sg = [cut(T) for _ in range(4)]
        t1 = cut(T)
        t2 = cut(T)
        yh = cut(16, T)
        used[0] -= 16 * T
        mTh = cut(8, T)
        used[0] = after_h
        qT = [cut(T) for _ in range(4)]
        sc = [cut(2, NT, P) for _ in range(2)]
        sc2 = cut(2, NT, P)
        v16 = cut(2, NT, TOPK)
        x16 = cut(2, NT, TOPK, dt=U32)
        f16 = cut(2, NT, TOPK)
        cand = cut(NT, 256)
        cand2 = cut(NT, 256)
        cvh = cut(NT, TOPK)
        ci = cut(NT * TOPK, dt=U32)
        pij = cut(2, NT * TOPK, dt=U32)
        pf = cut(2, NT * TOPK)
        hot = cut(NT, TOPK, 16)
        idh = cut(2, NT * TOPK)
        CV = cut(NT, PH, TOPK)
        ID = [cut(NT, PH, TOPK) for _ in range(2)]
        Ge = cut(NT, PH, TOPK)
        gsum = cut(32)
        grec = cut(32)
        gr = [cut(T) for _ in range(2)]
        assert used[0] <= 28 * T + 2 * D
        used[0] = KD * T
        Gs = [yT, cut(16, T)]
        gh = [cut(T) for _ in range(4)]
        ghh = [cut(T) for _ in range(4)]
        hi_u = [spare[0][:, :], spare[1][:, :]]
        hi_v = [late[:, 0:UNIT], late[:, UNIT:2 * UNIT], pr[:, 0:UNIT], cut(UNIT)]
        hi_u = [part(f"hi_u{n}", a) for n, a in enumerate(hi_u)]
        hi_v = [part(f"hi_v{n}", a) for n, a in enumerate(hi_v)]
        lo = [part(f"lo{n}", ring[n][:, :]) for n in range(7)]
        y_hi, y_lo = part("y_hi", yh), part("y_lo", yT[:, :, :])
        m_hi, m_lo = part("m_hi", mTh), part("m_lo", mT)
        hT_hi, hT_lo = part("hT_hi", hTh), part("hT_lo", hT[:, :, :])
        gh_h = [part(f"gh_hi{n}", a) for n, a in enumerate(ghh)]
        gh_l = [part(f"gh_lo{n}", a) for n, a in enumerate(gh)]
        idT = [late[:, 2 * UNIT + q * (T // 2):2 * UNIT + (q + 1) * (T // 2)].bitcast(BF16) for q in range(2)]
        gP = cut(3, T, dt=BF16)
        Bh = [cut(P, 16, dt=BF16) for _ in range(2)]
        eq = [cut(16, 16, dt=BF16) for _ in range(2)]
        A3 = [cut(3, 16, 16, dt=BF16) for _ in range(2)]
        used[0] = 0
        fin = [cut(D) for _ in range(2)]
        fjunk = cut(D)
        wfin = cut(D)

        w_in = [sem(f"w_in{j}") for j in range(SLOTS)]
        slot_free = Count(sem("slot_free"), UNITS, CREDIT)
        cst_in, x_in, rel_in, row_out, bias_out = (sem(n) for n in ("cst_in", "x_in", "rel_in", "row_out", "bias_out"))
        iota_ok, rel_mm, row_ok = sem("iota_ok"), sem("rel_mm"), sem("row_ok")
        par_in = count("par_in", 16)
        n_ss, n_ms, n_sqrt, n_rs, n_xn, n_tr, hT_ok = (count(n, k) for n, k in (
            ("n_ss", 8), ("n_ms", 2), ("n_sqrt", 2), ("n_rs", 2), ("n_xn", 8), ("n_tr", 16), ("hT_ok", 16)))
        dt_mm, dt_ax, dt_u, dt_w, dt_ln, dt_a, dt_cs, dt_T = (count(n, k) for n, k in (
            ("dt_mm", 1), ("dt_ax", 1), ("dt_u", 2), ("dt_w", 1), ("dt_ln", 1), ("dt_a", 1), ("dt_cs", 1), ("dt_T", 3)))
        dt_v = count("dt_v", 9)
        aT_out = count("aT_out", 16)
        bc_in = count("bc_in", 16 * GROUPS)
        g_cp = count("g_cp", 3 * GROUPS)
        arg, ex = count("arg", 8 * GROUPS), count("ex", 8 * GROUPS)
        c_mm, c_acc, c_tap, c_ok, c_s = (count(n, k * GROUPS) for n, k in (
            ("c_mm", 4), ("c_acc", 4), ("c_tap", 12), ("c_ok", 4), ("c_s", 4)))
        z_mm, z_s = count("z_mm", 2 * GROUPS), count("z_s", 2 * GROUPS, 2)
        xt_mm, xt_ok, xd_ok = (count(n, 2 * GROUPS) for n in ("xt_mm", "xt_ok", "xd_ok"))
        cb_mm, m_ok = count("cb_mm", 2 * GROUPS), count("m_ok", 8 * GROUPS)
        y_mm, y_v, y3_ok, sq_ok, y_ok = (count(n, 2 * GROUPS, b) for n, b in (
            ("y_mm", 0), ("y_v", 2), ("y3_ok", 0), ("sq_ok", 0), ("y_ok", 2)))
        sq_sum = count("sq_sum", 1 + 2 * GROUPS, 2)
        r_mm, r_ms, r_sq, r_ok = (count(n, 1) for n in ("r_mm", "r_ms", "r_sq", "r_ok"))
        bm_in = count("bm_in", 16 * 4)
        p_mm, p_evA, p_evV = count("p_mm", 36), count("p_evA", 20), count("p_evV", 16)
        vt_mm, vt_ok = count("vt_mm", 12), count("vt_ok", 12)
        s_mm, s_v, s_nm, p_x = (count(n, 32) for n in ("s_mm", "s_v", "s_nm", "p_x"))
        a_v, a_w = count("a_v", 4 * 6), count("a_w", 4)
        p_f = count("p_f", 32)
        t_mm, t_evA, t_evV = count("t_mm", 48), count("t_evA", 24), count("t_evV", 24)
        o_mm, o_ok = count("o_mm", 16), count("o_ok", 4, 1)
        ga_mm, gb_mm, pa_mm, pb_mm = (count(n, 8) for n in ("ga_mm", "gb_mm", "pa_mm", "pb_mm"))
        sg_ok = count("sg_ok", 16)
        m_v, mT_ok = count("m_v", 24), count("mT_ok", 8, 2)
        out_mm, x_mid = count("out_mm", 8), count("x_mid", 8)
        q_mm, q_ev, q_s, q_sv = (count(n, 16) for n in ("q_mm", "q_ev", "q_s", "q_sv"))
        TK = 16
        k_v, k_done = count("k_v", TK * PH), count("k_done", PH, 2)
        g_v, g_e, g_ok, gt_mm, gt_ok = (count(n, k) for n, k in (
            ("g_v", 3), ("g_e", 1), ("g_ok", 1), ("gt_mm", 3), ("gt_ok", 7)))
        g_fence = count("g_fence", 1)
        CH = (STRIPES + 1) * BLOCKS * 8
        h_eq, h_ok, h_mm, G_ok = (count(n, CH) for n in ("h_eq", "h_ok", "h_mm", "G_ok"))
        u_mm, u_ge, gh_m, gh_hi, gh_ok = (count(n, EXPERT_TILES, b) for n, b in (
            ("u_mm", 0), ("u_ge", 2), ("gh_m", 0), ("gh_hi", 0), ("gh_ok", 0)))
        w_hi, w_lo = count("w_hi", SPLITS), count("w_lo", SPLITS)
        hh_ok, hl_ok = count("hh_ok", 16), count("hl_ok", 16)
        yh_ok, yl_ok, mh_ok, ml_ok = (count(n, k) for n, k in (("yh_ok", 16), ("yl_ok", 16), ("mh_ok", 8), ("ml_ok", 8)))
        v_mm, v_add = count("v_mm", 256), count("v_add", 256, 2)
        f_w, f_ss, f_v, f_sq, f_x, f_ok, f_out = (sem(n) for n in ("f_w", "f_ss", "f_v", "f_sq", "f_x", "f_ok", "f_out"))

        block = ctx.enter_context(nc.Block())

        def wait_alone(e, c, layer, n):
            value = c.at(layer, n)
            e.compute_val(value)
            e.wait_ge(cst_in, 16)
            e.wait_ge(c.sem, value)

        def h_piece(h, n):
            return h[:, 4 * (n % 2):4 * (n % 2) + 4, (n // 2) * P:(n // 2 + 1) * P]

        def loaded(e, l, name, i, j):
            slots = PHASES[NAMES.index(name)][2]
            s = slots[j]
            first, each = LOADS[name][s], slots.count(s)
            e.wait_ge(w_in[s], (l * SLOT_LOADS[s] + i * each + (first + slots[:j].count(s) + 1)) * 16)

        def split_no(name, i, j):
            slots = PHASES[NAMES.index(name)][2]
            if name == "peer":
                j = SPLIT_PEER.index(j)
            return i * (4 if name == "mrg" else len(slots)) + (SPLIT[name] + j)

        def places(name, j):
            slot = PHASES[NAMES.index(name)][2][j]
            return slot, hi_v[j - 4] if name == "peer" and j >= 4 else hi_u[j % 2]

        @block.sync
        def _(sp):
            sp.dma_start(cst[:, :], consts).then_inc(cst_in, 16)
            sp.dma_start(x[:, 0:2, :], x_prompt.rearrange("b (t p) d -> p (b t) d", p=P)).then_inc(x_in, 16)
            sp.dma_start(x[:, 2:4, :], x_sample.rearrange("b (t p) d -> p (b t) d", p=P)).then_inc(x_in, 16)

            def load(src, j, free_at):
                sp.compute_val(src.offset)
                if free_at is not None:
                    sp.compute_val(free_at)
                    sp.wait_ge(cst_in, 16)
                    sp.wait_ge(slot_free.sem, free_at)
                sp.dma_start(ring[j][:, :], src).then_inc(w_in[j], 16)

            def phase(l, name, unit, order=None):
                _, iters, slots = PHASES[NAMES.index(name)]
                n = len(slots)
                order = order or range(n)
                for j in order:
                    u = last_user(name, j)
                    load(unit(0, j), slots[j], slot_free.at(l, u + 1) if u >= -CREDIT else None)
                if iters > 1:
                    with sp.Fori(1, iters) as i:
                        for j in order:
                            earlier = [jj for jj in range(j) if slots[jj] == slots[j]]
                            if earlier:
                                u = i * n + (BASE[name] + earlier[-1])
                            else:
                                last = max(jj for jj in range(n) if slots[jj] == slots[j])
                                u = (i - 1) * n + (BASE[name] + last)
                            load(unit(i, j), slots[j], slot_free.at(l, u + 1))

            with sp.Fori(0, DEPTH) as l:
                phase(l, "ssd", lambda i, j: w_ssd[l, i, j])
                phase(l, "att", lambda i, j: w_att[l, i, j])
                phase(l, "mrg", lambda i, j: w_mrg[l, i, j])
                phase(l, "out", lambda i, j: w_out[l, j])
                phase(l, "qry", lambda i, j: w_qry[l, i, j])
                phase(l, "peer", lambda i, j: w_u[l, i, j] if j < 4 else w_v[l, i, j - 4], LOAD_PEER)
            yp = y_prompt.rearrange("b (t p) d -> p (b t) d", p=P)
            ys = y_sample.rearrange("b (t p) d -> p (b t) d", p=P)
            for tt in range(NT):
                sp.wait_ge(f_ok, tt + 1)
                dst = yp[:, tt, :] if tt < 2 else ys[:, tt - 2, :]
                sp.dma_start(dst, fin[tt % 2]).then_inc(f_out, 16)
                sp.wait_ge(f_out, 16 * (tt + 1))

        @block.gpsimd
        def _(pool):
            pool.wait_ge(row_ok, 1)
            pool.dma_start(r_dram, oT[0:NG * 8, 0, :]).then_inc(row_out, 16)
            pool.wait_ge(row_out, 16)
            for hp in range(4):
                for qt in range(2):
                    for j in range(2):
                        src = bass.AP(tensor=r_dram.tensor, offset=(2 * hp + j) * RW + (SEQ - 1) - qt * P,
                                      ap=[[8 * RW, NG], [-1, P], [1, SEQ]])
                        dst = bias_dram[hp, qt, :, 3 * j:3 * j + 3, :].rearrange("q g k -> g q k")
                        pool.dma_start(dst, src).then_inc(bias_out, 16)
                        pool.wait_ge(bias_out, 16 * (4 * hp + 2 * qt + j + 1))
            pool.dma_start(pr[:, :], par[0]).then_inc(par_in.sem, 16)
            with pool.Fori(0, DEPTH) as l:
                wait_alone(pool, dt_T, l, 3)
                pool.dma_start(a_dram.rearrange("d h t -> h d t"), aT[0:SSD_HEADS]).then_inc(aT_out.sem, 16)
                nc.gpsimd.memset(sqsum, 0.0).then_inc(sq_sum.sem, 1)

                def spread_rows(g):
                    return (aBC, spread(a_dram[:, bass.ds(g * RH, RH), :].rearrange("d h t -> d (h t)"), 0, P))

                def low(name, i, j):
                    slot, hi = places(name, j)
                    pool.wait_ge(w_hi.sem, w_hi.at(l, split_no(name, i, j) + 1))
                    nc.gpsimd.tensor_tensor(lo[slot][:, :], ring[slot][:, :], hi[:, :], ALU.subtract).then_inc(w_lo.sem, 1)

                dst, src = spread_rows(0)
                wait_alone(pool, aT_out, l, 16)
                pool.dma_start(dst.rearrange("p d h t -> p d (h t)"), src).then_inc(bc_in.sem, 16)

                def add_squares(g):
                    for i in range(2):
                        pool.wait_ge(sq_ok.sem, sq_ok.at(l, g * 2 + (i + 1)))
                        pool.wait_ge(sq_sum.sem, sq_sum.at(l, g * 2 + (i + 1)))
                        nc.gpsimd.tensor_tensor(sqsum, sqsum, sq[i], ALU.add).then_inc(sq_sum.sem, 1)

                low("ssd", 0, 0)
                low("ssd", 0, 1)

                def group(g, more):
                    for j in range(2, 6):
                        low("ssd", g, j)
                    if more:
                        dst, src = spread_rows(g + 1)
                        pool.compute_val(src.offset)
                        wait_alone(pool, arg, l, g * 8 + 8)
                        pool.dma_start(dst.rearrange("p d h t -> p d (h t)"), src).then_inc(bc_in.sem, 16)
                    low("ssd", g + 1, 0)
                    low("ssd", g + 1, 1)
                    add_squares(g)

                with pool.Fori(0, GROUPS - 1) as g:
                    group(g, True)
                group(GROUPS - 1, False)

                def bias_tiles(hp):
                    return BM.rearrange("p q h k -> p q (h k)"), bias_dram[hp].rearrange("q p h k -> p q (h k)")

                wait_alone(pool, r_ok, l, 1)
                dst, src = bias_tiles(0)
                pool.dma_start(dst, src).then_inc(bm_in.sem, 16)

                def pair(hp, more):
                    for j in range(2, 9):
                        low("att", hp, j)
                    low("att", hp + 1, 0)
                    low("att", hp + 1, 1)
                    if more:
                        dst, src = bias_tiles(hp + 1)
                        pool.compute_val(src.offset)
                        wait_alone(pool, s_v, l, hp * 8 + 8)
                        pool.dma_start(dst, src).then_inc(bm_in.sem, 16)

                with pool.Fori(0, 3) as hp:
                    pair(hp, True)
                pair(3, False)
                with pool.Fori(0, 8) as c:
                    low("mrg", c, 2)
                    low("mrg", c, 3)
                    low("mrg", c + 1, 0)
                    low("mrg", c + 1, 1)
                for j in range(2, 8):
                    low("out", 0, j)
                with pool.Fori(0, PH // 2) as h2:
                    for n in range(4):
                        low("qry", h2, n)
                with pool.Fori(0, STRIPES * BLOCKS) as blk:
                    for n in SPLIT_PEER:
                        low("peer", blk, n)
                src = par[l + 1]
                pool.compute_val(src.offset)
                wait_alone(pool, v_mm, l, 256)
                pool.dma_start(pr[:, :], src).then_inc(par_in.sem, 16)
            pool.wait_ge(par_in.sem, 16 * (DEPTH + 1))
            pool.wait_ge(v_add.sem, v_add.at(DEPTH, 0))
            pool.dma_start(wfin, w_final.partition_broadcast(P)).then_inc(f_w, 16)
            pool.wait_ge(f_w, 16)

        @block.tensor
        def _(pe):
            pe.sem_inc(slot_free.sem, CREDIT - 1)
            pe.wait_ge(cst_in, 16)
            pe.wait_ge(rel_in, 48)
            pe.matmul(pb(0)[0:NG * 8, :], rel_w[0:REL_BUCKETS], hot_rel[0:REL_BUCKETS], start=True, stop=True).then_inc(rel_mm, 1)

            def project(l, name, i, j, out, rhs, n=KD):
                loaded(pe, l, name, i, j)
                for k in range(n):
                    mm = pe.matmul(out, ring[j][:, k * P:(k + 1) * P], rhs[:, k, :], start=k == 0, stop=k == n - 1)
                    if k == 0:
                        mm.then_inc(slot_free.sem, 1)
                return mm

            def product3(out, a, b, start, stop):
                return [pe.matmul(out, a[p], b[q], start=start and n == 0, stop=stop and n == 2)
                        for n, (p, q) in enumerate(((0, 0), (0, 1), (1, 0)))]

            def project3(l, name, i, j, out, high=hT_hi, low=hT_lo, start=True, stop=True, k0=0):
                slot, hi = places(name, j)
                pe.wait_ge(w_lo.sem, w_lo.at(l, split_no(name, i, j) + 1))
                for k in range(KD):
                    cols = slice(k * P, (k + 1) * P)
                    mm = product3(out, (hi[:, cols], lo[slot][:, cols]), (high[:, k0 + k, :], low[:, k0 + k, :]),
                                  start and k == 0, stop and k == KD - 1)
                    if k == 0:
                        mm[0].then_inc(slot_free.sem, 1)
                return mm[-1]

            def norm(l, w):
                for tt in range(NT):
                    pe.wait_ge(n_xn.sem, n_xn.at(l, 4 * w + tt + 1))
                    if tt >= 2:
                        pe.wait_ge(hT_ok.sem, hT_ok.at(l, 8 * w + 2 * (tt - 1)))
                    for half in range(2):
                        out = pb(2 * (tt % 2) + half)
                        for k in range(4):
                            kk = 4 * half + k
                            mm = pe.transpose(out[:, k * P:(k + 1) * P], xn[tt % 2][:, kk * P:(kk + 1) * P], ident)
                        mm.then_inc(n_tr.sem, 1)

            with pe.Fori(0, DEPTH) as l:
                norm(l, 0)
                pe.wait_ge(hT_ok.sem, hT_ok.at(l, 8))
                pe.wait_ge(par_in.sem, par_in.at(l, 16))
                for tt in range(NT):
                    for k in range(KD):
                        mm = pe.matmul(pb(4)[:, tt * 64:(tt + 1) * 64], hT[:, k, tt * P:(tt + 1) * P],
                                       pr[:, PW_WDT + 64 * k:PW_WDT + 64 * (k + 1)], start=(k == 0), stop=(k == KD - 1))
                mm.then_inc(dt_mm.sem, 1)
                pe.wait_ge(dt_a.sem, dt_a.at(l, 1))
                for s in range(NSEQ):
                    for d, tri in ((0, le), (1, ge)):
                        first, second = (2 * s, 2 * s + 1) if d == 0 else (2 * s + 1, 2 * s)
                        cols = slice(32 * d, 32 * d + 32)
                        for tt, parts in ((first, [(tri, first)]), (second, [(ones, first), (tri, second)])):
                            for n, (m, src) in enumerate(parts):
                                pe.matmul(pb(5)[:, tt * 64 + 32 * d:tt * 64 + 32 * d + 32], m, da[:, src, cols],
                                          start=(n == 0), stop=(n == len(parts) - 1))
                            for n, (m, src) in enumerate(parts):
                                mm = pe.matmul(pb(6 + d)[0:32, tt * P:(tt + 1) * P], da[:, src, cols], m,
                                               start=(n == 0), stop=(n == len(parts) - 1))
                mm.then_inc(dt_cs.sem, 1)
                wait_alone(pe, dt_T, l, 3)

                wait_alone(pe, hl_ok, l, 8)
                with pe.Fori(0, GROUPS) as g:
                    for j in range(4):
                        if j == 2:
                            pe.wait_ge(y_v.sem, y_v.at(l, g * 2))
                        project3(l, "ssd", g, j, pb(j)).then_inc(c_mm.sem, 1)
                    for i in range(2):
                        pe.wait_ge(z_s.sem, z_s.at(l, g * 2 + i - 1))
                        project3(l, "ssd", g, 4 + i, pb(4 + i)).then_inc(z_mm.sem, 1)
                    for s in range(NSEQ):
                        pe.wait_ge(c_s.sem, c_s.at(l, g * 4 + 2))
                        for si in range(2):
                            mm = pe.matmul(pb(s)[:, si * SEQ:(si + 1) * SEQ],
                                           cx[0][:, s * SEQ + si * P:s * SEQ + (si + 1) * P],
                                           cx[1][:, s * SEQ:(s + 1) * SEQ], start=True, stop=True)
                        mm.then_inc(cb_mm.sem, 1)
                    for i in range(2):
                        pe.wait_ge(c_s.sem, c_s.at(l, g * 4 + (3 + i)))
                        for tt in range(NT):
                            mm = pe.transpose(pb(6 + i)[:, tt * P:(tt + 1) * P],
                                              cx[2 + i][:, tt * P:(tt + 1) * P], ident)
                        mm.then_inc(xt_mm.sem, 1)
                    pe.wait_ge(xd_ok.sem, xd_ok.at(l, g * 2 + 2))
                    for n in range(8):
                        r, s = 2 * (n // 4) + (n % 4) // 2, n % 2
                        pe.wait_ge(m_ok.sem, m_ok.at(l, g * 8 + (n + 1)))
                        out = pb(2 + r // 2)[64 * (r % 2):64 * (r % 2) + 64, :]
                        o = s * SEQ
                        xs = slice(r * HD, (r + 1) * HD)
                        parts = [(0, 0, 0, 256, 0), (1, 1, 256, 256, 0), (1, 0, 512, 128, 0), (0, 1, 640, 128, 128)]
                        for q, (d, si, c0, w, l0) in enumerate(parts):
                            mm = pe.matmul(out[:, o + l0:o + l0 + w], xdt[d][:, 2 * s + si, xs],
                                           E[:, n, c0:c0 + w], start=(q == 0), stop=(q == 3))
                        if n % 4 == 3:
                            mm.then_inc(y_mm.sem, 1)
                pe.wait_ge(sq_sum.sem, sq_sum.at(l, 1 + 2 * GROUPS))
                pe.wait_ge(z_s.sem, z_s.at(l, 2 * GROUPS))
                pe.matmul(pb(4), ones, sqsum, start=True, stop=True).then_inc(r_mm.sem, 1)
                wait_alone(pe, y_v, l, 2 * GROUPS)
                wait_alone(pe, r_ok, l, 1)

                with pe.Fori(0, 4) as hp:
                    pe.wait_ge(o_ok.sem, o_ok.at(l, hp))
                    for u in range(9):
                        if u >= 4:
                            if u % 2 == 0:
                                pe.wait_ge(p_evA.sem, p_evA.at(l, hp * 5 + (u - 4) // 2 + 1))
                            else:
                                pe.wait_ge(p_evV.sem, p_evV.at(l, hp * 4 + (u - 4) // 2 + 1))
                        project3(l, "att", hp, u, pb(u % 4)).then_inc(p_mm.sem, 1)
                    pe.wait_ge(p_evA.sem, p_evA.at(l, hp * 5 + 5))
                    pe.wait_ge(p_evV.sem, p_evV.at(l, hp * 4 + 4))
                    for g in range(NG):
                        for tt in range(NT):
                            mm = pe.transpose(pb(4 + g)[:, tt * P:(tt + 1) * P], vraw[g][:, tt * P:(tt + 1) * P], ident)
                        mm.then_inc(vt_mm.sem, 1)
                    for c in range(8):
                        j, s, qt = c // 4, (c // 2) % 2, c % 2
                        if c >= 2:
                            pe.wait_ge(s_v.sem, s_v.at(l, hp * 8 + (c - 1)))
                        hd = slice(64 * j, 64 * j + 64)
                        for g in range(NG):
                            mm = pe.matmul(pb(2 * (c % 2) + g // 2)[:, (g % 2) * SEQ:(g % 2 + 1) * SEQ],
                                           qk[2 * g][hd, s * SEQ + qt * P:s * SEQ + (qt + 1) * P],
                                           qk[2 * g + 1][hd, s * SEQ:(s + 1) * SEQ], start=True, stop=True)
                        mm.then_inc(s_mm.sem, 1)
                    pe.wait_ge(vt_ok.sem, vt_ok.at(l, hp * 3 + 3))

                    def values(js):
                        j, s = js // 2, js % 2
                        pe.wait_ge(t_evA.sem, t_evA.at(l, hp * 6 + (3 * js + 4) // 2))
                        pe.wait_ge(t_evV.sem, t_evV.at(l, hp * 6 + (3 * js + 3) // 2))
                        for q in range(6):
                            g, kt = q // 2, q % 2
                            mm = pe.matmul(pb(0)[64 * j:64 * j + 64, s * SEQ:(s + 1) * SEQ],
                                           vtok[g][:, 2 * s + kt, 64 * j:64 * j + 64],
                                           PTt[js % 2][:, q * SEQ:(q + 1) * SEQ], start=(q == 0), stop=(q == 5))
                        mm.then_inc(o_mm.sem, 1)

                    for n in range(12):
                        js, m = n // 3, n % 3
                        if m == 0:
                            pe.wait_ge(p_f.sem, p_f.at(l, hp * 8 + (2 * js + 2)))
                        if n >= 4:
                            if n % 2 == 0:
                                pe.wait_ge(t_evA.sem, t_evA.at(l, hp * 6 + (n - 4) // 2 + 1))
                            else:
                                pe.wait_ge(t_evV.sem, t_evV.at(l, hp * 6 + (n - 4) // 2 + 1))
                        for q in range(4):
                            gk, qt = 2 * m + q // 2, q % 2
                            g, kt = gk // 2, gk % 2
                            mm = pe.transpose(pb(4 + n % 4)[:, q * P:(q + 1) * P],
                                              Pm[:, 2 * js + qt, g, kt * P:(kt + 1) * P], ident)
                        mm.then_inc(t_mm.sem, 1)
                        if m == 1 and js:
                            values(js - 1)
                    values(3)

                pe.wait_ge(y_ok.sem, y_ok.at(l, 2 * GROUPS))
                wait_alone(pe, o_ok, l, 4)
                with pe.Fori(0, 4) as c2:
                    for h in range(2):
                        c, b = c2 * 2 + h, 4 * h
                        pe.wait_ge(mT_ok.sem, mT_ok.at(l, c - 1))
                        project3(l, "mrg", c, 0, pb(b)).then_inc(ga_mm.sem, 1)
                        project3(l, "mrg", c, 1, pb(b + 1)).then_inc(gb_mm.sem, 1)
                        pe.wait_ge(yl_ok.sem, yl_ok.at(l, 8))
                        project3(l, "mrg", c, 2, pb(b + 2), y_hi, y_lo, stop=False)
                        pe.wait_ge(yl_ok.sem, yl_ok.at(l, 16))
                        project3(l, "mrg", c, 3, pb(b + 2), y_hi, y_lo, start=False, k0=8).then_inc(pa_mm.sem, 1)
                        project(l, "mrg", c, 4, pb(b + 3), oT, n=4).then_inc(pb_mm.sem, 1)

                for k in range(KD):
                    pe.wait_ge(ml_ok.sem, ml_ok.at(l, k + 1))
                    pe.wait_ge(w_lo.sem, w_lo.at(l, split_no("out", 0, k) + 1))
                    slot, hi = places("out", k)
                    for n in range(8):
                        tok, cols = slice(n // 2 * P, (n // 2 + 1) * P), slice(n % 2 * 512, (n % 2 + 1) * 512)
                        mm = product3(pb(n), (m_hi[:, k, tok], m_lo[:, k, tok]), (hi[:, cols], lo[slot][:, cols]),
                                      k == 0, k == KD - 1)
                        if n == 0:
                            mm[0].then_inc(slot_free.sem, 1)
                        if k == KD - 1:
                            mm[-1].then_inc(out_mm.sem, 1)
                pe.wait_ge(x_mid.sem, x_mid.at(l, 8))

                norm(l, 1)
                wait_alone(pe, hl_ok, l, 16)
                with pe.Fori(0, PH // 2) as h2:
                    for hh in range(2):
                        h = h2 * 2 + hh
                        for s in range(2):
                            project3(l, "qry", h2, 2 * hh + s, pb(2 * hh + s)).then_inc(q_mm.sem, 1)
                        for s in range(2):
                            pe.wait_ge(q_ev.sem, q_ev.at(l, h * 2 + (s + 1)))
                            for tt in range(NT):
                                mm = pe.matmul(pb(4 + 2 * hh + s)[:, tt * P:(tt + 1) * P],
                                               qT[2 * hh + s][:, tt * P:(tt + 1) * P],
                                               pr[:, PW_KEYS + s * P:PW_KEYS + (s + 1) * P], start=True, stop=True)
                            mm.then_inc(q_s.sem, 1)
                    pe.wait_ge(q_sv.sem, q_sv.at(l, h2 * 4 + 4))
                pe.wait_ge(g_ok.sem, g_ok.at(l, 1))
                for n, src in enumerate((ID[0], ID[1], Ge)):
                    for tt in range(NT):
                        mm = pe.transpose(pb(n)[:, tt * P:(tt + 1) * P], src[:, tt].rearrange("p h k -> p (h k)"), ident)
                    mm.then_inc(gt_mm.sem, 1)
                wait_alone(pe, gt_ok, l, 7)

                def outer(l, base, c):
                    pe.wait_ge(h_ok.sem, h_ok.at(l, base + (c + 1)))
                    for t in range(16):
                        mm = pe.matmul(routes[:, 2 * (c % 2) + t // 8, 64 * (t % 8):64 * (t % 8) + 48],
                                       Bh[c % 2][:, :, t], A3[c % 2][:, :, :, t], start=True, stop=True)
                    mm.then_inc(h_mm.sem, 1)

                with pe.Fori(0, BLOCKS) as b:
                    for c in range(8):
                        outer(l, b * 8, c)
                with pe.Fori(0, STRIPES // 2) as sp2:
                    for par2 in range(2):
                        with pe.Fori(0, BLOCKS) as b:
                            blk = sp2 * (2 * BLOCKS) + par2 * BLOCKS + b
                            base = blk * 8 + BLOCKS * 8
                            for j in range(4):
                                pe.wait_ge(u_ge.sem, u_ge.at(l, blk * 4 + j - 1))
                                project3(l, "peer", blk, j, pb(j % 2)).then_inc(u_mm.sem, 1)
                                outer(l, base, j)

                            def values(n, j):
                                tt, nh = n // 2, n % 2
                                tok, cols = slice(tt * P, (tt + 1) * P), slice(nh * 512, (nh + 1) * 512)
                                return product3(pb(2 + n % 2), (gh_h[j][:, tok], gh_l[j][:, tok]),
                                                (hi_v[j][:, cols], lo[3 + j][:, cols]), j == 0, j == 3)

                            for n in range(2):
                                pe.wait_ge(v_add.sem, v_add.at(l, blk * 8 + n - 1))
                                for j in range(3):
                                    if n == 0:
                                        pe.wait_ge(w_lo.sem, w_lo.at(l, split_no("peer", blk, 4 + j) + 1))
                                        pe.wait_ge(gh_ok.sem, gh_ok.at(l, blk * 4 + (j + 1)))
                                    mm = values(n, j)
                                    if n == 0 and j == 0:
                                        mm[0].then_inc(slot_free.sem, 1)
                            pe.wait_ge(w_lo.sem, w_lo.at(l, split_no("peer", blk, 7) + 1))
                            pe.wait_ge(gh_ok.sem, gh_ok.at(l, blk * 4 + 4))
                            for n in range(8):
                                if n < 2:
                                    mm = values(n, 3)
                                else:
                                    pe.wait_ge(v_add.sem, v_add.at(l, blk * 8 + n - 1))
                                    for j in range(4):
                                        mm = values(n, j)
                                        if n == 7 and j < 3:
                                            mm[-1].then_inc(slot_free.sem, 1)
                                mm[-1].then_inc(v_mm.sem, 1)
                                if n % 2:
                                    outer(l, base, 4 + n // 2)

        @block.scalar
        def _(act):
            act.dma_start(rel_w[0:REL_BUCKETS], rel).then_inc(rel_in, 16)
            act.dma_start(hot_rel[0:REL_BUCKETS], biases[0:32]).then_inc(rel_in, 16)
            act.dma_start(mask_rel[0:NG * 8], biases[32:56]).then_inc(rel_in, 16)
            act.wait_ge(rel_in, 48)

            def norm(l, w):
                if w == 0:
                    act.wait_ge(v_add.sem, v_add.at(l, 0))
                else:
                    act.wait_ge(x_mid.sem, x_mid.at(l, 8))
                for tt in range(NT):
                    if tt:
                        act.wait_ge(n_ss.sem, n_ss.at(l, 4 * w + tt))
                    act.activation(junk, x[:, tt, :], ACT.Square, accum_out=stat[:, tt:tt + 1]).then_inc(n_ss.sem, 1)
                act.wait_ge(n_ms.sem, n_ms.at(l, w + 1))
                act.activation(stat[:, 8:12], stat[:, 4:8], ACT.Sqrt).then_inc(n_sqrt.sem, 1)
                for n in range(8):
                    act.wait_ge(hT_ok.sem, hT_ok.at(l, 8 * w + (n + 1)))
                    act.activation(h_piece(hT_hi, n), h_piece(hT, n), ACT.Copy).then_inc(hh_ok.sem, 1)

            act.wait_ge(x_in, 32)
            with act.Fori(0, DEPTH) as l:
                def high(name, i, j):
                    slot, hi = places(name, j)
                    loaded(act, l, name, i, j)
                    act.activation(hi[:, :], ring[slot][:, :], ACT.Copy).then_inc(w_hi.sem, 1)

                norm(l, 0)
                high("ssd", 0, 0)
                high("ssd", 0, 1)
                act.wait_ge(par_in.sem, par_in.at(l, 16))
                act.activation(aexp, pr[:, PW_ALOG:PW_ALOG + 64], ACT.Exp).then_inc(dt_u.sem, 1)
                act.wait_ge(dt_ax.sem, dt_ax.at(l, 1))
                act.activation(du, dax, ACT.Exp, scale=-1.0).then_inc(dt_u.sem, 1)
                act.wait_ge(dt_w.sem, dt_w.at(l, 1))
                act.activation(dln, dw, ACT.Ln).then_inc(dt_ln.sem, 1)

                with act.Fori(0, GROUPS) as g:
                    def decay(n):
                        act.wait_ge(arg.sem, arg.at(l, g * 8 + (n + 1)))
                        act.activation(E[:, n, :], E[:, n, :], ACT.Exp).then_inc(ex.sem, 1)

                    def centre(j):
                        act.wait_ge(c_mm.sem, c_mm.at(l, g * 4 + (j + 1)))
                        act.activation(cx[j], pb(j), ACT.Identity, bias=gp[:, 8 * j + 5:8 * j + 6],
                                       scale=gp[:, 8 * j + 2:8 * j + 3]).then_inc(c_acc.sem, 1)

                    def silu(j):
                        act.wait_ge(c_ok.sem, c_ok.at(l, g * 4 + (j + 1)))
                        act.activation(cx[j], cx[j], ACT.Silu).then_inc(c_s.sem, 1)

                    def silu_z(i):
                        act.wait_ge(z_mm.sem, z_mm.at(l, g * 2 + (i + 1)))
                        act.activation(zs[i], pb(4 + i), ACT.Silu).then_inc(z_s.sem, 1)

                    act.wait_ge(g_cp.sem, g_cp.at(l, g * 3 + 3))
                    centre(0)
                    high("ssd", g, 2)
                    for n in range(4):
                        decay(n)
                    centre(1)
                    high("ssd", g, 3)
                    for n in range(4, 8):
                        decay(n)
                    silu(0)
                    centre(2)
                    high("ssd", g, 4)
                    silu(1)
                    centre(3)
                    high("ssd", g, 5)
                    silu(2)
                    silu_z(0)
                    high("ssd", g + 1, 0)
                    silu(3)
                    silu_z(1)
                    high("ssd", g + 1, 1)
                    for i in range(2):
                        act.wait_ge(xt_mm.sem, xt_mm.at(l, g * 2 + (i + 1)))
                        act.activation(xtok[:, :, i * P:(i + 1) * P], pb(6 + i).rearrange("p (t c) -> p t c", t=NT),
                                       ACT.Copy).then_inc(xt_ok.sem, 1)
                    for i in range(2):
                        act.wait_ge(y3_ok.sem, y3_ok.at(l, g * 2 + (i + 1)))
                        act.wait_ge(sq_sum.sem, sq_sum.at(l, g * 2 + i))
                        act.activation(sq[i], y3[i], ACT.Square).then_inc(sq_ok.sem, 1)
                        act.activation(yT[:, g * 2 + i, :], y3[i], ACT.Copy,
                                       scale=gp[:, 8 * (2 + i) + 7:8 * (2 + i) + 8]).then_inc(y_ok.sem, 1)
                act.wait_ge(r_ms.sem, r_ms.at(l, 1))
                act.activation(sqsum, sqsum, ACT.Sqrt).then_inc(r_sq.sem, 1)
                wait_alone(act, r_ok, l, 1)

                with act.Fori(0, 4) as hp:
                    for u in range(9):
                        act.wait_ge(p_mm.sem, p_mm.at(l, hp * 9 + (u + 1)))
                        if u % 2 == 0:
                            dst = qk[u] if u < 6 else vraw[u - 6]
                            act.activation(dst, pb(u % 4), ACT.Copy, scale=HD ** -0.5 if u < 6 else 1.0).then_inc(p_evA.sem, 1)
                        if u < 7:
                            high("att", hp, u + 2)
                    high("att", hp + 1, 0)
                    high("att", hp + 1, 1)
                    for g in range(NG):
                        act.wait_ge(vt_mm.sem, vt_mm.at(l, hp * 3 + (g + 1)))
                        act.activation(vtok[g], pb(4 + g).rearrange("p (t c) -> p t c", t=NT),
                                       ACT.Copy).then_inc(vt_ok.sem, 1)
                    for c in range(8):
                        act.wait_ge(s_nm.sem, s_nm.at(l, hp * 8 + (c + 1)))
                        for g in range(NG):
                            ins = act.activation(Pm[:, c, g, :], Pm[:, c, g, :], ACT.Exp, bias=nm[:, c, g:g + 1],
                                                 accum_out=den[:, c, g:g + 1])
                        ins.then_inc(p_x.sem, 1)
                    act.wait_ge(a_v.sem, a_v.at(l, hp * 6 + 2))
                    act.activation(wg, wg, ACT.Exp).then_inc(a_w.sem, 1)
                    for n in range(0, 12, 2):
                        act.wait_ge(t_mm.sem, t_mm.at(l, hp * 12 + (n + 1)))
                        js, m = n // 3, n % 3
                        if js >= 2:
                            act.wait_ge(o_mm.sem, o_mm.at(l, hp * 4 + js - 1))
                        act.activation(PTt[js % 2][:, m * 512:(m + 1) * 512], pb(4 + n % 4), ACT.Copy).then_inc(t_evA.sem, 1)
                    act.wait_ge(o_mm.sem, o_mm.at(l, hp * 4 + 4))
                    act.activation(oT[:, hp, :], pb(0), ACT.Copy).then_inc(o_ok.sem, 1)
                for k in range(16):
                    act.activation(y_hi[:, k, :], yT[:, k, :], ACT.Copy).then_inc(yh_ok.sem, 1)

                with act.Fori(0, 4) as c2:
                    for h in range(2):
                        c, b = c2 * 2 + h, 4 * h
                        act.wait_ge(mT_ok.sem, mT_ok.at(l, c - 1))
                        act.wait_ge(ga_mm.sem, ga_mm.at(l, c + 1))
                        act.activation(sg[2 * h], pb(b), ACT.Sigmoid).then_inc(sg_ok.sem, 1)
                        high("mrg", c, 2)
                        act.wait_ge(gb_mm.sem, gb_mm.at(l, c + 1))
                        act.activation(sg[2 * h + 1], pb(b + 1), ACT.Sigmoid).then_inc(sg_ok.sem, 1)
                        high("mrg", c, 3)
                        for j in range(2):
                            act.wait_ge(slot_free.sem, slot_free.at(l, c * 5 + (BASE["mrg"] + 3 + j)))
                            high("mrg", c + 1, j)
                act.wait_ge(mT_ok.sem, mT_ok.at(l, 8))
                for k in range(KD):
                    act.activation(m_hi[:, k, :], mT[:, k, :], ACT.Copy).then_inc(mh_ok.sem, 1)
                for j in range(2, 8):
                    act.wait_ge(slot_free.sem, slot_free.at(l, BASE["out"] + j - 1))
                    high("out", 0, j)

                norm(l, 1)
                with act.Fori(0, PH // 2) as h2:
                    def high_q(n):
                        high("qry", h2, n)

                    def query(n):
                        act.wait_ge(q_mm.sem, q_mm.at(l, h2 * 4 + (n + 1)))
                        act.activation(qT[n], pb(n), ACT.Copy).then_inc(q_ev.sem, 1)

                    def scores(hh):
                        act.wait_ge(k_done.sem, k_done.at(l, h2 * 2 + hh - 1))
                        for s in range(2):
                            act.wait_ge(q_s.sem, q_s.at(l, h2 * 4 + (2 * hh + s + 1)))
                            act.activation(sc[hh][:, s], pb(4 + 2 * hh + s).rearrange("p (t n) -> p t n", t=NT),
                                           ACT.Copy).then_inc(q_sv.sem, 1)

                    high_q(0)
                    high_q(1)
                    query(0)
                    high_q(2)
                    query(1)
                    high_q(3)
                    scores(0)
                    query(2)
                    query(3)
                    scores(1)
                act.wait_ge(g_v.sem, g_v.at(l, 1))
                act.activation(Ge, Ge, ACT.Exp).then_inc(g_e.sem, 1)
                act.wait_ge(gt_mm.sem, gt_mm.at(l, 3))

                with act.Fori(0, STRIPES * BLOCKS) as blk:
                    def high_p(n):
                        high("peer", blk, n)

                    def gelu(j):
                        act.wait_ge(u_mm.sem, u_mm.at(l, blk * 4 + (j + 1)))
                        act.activation(gh[j], pb(j % 2), ACT.Gelu).then_inc(u_ge.sem, 1)

                    def routed_high(j):
                        act.wait_ge(gh_m.sem, gh_m.at(l, blk * 4 + (j + 1)))
                        act.activation(gh_h[j][:, :], gh[j], ACT.Copy).then_inc(gh_hi.sem, 1)

                    high_p(0)
                    high_p(1)
                    gelu(0)
                    high_p(2)
                    high_p(4)
                    gelu(1)
                    high_p(3)
                    routed_high(0)
                    high_p(5)
                    gelu(2)
                    routed_high(1)
                    high_p(6)
                    high_p(7)
                    gelu(3)
                    routed_high(2)
                    routed_high(3)

            act.wait_ge(v_add.sem, v_add.at(DEPTH, 0))
            for tt in range(NT):
                if tt:
                    act.wait_ge(f_ss, tt)
                act.activation(fjunk, x[:, tt, :], ACT.Square, accum_out=stat[:, tt:tt + 1]).then_inc(f_ss, 1)
            act.wait_ge(f_v, 1)
            act.activation(stat[:, 8:12], stat[:, 4:8], ACT.Sqrt).then_inc(f_sq, 1)

        @block.vector
        def _(v):
            v.sem_inc(z_s.sem, 2)
            v.sem_inc(y_v.sem, 2)
            v.sem_inc(y_ok.sem, 2)
            v.sem_inc(sq_sum.sem, 2)
            v.sem_inc(o_ok.sem, 1)
            v.sem_inc(mT_ok.sem, 2)
            v.sem_inc(k_done.sem, 2)
            v.sem_inc(u_ge.sem, 2)
            v.wait_ge(cst_in, 16)
            v.tensor_copy(iota_b[:, :, :], spread(cst[:, C_IOTA:C_IOTA + 144], 2, 16)).then_inc(iota_ok, 1)
            v.wait_ge(rel_in, 48)
            v.wait_ge(rel_mm, 1)
            v.tensor_tensor(oT[0:NG * 8, 0, :], pb(0)[0:NG * 8, :], mask_rel[0:NG * 8], ALU.add).then_inc(row_ok, 1)
            v.wait_ge(iota_ok, 1)
            v.wait_ge(row_out, 16)
            v.wait_ge(x_in, 32)
            v.memset(stat[:, 60:61], 0.0).then_inc(v_add.sem, 2)

            def norm(l, w):
                v.wait_ge(n_ss.sem, n_ss.at(l, 4 * w + 4))
                v.tensor_scalar(stat[:, 4:8], stat[:, 0:4], 1.0 / D, EPS, ALU.mult, ALU.add).then_inc(n_ms.sem, 1)
                v.wait_ge(n_sqrt.sem, n_sqrt.at(l, w + 1))
                v.reciprocal(stat[:, 12:16], stat[:, 8:12]).then_inc(n_rs.sem, 1)
                v.wait_ge(n_rs.sem, n_rs.at(l, w + 1))
                v.wait_ge(par_in.sem, par_in.at(l, 16))

                def scale(tt):
                    if tt >= 2:
                        v.wait_ge(n_tr.sem, n_tr.at(l, 8 * w + 2 * (tt - 1)))
                    v.tensor_scalar(xn[tt % 2], x[:, tt, :], stat[:, 12 + tt:13 + tt], None, ALU.mult).then_inc(n_xn.sem, 1)

                def store(tt):
                    for half in range(2):
                        v.wait_ge(n_tr.sem, n_tr.at(l, 8 * w + 2 * tt + half + 1))
                        o = (PW_N1, PW_N2)[w] + 4 * half
                        v.tensor_tensor(hT[:, 4 * half:4 * half + 4, tt * P:(tt + 1) * P],
                                        pb(2 * (tt % 2) + half).rearrange("p (k t) -> p k t", k=4),
                                        spread(pr[:, o:o + 4], 2, P), ALU.mult).then_inc(hT_ok.sem, 1)

                scale(0)
                scale(1)
                store(0)
                scale(2)
                store(1)
                scale(3)
                store(2)
                store(3)

            def low_h(l, w):
                for n in range(8):
                    v.wait_ge(hh_ok.sem, hh_ok.at(l, 8 * w + n + 1))
                    v.tensor_tensor(h_piece(hT_lo, n), h_piece(hT, n), h_piece(hT_hi, n), ALU.subtract).then_inc(hl_ok.sem, 1)

            with v.Fori(0, DEPTH) as l:
                norm(l, 0)
                v.wait_ge(dt_mm.sem, dt_mm.at(l, 1))
                low_h(l, 0)
                step = [0]

                def link(ins):
                    step[0] += 1
                    ins.then_inc(dt_v.sem, 1)
                    v.wait_ge(dt_v.sem, dt_v.at(l, step[0]))

                link(v.tensor_tensor(dr0, pb(4)[:, 0:256].rearrange("p (t h) -> p t h", t=NT),
                                     spread(pr[:, PW_DTB:PW_DTB + 64], 1, NT), ALU.add))
                v.scalar_tensor_tensor(out=dax, in0=dr0, scalar=-1.0, in1=dr0, op0=ALU.mult, op1=ALU.max).then_inc(dt_ax.sem, 1)
                v.wait_ge(dt_u.sem, dt_u.at(l, 2))
                v.tensor_scalar(dw, du, 1.0, None, ALU.add).then_inc(dt_w.sem, 1)
                v.wait_ge(dt_w.sem, dt_w.at(l, 1))
                link(v.tensor_scalar(dd, dw, -1.0, None, ALU.add))
                link(v.tensor_scalar(dz, dd, 0.0, None, ALU.is_equal))
                link(v.tensor_tensor(dd, dd, dz, ALU.add))
                link(v.reciprocal(dd, dd))
                v.wait_ge(dt_ln.sem, dt_ln.at(l, 1))
                link(v.tensor_tensor(dd, dd, dln, ALU.mult))
                link(v.tensor_tensor(dd, dd, dz, ALU.add))
                link(v.tensor_tensor(dd, dd, du, ALU.mult))
                link(v.scalar_tensor_tensor(out=dtv, in0=dr0, scalar=0.0, in1=dd, op0=ALU.max, op1=ALU.add))
                v.scalar_tensor_tensor(out=da, in0=dtv, scalar=-1.0, in1=spread(aexp, 1, NT),
                                       op0=ALU.mult, op1=ALU.mult).then_inc(dt_a.sem, 1)
                v.wait_ge(dt_cs.sem, dt_cs.at(l, 1))
                v.tensor_scalar(negA, pb(5)[:, 0:256].rearrange("p (t h) -> p t h", t=NT), -1.0, None,
                                ALU.mult).then_inc(dt_T.sem, 1)
                for d in range(2):
                    v.tensor_copy(aT[0:32, d, :], pb(6 + d)[0:32, :]).then_inc(dt_T.sem, 1)
                wait_alone(v, dt_T, l, 3)

                with v.Fori(0, GROUPS) as g:
                    v.wait_ge(y_ok.sem, y_ok.at(l, g * 2))
                    v.tensor_copy(gneg, negA.rearrange("p t (d h) -> p t d h", d=2)[:, :, :, bass.ds(g * RH, RH)]).then_inc(g_cp.sem, 1)
                    v.tensor_copy(gdt, dtv.rearrange("p t (d h) -> p t d h", d=2)[:, :, :, bass.ds(g * RH, RH)]).then_inc(g_cp.sem, 1)
                    v.tensor_copy(gp, pr[:, bass.ds(g * 32 + PW_CONV, 32)]).then_inc(g_cp.sem, 1)
                    v.wait_ge(g_cp.sem, g_cp.at(l, g * 3 + 3))
                    v.wait_ge(bc_in.sem, bc_in.at(l, g * 16 + 16))
                    for n in range(8):
                        r, s = 2 * (n // 4) + (n % 4) // 2, n % 2
                        parts = [(0, 0, 0, 256, 0, C_MF), (1, 1, 256, 256, 0, C_MB), (1, 0, 512, 128, 0, C_MB + P),
                                 (0, 1, 640, 128, 128, C_MF)]
                        for d, si, c0, w, l0, m in parts:
                            ins = v.scalar_tensor_tensor(
                                out=E[:, n, c0:c0 + w], in0=aBC[:, d, r, s * SEQ + l0:s * SEQ + l0 + w],
                                scalar=gneg[:, 2 * s + si, d, r:r + 1], in1=cst[:, m:m + w], op0=ALU.add, op1=ALU.add)
                        ins.then_inc(arg.sem, 1)
                    for j in range(4):
                        v.wait_ge(c_acc.sem, c_acc.at(l, g * 4 + (j + 1)))
                        for q, k in enumerate((0, 1, 3, 4)):
                            o = k - CONV // 2
                            lo, w = max(0, -o), SEQ - abs(o)
                            acc = cx[j].rearrange("p (s t) -> p s t", s=NSEQ)[:, :, lo:lo + w]
                            src = pb(j).rearrange("p (s t) -> p s t", s=NSEQ)[:, :, lo + o:lo + o + w]
                            ins = v.scalar_tensor_tensor(out=acc, in0=src, scalar=gp[:, 8 * j + k:8 * j + k + 1], in1=acc,
                                                         op0=ALU.mult, op1=ALU.add)
                            if q < 3:
                                ins.then_inc(c_tap.sem, 1)
                                v.wait_ge(c_tap.sem, c_tap.at(l, g * 12 + (3 * j + q + 1)))
                            else:
                                ins.then_inc(c_ok.sem, 1)
                    v.wait_ge(xt_ok.sem, xt_ok.at(l, g * 2 + 2))
                    for d in range(2):
                        v.tensor_tensor(xdt[d].rearrange("p t (r e) -> p t r e", r=RH),
                                        xtok.rearrange("p t (r e) -> p t r e", r=RH),
                                        spread(gdt[:, :, d, :], 3, HD), ALU.mult).then_inc(xd_ok.sem, 1)
                    for n in range(8):
                        s = n % 2
                        v.wait_ge(cb_mm.sem, cb_mm.at(l, g * 2 + 2))
                        v.wait_ge(ex.sem, ex.at(l, g * 8 + (n + 1)))
                        v.tensor_tensor(E[:, n, 0:512], E[:, n, 0:512], pb(s), ALU.mult)
                        two = pb(s)[:, 0:512].rearrange("p (a b) -> p a b", b=P)[:, 0:4:3, :]
                        v.tensor_tensor(E[:, n, 512:768].rearrange("p (a b) -> p a b", b=P),
                                        E[:, n, 512:768].rearrange("p (a b) -> p a b", b=P), two, ALU.mult).then_inc(m_ok.sem, 1)
                    for i in range(2):
                        v.wait_ge(y_mm.sem, y_mm.at(l, g * 2 + (i + 1)))
                        q = 8 * (2 + i) + 6
                        v.scalar_tensor_tensor(out=y3[i], in0=cx[2 + i], scalar=gp[:, q:q + 1], in1=pb(2 + i),
                                               op0=ALU.mult, op1=ALU.add).then_inc(y_v.sem, 1)
                        v.wait_ge(y_v.sem, y_v.at(l, g * 2 + (i + 1)))
                        v.wait_ge(z_s.sem, z_s.at(l, g * 2 + (i + 1)))
                        v.tensor_tensor(y3[i], y3[i], zs[i], ALU.mult).then_inc(y3_ok.sem, 1)
                v.wait_ge(r_mm.sem, r_mm.at(l, 1))
                v.tensor_scalar(sqsum, pb(4), 1.0 / D_INNER, EPS, ALU.mult, ALU.add).then_inc(r_ms.sem, 1)
                v.wait_ge(r_sq.sem, r_sq.at(l, 1))
                v.wait_ge(y_ok.sem, y_ok.at(l, 2 * GROUPS))
                v.reciprocal(rstdB, sqsum).then_inc(r_ok.sem, 1)

                with v.Fori(0, 4) as hp:
                    for u in range(1, 9, 2):
                        dst = qk[u] if u < 6 else vraw[u - 6]
                        v.wait_ge(p_mm.sem, p_mm.at(l, hp * 9 + (u + 1)))
                        v.tensor_copy(dst, pb(u % 4)).then_inc(p_evV.sem, 1)
                    v.wait_ge(bm_in.sem, bm_in.at(l, hp * 16 + 16))
                    for c in range(8):
                        j, qt = c // 4, c % 2
                        wait_alone(v, s_mm, l, hp * 8 + (c + 1))
                        for g in range(NG):
                            ins = v.tensor_tensor_reduce(
                                Pm[:, c, g, :], pb(2 * (c % 2) + g // 2)[:, (g % 2) * SEQ:(g % 2 + 1) * SEQ],
                                BM[:, qt, 3 * j + g, :], 1.0, -3e38, ALU.add, ALU.max, mx[:, c, g:g + 1])
                        ins.then_inc(s_v.sem, 1)
                        v.wait_ge(s_v.sem, s_v.at(l, hp * 8 + (c + 1)))
                        v.tensor_scalar(nm[:, c, :], mx[:, c, :], -1.0, None, ALU.mult).then_inc(s_nm.sem, 1)
                    st = [0]

                    def link(ins):
                        st[0] += 1
                        ins.then_inc(a_v.sem, 1)
                        v.wait_ge(a_v.sem, a_v.at(l, hp * 6 + st[0]))

                    link(v.tensor_reduce(m1, mx, AX, ALU.max))
                    link(v.tensor_tensor(wg, mx, spread(m1, 2, NG), ALU.subtract))
                    v.wait_ge(a_w.sem, a_w.at(l, hp + 1))
                    v.wait_ge(p_x.sem, p_x.at(l, hp * 8 + 8))
                    link(v.tensor_tensor(fw, wg, den, ALU.mult))
                    link(v.tensor_reduce(s1, fw, AX, ALU.add))
                    link(v.reciprocal(r1, s1))
                    link(v.tensor_tensor(fw, wg, spread(r1, 2, NG), ALU.mult))
                    assert st[0] == 6
                    for c in range(8):
                        for g in range(NG):
                            ins = v.tensor_scalar(Pm[:, c, g, :], Pm[:, c, g, :], fw[:, c, g:g + 1], None, ALU.mult)
                        ins.then_inc(p_f.sem, 1)
                    for n in range(1, 12, 2):
                        v.wait_ge(t_mm.sem, t_mm.at(l, hp * 12 + (n + 1)))
                        js, m = n // 3, n % 3
                        if js >= 2:
                            v.wait_ge(o_mm.sem, o_mm.at(l, hp * 4 + js - 1))
                        v.tensor_copy(PTt[js % 2][:, m * 512:(m + 1) * 512], pb(4 + n % 4)).then_inc(t_evV.sem, 1)
                for k in range(16):
                    v.wait_ge(yh_ok.sem, yh_ok.at(l, k + 1))
                    v.tensor_tensor(y_lo[:, k, :], yT[:, k, :], y_hi[:, k, :], ALU.subtract).then_inc(yl_ok.sem, 1)

                with v.Fori(0, 4) as c2:
                    for h in range(2):
                        c, b = c2 * 2 + h, 4 * h
                        v.wait_ge(mT_ok.sem, mT_ok.at(l, c))
                        v.wait_ge(pa_mm.sem, pa_mm.at(l, c + 1))
                        v.tensor_tensor(t1, pb(b + 2), rstdB, ALU.mult).then_inc(m_v.sem, 1)
                        v.wait_ge(m_v.sem, m_v.at(l, c * 3 + 1))
                        v.wait_ge(sg_ok.sem, sg_ok.at(l, c * 2 + 2))
                        v.tensor_tensor(t1, t1, sg[2 * h], ALU.mult).then_inc(m_v.sem, 1)
                        v.wait_ge(pb_mm.sem, pb_mm.at(l, c + 1))
                        v.tensor_tensor(t2, pb(b + 3), sg[2 * h + 1], ALU.mult).then_inc(m_v.sem, 1)
                        v.wait_ge(m_v.sem, m_v.at(l, c * 3 + 3))
                        v.tensor_tensor(mT[:, c, :], t1, t2, ALU.add).then_inc(mT_ok.sem, 1)

                for k in range(KD):
                    v.wait_ge(mh_ok.sem, mh_ok.at(l, k + 1))
                    v.tensor_tensor(m_lo[:, k, :], mT[:, k, :], m_hi[:, k, :], ALU.subtract).then_inc(ml_ok.sem, 1)
                for n in range(8):
                    tt, nh = n // 2, n % 2
                    xo = x[:, tt, nh * 512:(nh + 1) * 512]
                    v.wait_ge(out_mm.sem, out_mm.at(l, n + 1))
                    v.tensor_tensor(xo, xo, pb(n), ALU.add).then_inc(x_mid.sem, 1)

                norm(l, 1)
                low_h(l, 1)
                with v.Fori(0, PH // 2) as h2:
                    for hh in range(2):
                        h = h2 * 2 + hh
                        st = [0]

                        def link(ins):
                            st[0] += 1
                            ins.then_inc(k_v.sem, 1)
                            wait_alone(v, k_v, l, h * TK + st[0])

                        def top16(src, tmp, val, idx, n):
                            for i in range(n):
                                ins = v.max(val(i)[:, 0:8], src(i))
                            link(ins)
                            for i in range(n):
                                v.max_index(idx(i)[:, 0:8], val(i)[:, 0:8], src(i))
                                ins = v.match_replace(out=tmp(i), in_to_replace=val(i)[:, 0:8], in_values=src(i), imm_value=-3e38)
                            link(ins)
                            for i in range(n):
                                ins = v.max(val(i)[:, 8:16], tmp(i))
                            link(ins)
                            for i in range(n):
                                ins = v.max_index(idx(i)[:, 8:16], val(i)[:, 8:16], tmp(i))
                            link(ins)

                        wait_alone(v, q_sv, l, h * 2 + 2)
                        top16(lambda i: sc[hh][:, i // NT, i % NT, :], lambda i: sc2[:, i // NT, i % NT, :],
                              lambda i: v16[:, i // NT, i % NT, :], lambda i: x16[:, i // NT, i % NT, :], 2 * NT)
                        v.tensor_copy(f16, x16)
                        link(v.tensor_tensor(cand.rearrange("p t (i j) -> p t i j", i=16), spread(v16[:, 0], 3, 16),
                                             spread(v16[:, 1], 2, 16), ALU.add))
                        top16(lambda i: cand[:, i, :], lambda i: cand2[:, i, :], lambda i: cvh[:, i, :],
                              lambda i: ci.rearrange("p (t k) -> p t k", t=NT)[:, i, :], NT)
                        v.tensor_scalar(pij[:, 0, :], ci, 4, None, ALU.logical_shift_right)
                        link(v.tensor_scalar(pij[:, 1, :], ci, 15, None, ALU.bitwise_and))
                        link(v.tensor_copy(pf, pij))
                        for q in range(2):
                            flat = hot.rearrange("p t k j -> p (t k) j")
                            link(v.tensor_tensor(flat, spread(pf[:, q, :], 2, 16),
                                                 spread(cst[:, C_I16:C_I16 + 16], 1, NT * TOPK), ALU.is_equal))
                            link(v.tensor_tensor(hot, hot, spread(f16[:, q], 2, TOPK), ALU.mult))
                            ins = v.tensor_reduce(idh[:, q, :], flat, AX, ALU.add)
                            if q == 0:
                                link(ins)
                            else:
                                ins.then_inc(k_done.sem, 1)
                        assert st[0] == TK, st[0]
                        v.wait_ge(k_done.sem, k_done.at(l, h + 1))
                        v.tensor_copy(CV[:, :, h, :], cvh)
                        for q in range(2):
                            v.tensor_copy(ID[q][:, :, h, :], idh[:, q].rearrange("p (t k) -> p t k", t=NT))
                v.wait_ge(k_done.sem, k_done.at(l, PH))
                flat = [a.rearrange("p t h k -> p (t h) k") for a in (CV, Ge)]
                v.memset(gsum, 0.0).then_inc(g_fence.sem, 1)
                v.wait_ge(g_fence.sem, g_fence.at(l, 1))
                v.tensor_tensor(flat[1], flat[0], spread(flat[0][:, :, 0], 2, TOPK), ALU.subtract).then_inc(g_v.sem, 1)
                v.wait_ge(g_e.sem, g_e.at(l, 1))
                v.tensor_reduce(gsum, flat[1], AX, ALU.add).then_inc(g_v.sem, 1)
                v.wait_ge(g_v.sem, g_v.at(l, 2))
                v.reciprocal(grec, gsum).then_inc(g_v.sem, 1)
                v.wait_ge(g_v.sem, g_v.at(l, 3))
                v.tensor_tensor(flat[1], flat[1], spread(grec, 2, TOPK), ALU.mult).then_inc(g_ok.sem, 1)
                for q in range(2):
                    v.wait_ge(gt_mm.sem, gt_mm.at(l, q + 1))
                    v.tensor_copy(idT[q], pb(q)).then_inc(gt_ok.sem, 1)
                v.wait_ge(gt_mm.sem, gt_mm.at(l, 3))
                v.tensor_copy(gP[:, 0, :], pb(2)).then_inc(gt_ok.sem, 1)
                v.wait_ge(gt_ok.sem, gt_ok.at(l, 3))
                v.tensor_tensor(gr[0], pb(2), gP[:, 0, :], ALU.subtract).then_inc(gt_ok.sem, 1)
                v.wait_ge(gt_ok.sem, gt_ok.at(l, 4))
                v.tensor_copy(gP[:, 1, :], gr[0]).then_inc(gt_ok.sem, 1)
                v.wait_ge(gt_ok.sem, gt_ok.at(l, 5))
                v.tensor_tensor(gr[1], gr[0], gP[:, 1, :], ALU.subtract).then_inc(gt_ok.sem, 1)
                v.wait_ge(gt_ok.sem, gt_ok.at(l, 6))
                v.tensor_copy(gP[:, 2, :], gr[1]).then_inc(gt_ok.sem, 1)
                wait_alone(v, gt_ok, l, 7)

                def one_hots(l, base, stripe, tok, c):
                    n0 = base + (c + 1)
                    o = tok + 16 * c
                    v.tensor_tensor(eq[c % 2], spread(idT[0][:, bass.ds(o, 16)], 1, 16),
                                    iota_b[:, bass.ds(stripe * 16, 16), :], ALU.is_equal).then_inc(h_eq.sem, 1)
                    v.tensor_tensor(Bh[c % 2], spread(idT[1][:, bass.ds(o, 16)], 1, P), iota_b[:, 0:P, :], ALU.is_equal)
                    v.wait_ge(h_eq.sem, h_eq.at(l, n0))
                    v.tensor_tensor(A3[c % 2], spread(eq[c % 2], 1, 3), spread(gP[:, :, bass.ds(o, 16)], 2, 16),
                                    ALU.mult).then_inc(h_ok.sem, 1)

                def collect(l, base, G, tok, c):
                    v.wait_ge(h_mm.sem, h_mm.at(l, base + (c + 1)))
                    src = routes[:, 2 * (c % 2):2 * (c % 2) + 2, :].rearrange("p a (t x) -> p (a t) x", x=64)
                    src = src[:, :, 0:48].rearrange("p t (q n) -> p n t q", q=3)
                    v.tensor_reduce(G[:, :, bass.ds(tok + 16 * c, 16)], src, AX, ALU.add).then_inc(G_ok.sem, 1)

                with v.Fori(0, BLOCKS) as b:
                    for c in range(0, 8, 2):
                        one_hots(l, b * 8, 0, b * P, c)
                        one_hots(l, b * 8, 0, b * P, c + 1)
                        collect(l, b * 8, Gs[0], b * P, c)
                        collect(l, b * 8, Gs[0], b * P, c + 1)
                with v.Fori(0, STRIPES // 2) as sp2:
                    for par2 in range(2):
                        with v.Fori(0, BLOCKS) as b:
                            stripe = sp2 * 2 + par2
                            blk = sp2 * (2 * BLOCKS) + par2 * BLOCKS + b
                            base = blk * 8 + BLOCKS * 8
                            G, G_next = Gs[par2], Gs[1 - par2]

                            def routed(j):
                                v.wait_ge(u_ge.sem, u_ge.at(l, blk * 4 + (j + 1)))
                                v.wait_ge(G_ok.sem, G_ok.at(l, stripe * (8 * BLOCKS) + 8 * BLOCKS))
                                v.tensor_tensor(gh[j], gh[j], G[:, b * 4 + j, :], ALU.mult).then_inc(gh_m.sem, 1)

                            def routed_low(j):
                                v.wait_ge(gh_hi.sem, gh_hi.at(l, blk * 4 + (j + 1)))
                                v.tensor_tensor(gh_l[j][:, :], gh[j], gh_h[j][:, :], ALU.subtract).then_inc(gh_ok.sem, 1)

                            for j in range(4):
                                one_hots(l, base, stripe + 1, b * P, j)
                                if j:
                                    collect(l, base, G_next, b * P, j - 1)
                                routed(j)
                                if j:
                                    routed_low(j - 1)
                            routed_low(3)
                            for n in range(8):
                                tt, nh = n // 2, n % 2
                                xo = x[:, tt, nh * 512:(nh + 1) * 512]
                                if n % 2 == 0:
                                    collect(l, base, G_next, b * P, 3 + n // 2)
                                    one_hots(l, base, stripe + 1, b * P, 4 + n // 2)
                                v.wait_ge(v_mm.sem, v_mm.at(l, blk * 8 + (n + 1)))
                                v.tensor_tensor(xo, xo, pb(2 + n % 2), ALU.add).then_inc(v_add.sem, 1)
                            collect(l, base, G_next, b * P, 7)

            v.wait_ge(f_w, 16)
            v.wait_ge(f_ss, 4)
            v.tensor_scalar(stat[:, 4:8], stat[:, 0:4], 1.0 / D, EPS, ALU.mult, ALU.add).then_inc(f_v, 1)
            v.wait_ge(f_sq, 1)
            v.reciprocal(stat[:, 12:16], stat[:, 8:12]).then_inc(f_v, 1)
            v.wait_ge(f_v, 2)
            for tt in range(NT):
                if tt >= 2:
                    v.wait_ge(f_out, 16 * (tt - 1))
                v.scalar_tensor_tensor(out=fin[tt % 2], in0=x[:, tt, :], scalar=stat[:, 12 + tt:13 + tt], in1=wfin,
                                       op0=ALU.mult, op1=ALU.mult).then_inc(f_ok, 1)


def unit_tiles(w, cols):
    k = w.shape[0] // P
    r = w.reshape(k, P, -1)
    return np.stack([np.ascontiguousarray(r[:, :, c:c + P].transpose(1, 0, 2)).reshape(P, k * P) for c in cols])


def lay_out(i):
    w_in = i["w_in"]
    w_ssd, w_att, w_mrg, w_qry, w_u, par = [], [], [], [], [], []
    for l in range(DEPTH):
        w = w_in[l]
        r = range(GROUPS)
        cols = [[OFF_XBC + D_INNER + g * P, OFF_XBC + D_INNER + (GROUPS + g) * P, OFF_XBC + 2 * g * P,
                 OFF_XBC + (2 * g + 1) * P, 2 * g * P, (2 * g + 1) * P] for g in r]
        w_ssd.append(np.stack([unit_tiles(w, c) for c in cols]))
        cols = [[o + g * 512 + hp * P for g in range(NG) for o in (OFF_Q, OFF_K)]
                + [OFF_V + g * 512 + hp * P for g in range(NG)] for hp in range(4)]
        w_att.append(np.stack([unit_tiles(w, c) for c in cols]))
        m = np.zeros((8, 5, P, UNIT), np.float32)
        for c in range(8):
            m[c, 0:2] = unit_tiles(w, [OFF_GATE + c * P, OFF_GATE + D + c * P])
            m[c, 2] = unit_tiles(i["w_ssd_out"][l][:D], [c * P])[0]
            m[c, 3] = unit_tiles(i["w_ssd_out"][l][D:], [c * P])[0]
            m[c, 4, :, 0:512] = unit_tiles(i["w_attn_out"][l], [c * P])[0]
        w_mrg.append(m)
        w_qry.append(unit_tiles(i["w_query"][l], [n * P for n in range(2 * PH)]).reshape(PH // 2, 4, P, UNIT))
        u = i["expert_u"][l].reshape(EXPERT_TILES, P, KD, P)
        w_u.append(u.transpose(0, 3, 2, 1).reshape(STRIPES * BLOCKS, 4, P, UNIT))
        q = np.zeros((P, PW), np.float32)
        q[:, PW_N1:PW_N1 + KD] = i["norm1_w"][l].reshape(KD, P).T
        q[:, PW_N2:PW_N2 + KD] = i["norm2_w"][l].reshape(KD, P).T
        skip = np.repeat(i["D_skip"][l], HD)
        for g in r:
            for t, ch in enumerate((D_INNER + g * P, D_INNER + (GROUPS + g) * P, 2 * g * P, (2 * g + 1) * P)):
                o = PW_CONV + g * 32 + t * 8
                q[:, o:o + CONV] = i["conv_w"][l][:, ch:ch + P].T
                q[:, o + 5] = i["conv_b"][l][ch:ch + P]
                if t >= 2:
                    q[:, o + 6] = skip[ch:ch + P]
                    q[:, o + 7] = i["ssd_norm_w"][l][ch:ch + P]
        q[:, PW_DTB:PW_DTB + 64] = i["dt_bias"][l].reshape(1, 64)
        q[:, PW_ALOG:PW_ALOG + 64] = i["A_log"][l].reshape(1, 64)
        q[:, PW_KEYS:PW_KEYS + 256] = i["sub_keys"][l].transpose(2, 0, 1).reshape(P, 256)
        q[:, PW_WDT:PW] = w[:, OFF_DT:OFF_Q].reshape(KD, P, 64).transpose(1, 0, 2).reshape(P, KD * 64)
        par.append(q)
    par.append(par[0])
    return {
        "x_prompt": i["x_prompt"], "x_sample": i["x_sample"], "consts": constants(), "biases": bias_constants(),
        "rel": i["rel_bias"], "par": np.stack(par), "w_ssd": np.stack(w_ssd), "w_att": np.stack(w_att),
        "w_mrg": np.stack(w_mrg), "w_out": i["w_out"].reshape(DEPTH, KD, P, D), "w_qry": np.stack(w_qry),
        "w_u": np.stack(w_u), "w_v": i["expert_v"].reshape(DEPTH, STRIPES * BLOCKS, 4, P, D),
        "w_final": i["final_norm_w"],
    }


def kernel(**inputs):
    import numpy as _np
    import concourse.bacc as _bacc
    from concourse.bass_utils import run_bass_kernel_spmd as _run

    nc = _bacc.Bacc("TRN2", target_bir_lowering=False, num_devices=1)
    arrays, args = {}, {}
    for name, a in lay_out({k: _np.asarray(v) for k, v in inputs.items()}).items():
        a = _np.ascontiguousarray(a)
        arrays[f"in_{name}"] = a
        args[name] = nc.dram_tensor(f"in_{name}", a.shape, F32, kind="ExternalInput").ap()
    for name in ("y_prompt", "y_sample"):
        args[name] = nc.dram_tensor(f"out_{name}", (1, SEQ, D), F32, kind="ExternalOutput").ap()
    build(nc, **args)
    r = _run(nc, [arrays], core_ids=[0])
    return tuple(r.results[0][f"out_{n}"] for n in ("y_prompt", "y_sample"))
```

```python
from contextlib import ExitStack

import numpy as np
import concourse.bass as bass
from concourse import mybir

F32 = mybir.dt.float32
F32R = mybir.dt.float32r
BF16 = mybir.dt.bfloat16
U32 = mybir.dt.uint32
ALU = mybir.AluOpType
ACT = mybir.ActivationFunctionType
AX = mybir.AxisListType.X

P = 128
D = 1024
KD = D // P
SEQ = 256
NSEQ = 2
T = NSEQ * SEQ
NT = T // P
DEPTH = 2
D_INNER = 2048
GROUPS = 8
RH = 4
HD = 64
SSD_HEADS = 32
CONV = 5
CONV_DIM = D_INNER + 2 * GROUPS * P
ATTN_WIDTH = 1536
NG = 3
WINDOWS = ((128, 1), (512, 4), (2048, 16))
REL_BUCKETS = 32
REL_MAX = 1024
PH = 8
TOPK = 16
ROWS = 4
COLS = 4
CANDS = ROWS * TOPK + (TOPK - ROWS) * COLS
EXPERT_TILES = 128
EPS = 1e-6
OFF_XBC = D_INNER
OFF_DT = OFF_XBC + CONV_DIM
OFF_Q = OFF_DT + 2 * SSD_HEADS
OFF_K = OFF_Q + ATTN_WIDTH
OFF_V = OFF_K + ATTN_WIDTH
OFF_GATE = OFF_V + ATTN_WIDTH
NEG = -1e30

UNIT = KD * P
SLOTS = 7
CREDIT = 16
STRIPES = 8
BLOCKS = 4
PHASES = (("ssd", GROUPS, (0, 1, 2, 3, 4, 5)), ("att", 4, (0, 1, 2, 3, 4, 5, 6, 2, 3)), ("mrg", 8, (0, 1, 2, 3, 4)),
          ("out", 1, (0, 1, 2, 3, 4, 5, 6, 2)), ("qry", PH // 2, (0, 1, 2, 3, 4, 5)),
          ("pre", BLOCKS, (0, 1)), ("val", BLOCKS // 2, (3, 4, 5, 6, 0, 1, 2, 6)), ("peer", (STRIPES - 1) * BLOCKS, (0, 1, 2, 0, 3, 4, 5, 6)))
NAMES = [q[0] for q in PHASES]
UNITS = sum(i * len(n) for _, i, n in PHASES)
BASE = {}
LOADS = {}
_u = 0
_per_slot = [0] * SLOTS
for _name, _i, _n in PHASES:
    BASE[_name] = _u
    LOADS[_name] = list(_per_slot)
    _u += _i * len(_n)
    for _j in _n:
        _per_slot[_j] += _i
SLOT_LOADS = list(_per_slot)


def last_user(name, j):
    k = NAMES.index(name)
    slot = PHASES[k][2][j]
    for jj in range(j - 1, -1, -1):
        if PHASES[k][2][jj] == slot:
            return BASE[name] + jj
    for back in range(1, len(PHASES) + 1):
        pn, it, slots = PHASES[(k - back) % len(PHASES)]
        for jj in range(len(slots) - 1, -1, -1):
            if slots[jj] == slot:
                return BASE[pn] + (it - 1) * len(slots) + jj - (UNITS if k - back < 0 else 0)
    raise ValueError(name)


SPLIT = {}
_u = 0
for _name, _i, _n in PHASES:
    SPLIT[_name] = _u
    _u += _i * (4 if _name == "mrg" else len(_n))
SPLITS = _u
SPLIT_PEER = (0, 1, 2, 4, 3, 5, 6, 7)
LOAD_PEER = (0, 1, 2, 4, 5, 3, 6, 7)


PW_N1, PW_N2, PW_CONV = 0, 8, 16
PW_DTB = PW_CONV + GROUPS * 32
PW_ALOG = PW_DTB + 64
PW_KEYS = PW_ALOG + 64
PW_WDT = PW_KEYS + 256
PW = PW_WDT + KD * 64

C_ID, C_LE, C_GE, C_ONE, C_MF, C_MB, C_I16, C_IOTA = 0, 128, 256, 384, 512, 768, 1024, 1040
CW = C_IOTA + 144
RW = 2 * SEQ


def t5_bucket(rel):
    half = REL_BUCKETS // 2
    exact = half // 2
    n = np.abs(rel)
    large = exact + (np.log(np.maximum(n, 1) / exact) / np.log(REL_MAX / exact) * (half - exact)).astype(np.int32)
    large = np.minimum(large, half - 1)
    return np.where(rel > 0, half, 0) + np.where(n < exact, n, large)


def constants():
    c = np.zeros((P, CW), np.float32)
    i = np.arange(P)
    c[:, C_ID:C_ID + P] = np.eye(P)
    c[:, C_LE:C_LE + P] = i[:, None] <= i[None, :]
    c[:, C_GE:C_GE + P] = i[:, None] >= i[None, :]
    c[:, C_ONE:C_ONE + P] = 1.0
    c[:, C_MF:C_MF + P] = np.where(i[None, :] >= i[:, None], 0.0, NEG)
    c[:, C_MB + P:C_MB + 2 * P] = np.where(i[None, :] <= i[:, None], 0.0, NEG)
    c[:, C_I16:C_I16 + 16] = np.arange(16)
    c[:, C_IOTA:C_IOTA + 144] = np.arange(144)
    return c


def bias_constants():
    d = np.arange(RW) - (SEQ - 1)
    hot = (t5_bucket(d)[None, :] == np.arange(REL_BUCKETS)[:, None]).astype(np.float32)
    mask = np.full((NG * 8, RW), NEG, np.float32)
    for g, (win, dil) in enumerate(WINDOWS):
        ok = (d % dil == 0) & (np.abs(d // dil) <= (win // 2) // dil)
        mask[g * 8:(g + 1) * 8, ok] = 0.0
    out = np.zeros((56, RW), np.float32)
    out[0:32] = hot
    out[32:56] = mask
    return out


class Count:

    def __init__(self, sem, per_layer, before=0):
        self.sem, self.per_layer, self.before = sem, per_layer, before

    def at(self, layer, n):
        return layer * self.per_layer + (n + self.before)


def spread(ap, axis, n):
    s = ap.unsqueeze(axis)
    shape = list(s.shape)
    shape[axis] = n
    return s.broadcast_to(shape)


def build(nc, x_prompt, x_sample, consts, biases, rel, par, w_ssd, w_att, w_mrg, w_out, w_qry, w_u, w_v,
          w_final, y_prompt, y_sample):
    with ExitStack() as ctx:
        at_byte = {}

        def sb(name, shape, dt=F32):
            t = ctx.enter_context(nc.sbuf_tensor(name, shape, dt))
            at_byte[name] = nc.sbuf_base - int(np.prod(shape[1:])) * (2 if dt is BF16 else 4)
            return t

        def part(name, ap):
            shape = list(ap.shape)
            return nc.alloc_sbuf_tensor_at(name, shape, F32R, offset=at_byte[ap.tensor.name] + 4 * ap.offset)

        def sem(name):
            return ctx.enter_context(nc.semaphore(name))

        def count(name, per_layer, before=0):
            return Count(sem(name), per_layer, before)

        a_dram = nc.dram_tensor("a_rows", [2, SSD_HEADS, T], F32).ap()
        r_dram = nc.dram_tensor("bias_rows", [NG * 8, RW], F32).ap()
        bias_dram = nc.dram_tensor("bias_tiles", [4, 2, P, 6, SEQ], F32).ap()

        bank = [ctx.enter_context(nc.psum_tensor(f"bank{i}", [P, 512], F32)) for i in range(4)]
        routes = ctx.enter_context(nc.psum_tensor("banks4to7", [P, 4, 512], F32))

        def pb(i):
            return bank[i][:, :] if i < 4 else routes[:, i - 4, :]

        x = sb("x", [P, NT, D])
        hT = sb("hT", [P, KD, T])
        ring = [sb(f"ring{j}", [P, UNIT]) for j in range(SLOTS)]
        spare = [sb(f"spare{j}", [P, UNIT]) for j in range(2)]
        pr = sb("pr", [P, PW])
        cst = sb("cst", [P, CW])
        iota_b = sb("iota_b", [P, 144, 16], BF16)
        stat = sb("stat", [P, 64])
        yT = sb("yT", [P, 16, T])
        late = sb("late", [P, 5 * T])
        rstdB = late[:, 0:T]
        oT = late[:, T:].rearrange("p (h t) -> p h t", h=4)
        ident = cst[:, C_ID:C_ID + P]
        le = cst[:, C_LE:C_LE + P]
        ge = cst[:, C_GE:C_GE + P]
        ones = cst[:, C_ONE:C_ONE + P]
        iota16 = sb("iota16", [P, 16], BF16)

        WORDS = 21300
        arena = sb("arena", [P, WORDS])
        used = [0]

        def cut(*shape, dt=F32):
            n = 1
            for s in shape:
                n *= s
            words = n if dt in (F32, U32) else (n + 1) // 2
            o = used[0]
            used[0] += words
            assert used[0] <= WORDS, used[0]
            v = arena[:, o:o + words]
            if dt is not F32:
                v = v.bitcast(dt)
            if len(shape) > 1:
                names = " ".join(f"d{i}" for i in range(len(shape)))
                v = v.rearrange(f"p ({names}) -> p {names}", **{f"d{i}": s for i, s in enumerate(shape)})
            return v

        rel_w, hot_rel, mask_rel = cut(NG * 8), cut(RW), cut(RW)
        used[0] = 0
        hTh = cut(KD, T)
        after_h = used[0]
        xn = [cut(D), cut(D)]
        junk = cut(D)
        decays = used[0]
        used[0] = after_h
        xtok = cut(NT, 2 * P)
        xdt = [cut(NT, 2 * P) for _ in range(2)]
        used[0] = decays
        dtv = cut(NT, 64)
        negA = cut(NT, 64)
        keep = used[0]
        dr0, dax, du, dw, dln, dd, dz, da = (cut(NT, 64) for _ in range(8))
        aexp = cut(64)
        aT = cut(2, T)
        used[0] = keep
        aBC = cut(2, RH, T)
        E = cut(8, 768)
        cx = [cut(T) for _ in range(4)]
        zs = [oT[:, i, :] for i in range(2)]
        y3 = [oT[:, 2 + i, :] for i in range(2)]
        sq = [cut(T) for _ in range(2)]
        gneg = cut(NT, 2, RH)
        gdt = cut(NT, 2, RH)
        gp = cut(32)
        sqsum = rstdB
        used[0] = after_h
        qk = [cut(T) for _ in range(6)]
        vtok = [cut(NT, P) for _ in range(3)]
        BM = cut(2, 6, SEQ)
        Pm = cut(8, NG, SEQ)
        mx, nm, den, wg, fw = (cut(8, NG) for _ in range(5))
        m1, s1, r1 = (cut(8) for _ in range(3))
        top = used[0]
        PTt = [cut(NG * 2 * SEQ) for _ in range(2)]
        used[0] = top
        vraw = [cut(T) for _ in range(3)]
        used[0] = after_h
        mT = cut(8, T)
        sg = [cut(T) for _ in range(4)]
        t1 = cut(T)
        t2 = cut(T)
        yh = cut(16, T)
        used[0] -= 16 * T
        mTh = cut(8, T)
        used[0] = after_h
        qT = [cut(T) for _ in range(4)]
        sc = [cut(2, NT, P) for _ in range(2)]
        sc2 = cut(2, NT, P)
        v16 = cut(2, NT, TOPK)
        x16 = cut(2, NT, TOPK, dt=U32)
        b16 = cut(2, NT, TOPK, dt=BF16)
        cand = cut(NT, CANDS)
        cand2 = cut(NT, CANDS)
        cvh = cut(NT, TOPK)
        ci = cut(NT * TOPK, dt=U32)
        pij = cut(4, NT * TOPK, dt=U32)
        pf = cut(4, NT * TOPK)
        over = cut(NT * TOPK)
        ij = cut(2, NT * TOPK, dt=BF16)
        hot = cut(2 * NT, TOPK, 16, dt=BF16)
        idh = cut(2, NT * TOPK)
        CV = cut(NT, PH, TOPK)
        ID = cut(2, NT, PH, TOPK)
        Ge = cut(NT, PH, TOPK)
        gsum = cut(32)
        grec = cut(32)
        gr = [cut(T) for _ in range(2)]
        assert used[0] <= 28 * T + 2 * D
        used[0] = KD * T
        Gs = [yT, cut(16, T)]
        gh = [cut(T) for _ in range(4)]
        ghh = [cut(T) for _ in range(4)]
        hi_u = [spare[0][:, :], spare[1][:, :]]
        hi_v = [late[:, 0:UNIT], late[:, UNIT:2 * UNIT], pr[:, 0:UNIT], cut(UNIT)]
        hi_u = [part(f"hi_u{n}", a) for n, a in enumerate(hi_u)]
        hi_v = [part(f"hi_v{n}", a) for n, a in enumerate(hi_v)]
        lo = [part(f"lo{n}", ring[n][:, :]) for n in range(7)]
        y_hi, y_lo = part("y_hi", yh), part("y_lo", yT[:, :, :])
        m_hi, m_lo = part("m_hi", mTh), part("m_lo", mT)
        hT_hi, hT_lo = part("hT_hi", hTh), part("hT_lo", hT[:, :, :])
        gh_h = [part(f"gh_hi{n}", a) for n, a in enumerate(ghh)]
        gh_l = [part(f"gh_lo{n}", a) for n, a in enumerate(gh)]
        idT = [late[:, 2 * UNIT + q * (T // 2):2 * UNIT + (q + 1) * (T // 2)].bitcast(BF16) for q in range(2)]
        gP = cut(3, T, dt=BF16)
        Bh = [cut(P, 16, dt=BF16) for _ in range(2)]
        eq = [cut(16, 16, dt=BF16) for _ in range(2)]
        A3 = [cut(3, 16, 16, dt=BF16) for _ in range(2)]
        used[0] = 0
        fin = [cut(D) for _ in range(2)]
        fjunk = cut(D)
        wfin = cut(D)

        w_in = [sem(f"w_in{j}") for j in range(SLOTS)]
        slot_free = Count(sem("slot_free"), UNITS, CREDIT)
        cst_in, x_in, rel_in, row_out, bias_out = (sem(n) for n in ("cst_in", "x_in", "rel_in", "row_out", "bias_out"))
        iota_ok, rel_mm, row_ok = sem("iota_ok"), sem("rel_mm"), sem("row_ok")
        par_in = count("par_in", 16)
        n_ss, n_ms, n_sqrt, n_rs, n_xn, n_tr, hT_ok = (count(n, k) for n, k in (
            ("n_ss", 8), ("n_ms", 2), ("n_sqrt", 2), ("n_rs", 2), ("n_xn", 8), ("n_tr", 16), ("hT_ok", 16)))
        dt_mm, dt_ax, dt_u, dt_w, dt_ln, dt_a, dt_cs, dt_T = (count(n, k) for n, k in (
            ("dt_mm", 1), ("dt_ax", 1), ("dt_u", 2), ("dt_w", 1), ("dt_ln", 1), ("dt_a", 1), ("dt_cs", 1), ("dt_T", 3)))
        dt_v = count("dt_v", 9)
        aT_out = count("aT_out", 16)
        bc_in = count("bc_in", 16 * GROUPS)
        g_cp = count("g_cp", 3 * GROUPS)
        arg, ex = count("arg", 8 * GROUPS), count("ex", 8 * GROUPS)
        c_mm, c_acc, c_tap, c_ok, c_s = (count(n, k * GROUPS) for n, k in (
            ("c_mm", 4), ("c_acc", 4), ("c_tap", 12), ("c_ok", 4), ("c_s", 4)))
        z_mm, z_s = count("z_mm", 2 * GROUPS), count("z_s", 2 * GROUPS, 2)
        xt_mm, xt_ok, xd_ok = (count(n, 2 * GROUPS) for n in ("xt_mm", "xt_ok", "xd_ok"))
        cb_mm, m_ok = count("cb_mm", 2 * GROUPS), count("m_ok", 8 * GROUPS)
        y_mm, y_v, y3_ok, sq_ok, y_ok = (count(n, 2 * GROUPS, b) for n, b in (
            ("y_mm", 0), ("y_v", 2), ("y3_ok", 0), ("sq_ok", 0), ("y_ok", 2)))
        sq_sum = count("sq_sum", 1 + 2 * GROUPS, 2)
        r_mm, r_ms, r_sq, r_ok = (count(n, 1) for n in ("r_mm", "r_ms", "r_sq", "r_ok"))
        bm_in = count("bm_in", 16 * 4)
        p_mm, p_evA, p_evV = count("p_mm", 36), count("p_evA", 20), count("p_evV", 16)
        vt_mm, vt_ok = count("vt_mm", 12), count("vt_ok", 12)
        s_mm, s_v, s_nm, p_x = (count(n, 32) for n in ("s_mm", "s_v", "s_nm", "p_x"))
        a_v, a_w = count("a_v", 4 * 6), count("a_w", 4)
        p_f = count("p_f", 32)
        t_mm, t_evA, t_evV = count("t_mm", 48), count("t_evA", 24), count("t_evV", 24)
        o_mm, o_ok = count("o_mm", 16), count("o_ok", 4, 1)
        ga_mm, gb_mm, pa_mm, pb_mm = (count(n, 8) for n in ("ga_mm", "gb_mm", "pa_mm", "pb_mm"))
        sg_ok = count("sg_ok", 16)
        m_v, mT_ok = count("m_v", 24), count("mT_ok", 8, 2)
        out_mm, x_mid = count("out_mm", 8), count("x_mid", 8)
        q_mm, q_ev, q_s, q_sv = (count(n, 16, b) for n, b in (("q_mm", 0), ("q_ev", 0), ("q_s", 0), ("q_sv", 4)))
        TK = 23
        k_v, k_done = count("k_v", TK * PH), count("k_done", PH, 2)
        g_v, g_e, g_ok, gt_mm, gt_ok = (count(n, k) for n, k in (
            ("g_v", 3), ("g_e", 1), ("g_ok", 1), ("gt_mm", 3), ("gt_ok", 7)))
        g_fence = count("g_fence", 1)
        CH = STRIPES * BLOCKS * 8
        h_eq, h_ok, h_mm, G_ok = (count(n, CH) for n in ("h_eq", "h_ok", "h_mm", "G_ok"))
        h0_mm, hid_ok, gh0_m = count("h0_mm", 16), count("hid_ok", 16, 4), count("gh0_m", 16)
        u_mm, u_ge, gh_m = (count(n, EXPERT_TILES - 16, b) for n, b in (("u_mm", 0), ("u_ge", 2), ("gh_m", 0)))
        gh_hi, gh_ok = count("gh_hi", EXPERT_TILES), count("gh_ok", EXPERT_TILES)
        w_hi, w_lo = count("w_hi", SPLITS), count("w_lo", SPLITS)
        hh_ok, hl_ok = count("hh_ok", 16), count("hl_ok", 16)
        yh_ok, yl_ok, mh_ok, ml_ok = (count(n, k) for n, k in (("yh_ok", 16), ("yl_ok", 16), ("mh_ok", 8), ("ml_ok", 8)))
        v_mm, v_add = count("v_mm", 256), count("v_add", 256, 2)
        f_w, f_ss, f_v, f_sq, f_x, f_ok, f_out = (sem(n) for n in ("f_w", "f_ss", "f_v", "f_sq", "f_x", "f_ok", "f_out"))

        block = ctx.enter_context(nc.Block())

        def wait_alone(e, c, layer, n):
            value = c.at(layer, n)
            e.compute_val(value)
            e.wait_ge(cst_in, 16)
            e.wait_ge(c.sem, value)

        def h_piece(h, n):
            return h[:, 4 * (n % 2):4 * (n % 2) + 4, (n // 2) * P:(n // 2 + 1) * P]

        def loaded(e, l, name, i, j):
            slots = PHASES[NAMES.index(name)][2]
            s = slots[j]
            first, each = LOADS[name][s], slots.count(s)
            e.wait_ge(w_in[s], (l * SLOT_LOADS[s] + i * each + (first + slots[:j].count(s) + 1)) * 16)

        def split_no(name, i, j):
            slots = PHASES[NAMES.index(name)][2]
            if name == "peer":
                j = SPLIT_PEER.index(j)
            return i * (4 if name == "mrg" else len(slots)) + (SPLIT[name] + j)

        def places(name, j):
            slot = PHASES[NAMES.index(name)][2][j]
            if name == "val":
                return slot, (hi_v[2], hi_v[3], hi_v[0], hi_v[1], hi_u[0], hi_u[1], hi_v[0], hi_v[1])[j]
            return slot, hi_v[j - 4] if name == "peer" and j >= 4 else hi_u[j % 2]

        @block.sync
        def _(sp):
            sp.dma_start(cst[:, :], consts).then_inc(cst_in, 16)
            sp.dma_start(x[:, 0:2, :], x_prompt.rearrange("b (t p) d -> p (b t) d", p=P)).then_inc(x_in, 16)
            sp.dma_start(x[:, 2:4, :], x_sample.rearrange("b (t p) d -> p (b t) d", p=P)).then_inc(x_in, 16)

            def load(src, j, free_at):
                sp.compute_val(src.offset)
                if free_at is not None:
                    sp.compute_val(free_at)
                    sp.wait_ge(cst_in, 16)
                    sp.wait_ge(slot_free.sem, free_at)
                sp.dma_start(ring[j][:, :], src).then_inc(w_in[j], 16)

            def phase(l, name, unit, order=None):
                _, iters, slots = PHASES[NAMES.index(name)]
                n = len(slots)
                order = order or range(n)
                for j in order:
                    u = last_user(name, j)
                    load(unit(0, j), slots[j], slot_free.at(l, u + 1) if u >= -CREDIT else None)
                if iters > 1:
                    with sp.Fori(1, iters) as i:
                        for j in order:
                            earlier = [jj for jj in range(j) if slots[jj] == slots[j]]
                            if earlier:
                                u = i * n + (BASE[name] + earlier[-1])
                            else:
                                last = max(jj for jj in range(n) if slots[jj] == slots[j])
                                u = (i - 1) * n + (BASE[name] + last)
                            load(unit(i, j), slots[j], slot_free.at(l, u + 1))

            with sp.Fori(0, DEPTH) as l:
                phase(l, "ssd", lambda i, j: w_ssd[l, i, j])
                phase(l, "att", lambda i, j: w_att[l, i, j])
                phase(l, "mrg", lambda i, j: w_mrg[l, i, j])
                phase(l, "out", lambda i, j: w_out[l, j])
                tiles = w_u.rearrange("l b j p u -> l (b j) p u")
                phase(l, "qry", lambda i, j: tiles[l, i * 2 + j // 3] if j % 3 == 2 else w_qry[l, i, j // 3 * 2 + j % 3])
                phase(l, "pre", lambda i, j: tiles[l, i * 2 + (8 + j)])
                phase(l, "val", lambda i, j: w_v[l, i * 2 + j // 4, j % 4])
                phase(l, "peer", lambda i, j: w_u[l, i + BLOCKS, j] if j < 4 else w_v[l, i + BLOCKS, j - 4], LOAD_PEER)
            yp = y_prompt.rearrange("b (t p) d -> p (b t) d", p=P)
            ys = y_sample.rearrange("b (t p) d -> p (b t) d", p=P)
            for tt in range(NT):
                sp.wait_ge(f_ok, tt + 1)
                dst = yp[:, tt, :] if tt < 2 else ys[:, tt - 2, :]
                sp.dma_start(dst, fin[tt % 2]).then_inc(f_out, 16)
                sp.wait_ge(f_out, 16 * (tt + 1))

        @block.gpsimd
        def _(pool):
            pool.dma_start(pr[:, :], par[0]).then_inc(par_in.sem, 16)
            pool.wait_ge(row_ok, 1)
            pool.dma_start(r_dram, oT[0:NG * 8, 0, :]).then_inc(row_out, 16)
            pool.wait_ge(row_out, 16)
            for hp in range(4):
                for qt in range(2):
                    for j in range(2):
                        src = bass.AP(tensor=r_dram.tensor, offset=(2 * hp + j) * RW + (SEQ - 1) - qt * P,
                                      ap=[[8 * RW, NG], [-1, P], [1, SEQ]])
                        dst = bias_dram[hp, qt, :, 3 * j:3 * j + 3, :].rearrange("q g k -> g q k")
                        pool.dma_start(dst, src).then_inc(bias_out, 16)
            with pool.Fori(0, DEPTH) as l:
                wait_alone(pool, dt_T, l, 3)
                pool.dma_start(a_dram.rearrange("d h t -> h d t"), aT[0:SSD_HEADS]).then_inc(aT_out.sem, 16)
                nc.gpsimd.memset(sqsum, 0.0).then_inc(sq_sum.sem, 1)

                def spread_rows(g):
                    return (aBC, spread(a_dram[:, bass.ds(g * RH, RH), :].rearrange("d h t -> d (h t)"), 0, P))

                def low(name, i, j):
                    slot, hi = places(name, j)
                    pool.wait_ge(w_hi.sem, w_hi.at(l, split_no(name, i, j) + 1))
                    nc.gpsimd.tensor_tensor(lo[slot][:, :], ring[slot][:, :], hi[:, :], ALU.subtract).then_inc(w_lo.sem, 1)

                dst, src = spread_rows(0)
                wait_alone(pool, aT_out, l, 16)
                pool.dma_start(dst.rearrange("p d h t -> p d (h t)"), src).then_inc(bc_in.sem, 16)

                def add_squares(g):
                    for i in range(2):
                        pool.wait_ge(sq_ok.sem, sq_ok.at(l, g * 2 + (i + 1)))
                        pool.wait_ge(sq_sum.sem, sq_sum.at(l, g * 2 + (i + 1)))
                        nc.gpsimd.tensor_tensor(sqsum, sqsum, sq[i], ALU.add).then_inc(sq_sum.sem, 1)

                low("ssd", 0, 0)
                low("ssd", 0, 1)

                def group(g, more):
                    for j in range(2, 6):
                        low("ssd", g, j)
                    if more:
                        dst, src = spread_rows(g + 1)
                        pool.compute_val(src.offset)
                        wait_alone(pool, arg, l, g * 8 + 8)
                        pool.dma_start(dst.rearrange("p d h t -> p d (h t)"), src).then_inc(bc_in.sem, 16)
                    low("ssd", g + 1, 0)
                    low("ssd", g + 1, 1)
                    add_squares(g)

                with pool.Fori(0, GROUPS - 1) as g:
                    group(g, True)
                group(GROUPS - 1, False)

                def bias_tiles(hp):
                    return BM.rearrange("p q h k -> p q (h k)"), bias_dram[hp].rearrange("q p h k -> p q (h k)")

                wait_alone(pool, r_ok, l, 1)
                pool.wait_ge(bias_out, 16 * 16)
                dst, src = bias_tiles(0)
                pool.dma_start(dst, src).then_inc(bm_in.sem, 16)

                def pair(hp, more):
                    for j in range(2, 9):
                        low("att", hp, j)
                    low("att", hp + 1, 0)
                    low("att", hp + 1, 1)
                    if more:
                        dst, src = bias_tiles(hp + 1)
                        pool.compute_val(src.offset)
                        wait_alone(pool, s_v, l, hp * 8 + 8)
                        pool.dma_start(dst, src).then_inc(bm_in.sem, 16)

                with pool.Fori(0, 3) as hp:
                    pair(hp, True)
                pair(3, False)
                with pool.Fori(0, 8) as c:
                    low("mrg", c, 2)
                    low("mrg", c, 3)
                    low("mrg", c + 1, 0)
                    low("mrg", c + 1, 1)
                for j in range(2, 8):
                    low("out", 0, j)
                with pool.Fori(0, PH // 2) as h2:
                    for n in range(6):
                        low("qry", h2, n)
                with pool.Fori(0, BLOCKS) as b:
                    for n in range(2):
                        low("pre", b, n)
                with pool.Fori(0, BLOCKS // 2) as b2:
                    for n in range(8):
                        low("val", b2, n)
                with pool.Fori(0, (STRIPES - 1) * BLOCKS) as blk:
                    for n in SPLIT_PEER:
                        low("peer", blk, n)
                src = par[l + 1]
                pool.compute_val(src.offset)
                wait_alone(pool, v_mm, l, 256)
                pool.dma_start(pr[:, :], src).then_inc(par_in.sem, 16)
            pool.wait_ge(par_in.sem, 16 * (DEPTH + 1))
            pool.wait_ge(v_add.sem, v_add.at(DEPTH, 0))
            pool.dma_start(wfin, w_final.partition_broadcast(P)).then_inc(f_w, 16)
            pool.wait_ge(f_w, 16)

        @block.tensor
        def _(pe):
            pe.sem_inc(slot_free.sem, CREDIT - 1)
            pe.wait_ge(cst_in, 16)
            pe.wait_ge(rel_in, 48)
            pe.matmul(pb(0)[0:NG * 8, :], rel_w[0:REL_BUCKETS], hot_rel[0:REL_BUCKETS], start=True, stop=True).then_inc(rel_mm, 1)

            def project(l, name, i, j, out, rhs, n=KD):
                loaded(pe, l, name, i, j)
                for k in range(n):
                    mm = pe.matmul(out, ring[j][:, k * P:(k + 1) * P], rhs[:, k, :], start=k == 0, stop=k == n - 1)
                    if k == 0:
                        mm.then_inc(slot_free.sem, 1)
                return mm

            def product3(out, a, b, start, stop):
                return [pe.matmul(out, a[p], b[q], start=start and n == 0, stop=stop and n == 2)
                        for n, (p, q) in enumerate(((0, 0), (0, 1), (1, 0)))]

            def project3(l, name, i, j, out, high=hT_hi, low=hT_lo, start=True, stop=True, k0=0, ks=range(KD)):
                slot, hi = places(name, j)
                if ks[0] == 0:
                    pe.wait_ge(w_lo.sem, w_lo.at(l, split_no(name, i, j) + 1))
                for k in ks:
                    cols = slice(k * P, (k + 1) * P)
                    mm = product3(out, (hi[:, cols], lo[slot][:, cols]), (high[:, k0 + k, :], low[:, k0 + k, :]),
                                  start and k == 0, stop and k == KD - 1)
                    if k == 0:
                        mm[0].then_inc(slot_free.sem, 1)
                return mm[-1]

            def norm(l, w):
                for tt in range(NT):
                    pe.wait_ge(n_xn.sem, n_xn.at(l, 4 * w + tt + 1))
                    if tt >= 2:
                        pe.wait_ge(hT_ok.sem, hT_ok.at(l, 8 * w + 2 * (tt - 1)))
                    for half in range(2):
                        out = pb(2 * (tt % 2) + half)
                        for k in range(4):
                            kk = 4 * half + k
                            mm = pe.transpose(out[:, k * P:(k + 1) * P], xn[tt % 2][:, kk * P:(kk + 1) * P], ident)
                        mm.then_inc(n_tr.sem, 1)

            with pe.Fori(0, DEPTH) as l:
                norm(l, 0)
                pe.wait_ge(hT_ok.sem, hT_ok.at(l, 8))
                pe.wait_ge(par_in.sem, par_in.at(l, 16))
                for tt in range(NT):
                    for k in range(KD):
                        mm = pe.matmul(pb(4)[:, tt * 64:(tt + 1) * 64], hT[:, k, tt * P:(tt + 1) * P],
                                       pr[:, PW_WDT + 64 * k:PW_WDT + 64 * (k + 1)], start=(k == 0), stop=(k == KD - 1))
                mm.then_inc(dt_mm.sem, 1)
                pe.wait_ge(dt_a.sem, dt_a.at(l, 1))
                for s in range(NSEQ):
                    for d, tri in ((0, le), (1, ge)):
                        first, second = (2 * s, 2 * s + 1) if d == 0 else (2 * s + 1, 2 * s)
                        cols = slice(32 * d, 32 * d + 32)
                        for tt, parts in ((first, [(tri, first)]), (second, [(ones, first), (tri, second)])):
                            for n, (m, src) in enumerate(parts):
                                pe.matmul(pb(5)[:, tt * 64 + 32 * d:tt * 64 + 32 * d + 32], m, da[:, src, cols],
                                          start=(n == 0), stop=(n == len(parts) - 1))
                            for n, (m, src) in enumerate(parts):
                                mm = pe.matmul(pb(6 + d)[0:32, tt * P:(tt + 1) * P], da[:, src, cols], m,
                                               start=(n == 0), stop=(n == len(parts) - 1))
                mm.then_inc(dt_cs.sem, 1)
                wait_alone(pe, dt_T, l, 3)

                wait_alone(pe, hl_ok, l, 8)
                with pe.Fori(0, GROUPS) as g:
                    for j in range(4):
                        if j == 2:
                            pe.wait_ge(y_v.sem, y_v.at(l, g * 2))
                        project3(l, "ssd", g, j, pb(j)).then_inc(c_mm.sem, 1)
                    pe.wait_ge(c_s.sem, c_s.at(l, g * 4 + 2))
                    for s in range(NSEQ):
                        for si in range(2):
                            mm = pe.matmul(pb(s)[:, si * SEQ:(si + 1) * SEQ],
                                           cx[0][:, s * SEQ + si * P:s * SEQ + (si + 1) * P],
                                           cx[1][:, s * SEQ:(s + 1) * SEQ], start=True, stop=True)
                        mm.then_inc(cb_mm.sem, 1)
                    for i in range(2):
                        pe.wait_ge(z_s.sem, z_s.at(l, g * 2 + i - 1))
                        project3(l, "ssd", g, 4 + i, pb(4 + i)).then_inc(z_mm.sem, 1)
                        if i == 1:
                            continue
                        for t in range(2):
                            pe.wait_ge(c_s.sem, c_s.at(l, g * 4 + (3 + t)))
                            for tt in range(NT):
                                mm = pe.transpose(pb(6 + t)[:, tt * P:(tt + 1) * P],
                                                  cx[2 + t][:, tt * P:(tt + 1) * P], ident)
                            mm.then_inc(xt_mm.sem, 1)
                    pe.wait_ge(xd_ok.sem, xd_ok.at(l, g * 2 + 2))
                    for n in range(8):
                        r, s = 2 * (n // 4) + (n % 4) // 2, n % 2
                        pe.wait_ge(m_ok.sem, m_ok.at(l, g * 8 + (n + 1)))
                        out = pb(2 + r // 2)[64 * (r % 2):64 * (r % 2) + 64, :]
                        o = s * SEQ
                        xs = slice(r * HD, (r + 1) * HD)
                        parts = [(0, 0, 0, 256, 0), (1, 1, 256, 256, 0), (1, 0, 512, 128, 0), (0, 1, 640, 128, 128)]
                        for q, (d, si, c0, w, l0) in enumerate(parts):
                            mm = pe.matmul(out[:, o + l0:o + l0 + w], xdt[d][:, 2 * s + si, xs],
                                           E[:, n, c0:c0 + w], start=(q == 0), stop=(q == 3))
                        if n % 4 == 3:
                            mm.then_inc(y_mm.sem, 1)
                pe.wait_ge(sq_sum.sem, sq_sum.at(l, 1 + 2 * GROUPS))
                pe.wait_ge(z_s.sem, z_s.at(l, 2 * GROUPS))
                pe.matmul(pb(4), ones, sqsum, start=True, stop=True).then_inc(r_mm.sem, 1)
                wait_alone(pe, y_v, l, 2 * GROUPS)
                wait_alone(pe, r_ok, l, 1)

                with pe.Fori(0, 4) as hp:
                    pe.wait_ge(o_ok.sem, o_ok.at(l, hp))
                    for u in range(6):
                        if u >= 4:
                            if u % 2 == 0:
                                pe.wait_ge(p_evA.sem, p_evA.at(l, hp * 5 + 1))
                            else:
                                pe.wait_ge(p_evV.sem, p_evV.at(l, hp * 4 + 1))
                        project3(l, "att", hp, u, pb(u % 4)).then_inc(p_mm.sem, 1)
                    pe.wait_ge(p_evA.sem, p_evA.at(l, hp * 5 + 3))
                    pe.wait_ge(p_evV.sem, p_evV.at(l, hp * 4 + 3))
                    for c in range(8):
                        j, s, qt = c // 4, (c // 2) % 2, c % 2
                        if c >= 2:
                            pe.wait_ge(s_v.sem, s_v.at(l, hp * 8 + (c - 1)))
                        hd = slice(64 * j, 64 * j + 64)
                        for g in range(NG):
                            mm = pe.matmul(pb(2 * (c % 2) + g // 2)[:, (g % 2) * SEQ:(g % 2 + 1) * SEQ],
                                           qk[2 * g][hd, s * SEQ + qt * P:s * SEQ + (qt + 1) * P],
                                           qk[2 * g + 1][hd, s * SEQ:(s + 1) * SEQ], start=True, stop=True)
                        mm.then_inc(s_mm.sem, 1)
                        if c % 2 and c < 6:
                            project3(l, "att", hp, 6 + c // 2, pb(4 + c // 2)).then_inc(p_mm.sem, 1)
                    pe.wait_ge(p_evA.sem, p_evA.at(l, hp * 5 + 5))
                    pe.wait_ge(p_evV.sem, p_evV.at(l, hp * 4 + 4))
                    for g in range(NG):
                        for tt in range(NT):
                            mm = pe.transpose(pb(4 + g)[:, tt * P:(tt + 1) * P], vraw[g][:, tt * P:(tt + 1) * P], ident)
                        mm.then_inc(vt_mm.sem, 1)
                    pe.wait_ge(vt_ok.sem, vt_ok.at(l, hp * 3 + 3))

                    def values(js):
                        j, s = js // 2, js % 2
                        pe.wait_ge(t_evA.sem, t_evA.at(l, hp * 6 + (3 * js + 4) // 2))
                        pe.wait_ge(t_evV.sem, t_evV.at(l, hp * 6 + (3 * js + 3) // 2))
                        for q in range(6):
                            g, kt = q // 2, q % 2
                            mm = pe.matmul(pb(0)[64 * j:64 * j + 64, s * SEQ:(s + 1) * SEQ],
                                           vtok[g][:, 2 * s + kt, 64 * j:64 * j + 64],
                                           PTt[js % 2][:, q * SEQ:(q + 1) * SEQ], start=(q == 0), stop=(q == 5))
                        mm.then_inc(o_mm.sem, 1)

                    for n in range(12):
                        js, m = n // 3, n % 3
                        if m == 0:
                            pe.wait_ge(p_f.sem, p_f.at(l, hp * 8 + (2 * js + 2)))
                        if n >= 4:
                            if n % 2 == 0:
                                pe.wait_ge(t_evA.sem, t_evA.at(l, hp * 6 + (n - 4) // 2 + 1))
                            else:
                                pe.wait_ge(t_evV.sem, t_evV.at(l, hp * 6 + (n - 4) // 2 + 1))
                        for q in range(4):
                            gk, qt = 2 * m + q // 2, q % 2
                            g, kt = gk // 2, gk % 2
                            mm = pe.transpose(pb(4 + n % 4)[:, q * P:(q + 1) * P],
                                              Pm[:, 2 * js + qt, g, kt * P:(kt + 1) * P], ident)
                        mm.then_inc(t_mm.sem, 1)
                        if m == 1 and js:
                            values(js - 1)
                    values(3)

                pe.wait_ge(y_ok.sem, y_ok.at(l, 2 * GROUPS))
                wait_alone(pe, o_ok, l, 4)
                with pe.Fori(0, 4) as c2:
                    for h in range(2):
                        c, b = c2 * 2 + h, 4 * h
                        pe.wait_ge(mT_ok.sem, mT_ok.at(l, c - 1))
                        project3(l, "mrg", c, 0, pb(b)).then_inc(ga_mm.sem, 1)
                        project3(l, "mrg", c, 1, pb(b + 1)).then_inc(gb_mm.sem, 1)
                        pe.wait_ge(yl_ok.sem, yl_ok.at(l, 8))
                        project3(l, "mrg", c, 2, pb(b + 2), y_hi, y_lo, stop=False)
                        pe.wait_ge(yl_ok.sem, yl_ok.at(l, 16))
                        project3(l, "mrg", c, 3, pb(b + 2), y_hi, y_lo, start=False, k0=8).then_inc(pa_mm.sem, 1)
                        project(l, "mrg", c, 4, pb(b + 3), oT, n=4).then_inc(pb_mm.sem, 1)

                for k in range(KD):
                    pe.wait_ge(ml_ok.sem, ml_ok.at(l, k + 1))
                    pe.wait_ge(w_lo.sem, w_lo.at(l, split_no("out", 0, k) + 1))
                    slot, hi = places("out", k)
                    for n in range(8):
                        tok, cols = slice(n // 2 * P, (n // 2 + 1) * P), slice(n % 2 * 512, (n % 2 + 1) * 512)
                        mm = product3(pb(n), (m_hi[:, k, tok], m_lo[:, k, tok]), (hi[:, cols], lo[slot][:, cols]),
                                      k == 0, k == KD - 1)
                        if n == 0:
                            mm[0].then_inc(slot_free.sem, 1)
                        if k == KD - 1:
                            mm[-1].then_inc(out_mm.sem, 1)
                pe.wait_ge(x_mid.sem, x_mid.at(l, 8))

                norm(l, 1)
                wait_alone(pe, hl_ok, l, 16)
                with pe.Fori(0, PH // 2) as h2:
                    for hh in range(2):
                        for s in range(2):
                            if s == 0:
                                pe.wait_ge(hid_ok.sem, hid_ok.at(l, h2 * 2 + hh - 1))
                            project3(l, "qry", h2, 3 * hh + s, pb(2 * hh + s)).then_inc(q_mm.sem, 1)
                        pe.wait_ge(q_sv.sem, q_sv.at(l, h2 * 4 + 2 * hh - 2))
                        for s in range(2):
                            pe.wait_ge(q_ev.sem, q_ev.at(l, h2 * 4 + (2 * hh + s + 1)))
                            for tt in range(NT):
                                mm = pe.matmul(pb(4 + 2 * hh + s)[:, tt * P:(tt + 1) * P],
                                               qT[2 * hh + s][:, tt * P:(tt + 1) * P],
                                               pr[:, PW_KEYS + s * P:PW_KEYS + (s + 1) * P], start=True, stop=True)
                            mm.then_inc(q_s.sem, 1)
                        project3(l, "qry", h2, 3 * hh + 2, pb(2 * hh)).then_inc(h0_mm.sem, 1)
                pe.wait_ge(hid_ok.sem, hid_ok.at(l, 8))
                pe.wait_ge(g_ok.sem, g_ok.at(l, 1))
                for n, src in enumerate((ID[:, 0], ID[:, 1], Ge)):
                    for tt in range(NT):
                        mm = pe.transpose(pb(n)[:, tt * P:(tt + 1) * P], src[:, tt].rearrange("p h k -> p (h k)"), ident)
                    mm.then_inc(gt_mm.sem, 1)
                wait_alone(pe, gt_ok, l, 7)

                def outer(l, base, c):
                    pe.wait_ge(h_ok.sem, h_ok.at(l, base + (c + 1)))
                    for t in range(16):
                        mm = pe.matmul(routes[:, 2 * (c % 2) + t // 8, 64 * (t % 8):64 * (t % 8) + 48],
                                       Bh[c % 2][:, :, t], A3[c % 2][:, :, :, t], start=True, stop=True)
                    mm.then_inc(h_mm.sem, 1)

                with pe.Fori(0, BLOCKS) as b:
                    for c in range(8):
                        outer(l, b * 8, c)
                        if c < 2:
                            continue
                        n, third = (c - 2) // 3, (c - 2) % 3
                        if third == 0:
                            pe.wait_ge(hid_ok.sem, hid_ok.at(l, b * 2 + (7 + n)))
                        mm = project3(l, "pre", b, n, pb(n), ks=range(3 * third, min(3 * third + 3, KD)))
                        if third == 2:
                            mm.then_inc(h0_mm.sem, 1)
                def values(n, j, name, j0):
                    slot, hi = places(name, j0 + j)
                    tt, nh = n // 2, n % 2
                    tok, cols = slice(tt * P, (tt + 1) * P), slice(nh * 512, (nh + 1) * 512)
                    return product3(pb(2 + n % 2), (gh_h[j][:, tok], gh_l[j][:, tok]),
                                    (hi[:, cols], lo[slot][:, cols]), j == 0, j == 3)

                def block_values(name, i, j0, blk, after, first=lambda n: None):
                    first(0)
                    for n in range(2):
                        pe.wait_ge(v_add.sem, v_add.at(l, blk * 8 + n - 1))
                        for j in range(3):
                            if n == 0:
                                pe.wait_ge(w_lo.sem, w_lo.at(l, split_no(name, i, j0 + j) + 1))
                                pe.wait_ge(gh_ok.sem, gh_ok.at(l, blk * 4 + (j + 1)))
                            mm = values(n, j, name, j0)
                            if n == 0 and j == 0:
                                mm[0].then_inc(slot_free.sem, 1)
                    first(1)
                    pe.wait_ge(w_lo.sem, w_lo.at(l, split_no(name, i, j0 + 3) + 1))
                    pe.wait_ge(gh_ok.sem, gh_ok.at(l, blk * 4 + 4))
                    for n in range(8):
                        if n < 2:
                            mm = values(n, 3, name, j0)
                        else:
                            pe.wait_ge(v_add.sem, v_add.at(l, blk * 8 + n - 1))
                            for j in range(4):
                                mm = values(n, j, name, j0)
                                if n == 7 and j < 3:
                                    mm[-1].then_inc(slot_free.sem, 1)
                        mm[-1].then_inc(v_mm.sem, 1)
                        after(n)

                with pe.Fori(0, BLOCKS // 2) as b2:
                    for odd in range(2):
                        b = b2 * 2 + odd
                        chunk = lambda n: outer(l, b * 8 + BLOCKS * 8, n)
                        block_values("val", b2, 4 * odd, b, lambda n: chunk(n + 1) if 1 <= n < 7 else None, chunk)

                def block(blk, more):
                    base = blk * 8 + BLOCKS * 8
                    i = blk - BLOCKS
                    for j in range(4):
                        pe.wait_ge(u_ge.sem, u_ge.at(l, i * 4 + j - 1))
                        project3(l, "peer", i, j, pb(j % 2)).then_inc(u_mm.sem, 1)
                        if more:
                            outer(l, base, j)
                    block_values("peer", i, 4, blk, lambda n: outer(l, base, 4 + n // 2) if more and n % 2 else None)

                with pe.Fori(BLOCKS, (STRIPES - 1) * BLOCKS) as blk:
                    block(blk, True)
                with pe.Fori((STRIPES - 1) * BLOCKS, STRIPES * BLOCKS) as blk:
                    block(blk, False)

        @block.scalar
        def _(act):
            act.dma_start(rel_w[0:REL_BUCKETS], rel).then_inc(rel_in, 16)
            act.dma_start(hot_rel[0:REL_BUCKETS], biases[0:32]).then_inc(rel_in, 16)
            act.dma_start(mask_rel[0:NG * 8], biases[32:56]).then_inc(rel_in, 16)
            act.wait_ge(rel_in, 48)

            def norm(l, w):
                if w == 0:
                    act.wait_ge(v_add.sem, v_add.at(l, 0))
                for tt in range(NT):
                    if w:
                        act.wait_ge(x_mid.sem, x_mid.at(l, 2 * tt + 2))
                    if tt:
                        act.wait_ge(n_ss.sem, n_ss.at(l, 4 * w + tt))
                    act.activation(junk, x[:, tt, :], ACT.Square, accum_out=stat[:, tt:tt + 1]).then_inc(n_ss.sem, 1)
                act.wait_ge(n_ms.sem, n_ms.at(l, w + 1))
                act.activation(stat[:, 8:12], stat[:, 4:8], ACT.Sqrt).then_inc(n_sqrt.sem, 1)
                for n in range(8):
                    act.wait_ge(hT_ok.sem, hT_ok.at(l, 8 * w + (n + 1)))
                    act.activation(h_piece(hT_hi, n), h_piece(hT, n), ACT.Copy).then_inc(hh_ok.sem, 1)

            act.wait_ge(x_in, 32)
            with act.Fori(0, DEPTH) as l:
                def high(name, i, j):
                    slot, hi = places(name, j)
                    loaded(act, l, name, i, j)
                    act.activation(hi[:, :], ring[slot][:, :], ACT.Copy).then_inc(w_hi.sem, 1)

                norm(l, 0)
                high("ssd", 0, 0)
                high("ssd", 0, 1)
                act.wait_ge(par_in.sem, par_in.at(l, 16))
                act.activation(aexp, pr[:, PW_ALOG:PW_ALOG + 64], ACT.Exp).then_inc(dt_u.sem, 1)
                act.wait_ge(dt_ax.sem, dt_ax.at(l, 1))
                act.activation(du, dax, ACT.Exp, scale=-1.0).then_inc(dt_u.sem, 1)
                act.wait_ge(dt_w.sem, dt_w.at(l, 1))
                act.activation(dln, dw, ACT.Ln).then_inc(dt_ln.sem, 1)

                with act.Fori(0, GROUPS) as g:
                    def decay(n):
                        act.wait_ge(arg.sem, arg.at(l, g * 8 + (n + 1)))
                        act.activation(E[:, n, :], E[:, n, :], ACT.Exp).then_inc(ex.sem, 1)

                    def centre(j):
                        act.wait_ge(c_mm.sem, c_mm.at(l, g * 4 + (j + 1)))
                        act.activation(cx[j], pb(j), ACT.Identity, bias=gp[:, 8 * j + 5:8 * j + 6],
                                       scale=gp[:, 8 * j + 2:8 * j + 3]).then_inc(c_acc.sem, 1)

                    def silu(j):
                        act.wait_ge(c_ok.sem, c_ok.at(l, g * 4 + (j + 1)))
                        act.activation(cx[j], cx[j], ACT.Silu).then_inc(c_s.sem, 1)

                    def silu_z(i):
                        act.wait_ge(z_mm.sem, z_mm.at(l, g * 2 + (i + 1)))
                        act.activation(zs[i], pb(4 + i), ACT.Silu).then_inc(z_s.sem, 1)

                    act.wait_ge(g_cp.sem, g_cp.at(l, g * 3 + 3))
                    centre(0)
                    high("ssd", g, 2)
                    for n in range(4):
                        decay(n)
                    centre(1)
                    high("ssd", g, 3)
                    for n in range(4, 8):
                        decay(n)
                    silu(0)
                    centre(2)
                    high("ssd", g, 4)
                    silu(1)
                    centre(3)
                    high("ssd", g, 5)
                    silu(2)
                    silu(3)
                    silu_z(0)
                    high("ssd", g + 1, 0)
                    for i in range(2):
                        act.wait_ge(xt_mm.sem, xt_mm.at(l, g * 2 + (i + 1)))
                        act.activation(xtok[:, :, i * P:(i + 1) * P], pb(6 + i).rearrange("p (t c) -> p t c", t=NT),
                                       ACT.Copy).then_inc(xt_ok.sem, 1)
                    silu_z(1)
                    high("ssd", g + 1, 1)
                    for i in range(2):
                        act.wait_ge(y3_ok.sem, y3_ok.at(l, g * 2 + (i + 1)))
                        act.wait_ge(sq_sum.sem, sq_sum.at(l, g * 2 + i))
                        act.activation(sq[i], y3[i], ACT.Square).then_inc(sq_ok.sem, 1)
                        act.activation(yT[:, g * 2 + i, :], y3[i], ACT.Copy,
                                       scale=gp[:, 8 * (2 + i) + 7:8 * (2 + i) + 8]).then_inc(y_ok.sem, 1)
                act.wait_ge(r_ms.sem, r_ms.at(l, 1))
                act.activation(sqsum, sqsum, ACT.Sqrt).then_inc(r_sq.sem, 1)
                wait_alone(act, r_ok, l, 1)

                with act.Fori(0, 4) as hp:
                    def leave(u):
                        act.wait_ge(p_mm.sem, p_mm.at(l, hp * 9 + (u + 1)))
                        dst, src = (qk[u], pb(u % 4)) if u < 6 else (vraw[u - 6], pb(u - 2))
                        act.activation(dst, src, ACT.Copy, scale=HD ** -0.5 if u < 6 else 1.0).then_inc(p_evA.sem, 1)

                    def probabilities(c):
                        act.wait_ge(s_nm.sem, s_nm.at(l, hp * 8 + (c + 1)))
                        for g in range(NG):
                            ins = act.activation(Pm[:, c, g, :], Pm[:, c, g, :], ACT.Exp, bias=nm[:, c, g:g + 1],
                                                 accum_out=den[:, c, g:g + 1])
                        ins.then_inc(p_x.sem, 1)

                    for u in range(6):
                        if u % 2 == 0:
                            leave(u)
                        else:
                            act.wait_ge(p_mm.sem, p_mm.at(l, hp * 9 + (u + 1)))
                        high("att", hp, u + 2)
                    probabilities(0)
                    probabilities(1)
                    leave(6)
                    high("att", hp, 8)
                    for c in range(2, 6):
                        probabilities(c)
                    leave(8)
                    high("att", hp + 1, 0)
                    high("att", hp + 1, 1)
                    probabilities(6)
                    probabilities(7)
                    for g in range(NG):
                        act.wait_ge(vt_mm.sem, vt_mm.at(l, hp * 3 + (g + 1)))
                        act.activation(vtok[g], pb(4 + g).rearrange("p (t c) -> p t c", t=NT),
                                       ACT.Copy).then_inc(vt_ok.sem, 1)
                    act.wait_ge(a_v.sem, a_v.at(l, hp * 6 + 2))
                    act.activation(wg, wg, ACT.Exp).then_inc(a_w.sem, 1)
                    for n in range(0, 12, 2):
                        act.wait_ge(t_mm.sem, t_mm.at(l, hp * 12 + (n + 1)))
                        js, m = n // 3, n % 3
                        if js >= 2:
                            act.wait_ge(o_mm.sem, o_mm.at(l, hp * 4 + js - 1))
                        act.activation(PTt[js % 2][:, m * 512:(m + 1) * 512], pb(4 + n % 4), ACT.Copy).then_inc(t_evA.sem, 1)
                    act.wait_ge(o_mm.sem, o_mm.at(l, hp * 4 + 4))
                    act.activation(oT[:, hp, :], pb(0), ACT.Copy).then_inc(o_ok.sem, 1)
                for k in range(16):
                    act.activation(y_hi[:, k, :], yT[:, k, :], ACT.Copy).then_inc(yh_ok.sem, 1)

                with act.Fori(0, 4) as c2:
                    for h in range(2):
                        c, b = c2 * 2 + h, 4 * h
                        act.wait_ge(mT_ok.sem, mT_ok.at(l, c - 1))
                        act.wait_ge(ga_mm.sem, ga_mm.at(l, c + 1))
                        act.activation(sg[2 * h], pb(b), ACT.Sigmoid).then_inc(sg_ok.sem, 1)
                        high("mrg", c, 2)
                        act.wait_ge(gb_mm.sem, gb_mm.at(l, c + 1))
                        act.activation(sg[2 * h + 1], pb(b + 1), ACT.Sigmoid).then_inc(sg_ok.sem, 1)
                        high("mrg", c, 3)
                        for j in range(2):
                            act.wait_ge(slot_free.sem, slot_free.at(l, c * 5 + (BASE["mrg"] + 3 + j)))
                            high("mrg", c + 1, j)
                act.wait_ge(mT_ok.sem, mT_ok.at(l, 8))
                for k in range(KD):
                    act.activation(m_hi[:, k, :], mT[:, k, :], ACT.Copy).then_inc(mh_ok.sem, 1)
                for j in range(2, 8):
                    act.wait_ge(slot_free.sem, slot_free.at(l, BASE["out"] + j - 1))
                    high("out", 0, j)

                norm(l, 1)
                with act.Fori(0, PH // 2) as h2:
                    def high_q(n):
                        high("qry", h2, n)

                    def query(n):
                        act.wait_ge(q_mm.sem, q_mm.at(l, h2 * 4 + (n + 1)))
                        act.activation(qT[n], pb(n), ACT.Copy).then_inc(q_ev.sem, 1)

                    def hid(n):
                        act.wait_ge(h0_mm.sem, h0_mm.at(l, h2 * 2 + (n + 1)))
                        act.activation(yT[:, h2 * 2 + n, :], pb(2 * n), ACT.Gelu).then_inc(hid_ok.sem, 1)

                    def scores(hh):
                        act.wait_ge(k_done.sem, k_done.at(l, h2 * 2 + hh - 1))
                        for s in range(2):
                            act.wait_ge(q_s.sem, q_s.at(l, h2 * 4 + (2 * hh + s + 1)))
                            act.activation(sc[hh][:, s], pb(4 + 2 * hh + s).rearrange("p (t n) -> p t n", t=NT),
                                           ACT.Copy).then_inc(q_sv.sem, 1)

                    high_q(0)
                    high_q(1)
                    query(0)
                    high_q(2)
                    query(1)
                    high_q(3)
                    hid(0)
                    high_q(4)
                    scores(0)
                    query(2)
                    high_q(5)
                    query(3)
                    hid(1)
                    scores(1)
                act.wait_ge(g_v.sem, g_v.at(l, 1))
                act.activation(Ge, Ge, ACT.Exp).then_inc(g_e.sem, 1)
                act.wait_ge(gt_mm.sem, gt_mm.at(l, 3))

                with act.Fori(0, BLOCKS) as b:
                    high("pre", b, 0)
                    high("pre", b, 1)
                    for n in range(2):
                        act.wait_ge(h0_mm.sem, h0_mm.at(l, b * 2 + (9 + n)))
                        act.activation(yT[:, b * 2 + (8 + n), :], pb(n), ACT.Gelu).then_inc(hid_ok.sem, 1)

                high("val", 0, 0)
                high("val", 0, 1)
                for b in range(BLOCKS):
                    act.wait_ge(v_add.sem, v_add.at(l, b * 8))
                    for j in range(4):
                        act.wait_ge(gh0_m.sem, gh0_m.at(l, b * 4 + (j + 1)))
                        act.activation(gh_h[j][:, :], Gs[1][:, b * 4 + j, :], ACT.Copy).then_inc(gh_hi.sem, 1)
                    for j in range(2, 4):
                        high("val", b // 2, b % 2 * 4 + j)
                    if b < BLOCKS - 1:
                        for j in range(2):
                            high("val", (b + 1) // 2, (b + 1) % 2 * 4 + j)
                wait_alone(act, v_add, l, BLOCKS * 8)

                with act.Fori(0, (STRIPES - 1) * BLOCKS) as blk:
                    def high_p(n):
                        high("peer", blk, n)

                    def gelu(j):
                        act.wait_ge(u_mm.sem, u_mm.at(l, blk * 4 + (j + 1)))
                        act.activation(gh[j], pb(j % 2), ACT.Gelu).then_inc(u_ge.sem, 1)

                    def routed_high(j):
                        act.wait_ge(gh_m.sem, gh_m.at(l, blk * 4 + (j + 1)))
                        act.activation(gh_h[j][:, :], gh[j], ACT.Copy).then_inc(gh_hi.sem, 1)

                    high_p(0)
                    high_p(1)
                    gelu(0)
                    high_p(2)
                    high_p(4)
                    gelu(1)
                    high_p(3)
                    routed_high(0)
                    high_p(5)
                    gelu(2)
                    routed_high(1)
                    high_p(6)
                    high_p(7)
                    routed_high(2)
                    gelu(3)
                    routed_high(3)

            for tt in range(NT):
                act.wait_ge(v_add.sem, v_add.at(DEPTH, 2 * tt + 2 - 8))
                if tt:
                    act.wait_ge(f_ss, tt)
                act.activation(fjunk, x[:, tt, :], ACT.Square, accum_out=stat[:, tt:tt + 1]).then_inc(f_ss, 1)
            act.wait_ge(f_v, 1)
            act.activation(stat[:, 8:12], stat[:, 4:8], ACT.Sqrt).then_inc(f_sq, 1)

        @block.vector
        def _(v):
            v.sem_inc(z_s.sem, 2)
            v.sem_inc(y_v.sem, 2)
            v.sem_inc(y_ok.sem, 2)
            v.sem_inc(sq_sum.sem, 2)
            v.sem_inc(o_ok.sem, 1)
            v.sem_inc(mT_ok.sem, 2)
            v.sem_inc(k_done.sem, 2)
            v.sem_inc(u_ge.sem, 2)
            v.sem_inc(hid_ok.sem, 4)
            v.sem_inc(q_sv.sem, 4)
            v.wait_ge(cst_in, 16)
            v.tensor_copy(iota16[:, :], cst[:, C_I16:C_I16 + 16])
            v.tensor_copy(iota_b[:, :, :], spread(cst[:, C_IOTA:C_IOTA + 144], 2, 16)).then_inc(iota_ok, 1)
            v.wait_ge(rel_in, 48)
            v.wait_ge(rel_mm, 1)
            v.tensor_tensor(oT[0:NG * 8, 0, :], pb(0)[0:NG * 8, :], mask_rel[0:NG * 8], ALU.add).then_inc(row_ok, 1)
            v.wait_ge(iota_ok, 1)
            v.wait_ge(row_out, 16)
            v.wait_ge(x_in, 32)
            v.memset(stat[:, 60:61], 0.0).then_inc(v_add.sem, 2)

            def norm(l, w):
                v.wait_ge(n_ss.sem, n_ss.at(l, 4 * w + 4))
                v.tensor_scalar(stat[:, 4:8], stat[:, 0:4], 1.0 / D, EPS, ALU.mult, ALU.add).then_inc(n_ms.sem, 1)
                v.wait_ge(n_sqrt.sem, n_sqrt.at(l, w + 1))
                v.reciprocal(stat[:, 12:16], stat[:, 8:12]).then_inc(n_rs.sem, 1)
                v.wait_ge(n_rs.sem, n_rs.at(l, w + 1))
                v.wait_ge(par_in.sem, par_in.at(l, 16))

                def scale(tt):
                    if tt >= 2:
                        v.wait_ge(n_tr.sem, n_tr.at(l, 8 * w + 2 * (tt - 1)))
                    v.tensor_scalar(xn[tt % 2], x[:, tt, :], stat[:, 12 + tt:13 + tt], None, ALU.mult).then_inc(n_xn.sem, 1)

                def store(tt):
                    for half in range(2):
                        v.wait_ge(n_tr.sem, n_tr.at(l, 8 * w + 2 * tt + half + 1))
                        o = (PW_N1, PW_N2)[w] + 4 * half
                        v.tensor_tensor(hT[:, 4 * half:4 * half + 4, tt * P:(tt + 1) * P],
                                        pb(2 * (tt % 2) + half).rearrange("p (k t) -> p k t", k=4),
                                        spread(pr[:, o:o + 4], 2, P), ALU.mult).then_inc(hT_ok.sem, 1)

                scale(0)
                scale(1)
                store(0)
                scale(2)
                store(1)
                scale(3)
                store(2)
                store(3)

            def low_h(l, w):
                for n in range(8):
                    v.wait_ge(hh_ok.sem, hh_ok.at(l, 8 * w + n + 1))
                    v.tensor_tensor(h_piece(hT_lo, n), h_piece(hT, n), h_piece(hT_hi, n), ALU.subtract).then_inc(hl_ok.sem, 1)

            with v.Fori(0, DEPTH) as l:
                norm(l, 0)
                v.wait_ge(dt_mm.sem, dt_mm.at(l, 1))
                low_h(l, 0)
                step = [0]

                def link(ins):
                    step[0] += 1
                    ins.then_inc(dt_v.sem, 1)
                    v.wait_ge(dt_v.sem, dt_v.at(l, step[0]))

                link(v.tensor_tensor(dr0, pb(4)[:, 0:256].rearrange("p (t h) -> p t h", t=NT),
                                     spread(pr[:, PW_DTB:PW_DTB + 64], 1, NT), ALU.add))
                v.scalar_tensor_tensor(out=dax, in0=dr0, scalar=-1.0, in1=dr0, op0=ALU.mult, op1=ALU.max).then_inc(dt_ax.sem, 1)
                v.wait_ge(dt_u.sem, dt_u.at(l, 2))
                v.tensor_scalar(dw, du, 1.0, None, ALU.add).then_inc(dt_w.sem, 1)
                v.wait_ge(dt_w.sem, dt_w.at(l, 1))
                link(v.tensor_scalar(dd, dw, -1.0, None, ALU.add))
                link(v.tensor_scalar(dz, dd, 0.0, None, ALU.is_equal))
                link(v.tensor_tensor(dd, dd, dz, ALU.add))
                link(v.reciprocal(dd, dd))
                v.wait_ge(dt_ln.sem, dt_ln.at(l, 1))
                link(v.tensor_tensor(dd, dd, dln, ALU.mult))
                link(v.tensor_tensor(dd, dd, dz, ALU.add))
                link(v.tensor_tensor(dd, dd, du, ALU.mult))
                link(v.scalar_tensor_tensor(out=dtv, in0=dr0, scalar=0.0, in1=dd, op0=ALU.max, op1=ALU.add))
                v.scalar_tensor_tensor(out=da, in0=dtv, scalar=-1.0, in1=spread(aexp, 1, NT),
                                       op0=ALU.mult, op1=ALU.mult).then_inc(dt_a.sem, 1)
                v.wait_ge(dt_cs.sem, dt_cs.at(l, 1))
                v.tensor_scalar(negA, pb(5)[:, 0:256].rearrange("p (t h) -> p t h", t=NT), -1.0, None,
                                ALU.mult).then_inc(dt_T.sem, 1)
                for d in range(2):
                    v.tensor_copy(aT[0:32, d, :], pb(6 + d)[0:32, :]).then_inc(dt_T.sem, 1)
                wait_alone(v, dt_T, l, 3)

                with v.Fori(0, GROUPS) as g:
                    v.wait_ge(y_ok.sem, y_ok.at(l, g * 2))
                    v.tensor_copy(gneg, negA.rearrange("p t (d h) -> p t d h", d=2)[:, :, :, bass.ds(g * RH, RH)]).then_inc(g_cp.sem, 1)
                    v.tensor_copy(gdt, dtv.rearrange("p t (d h) -> p t d h", d=2)[:, :, :, bass.ds(g * RH, RH)]).then_inc(g_cp.sem, 1)
                    v.tensor_copy(gp, pr[:, bass.ds(g * 32 + PW_CONV, 32)]).then_inc(g_cp.sem, 1)
                    v.wait_ge(g_cp.sem, g_cp.at(l, g * 3 + 3))
                    v.wait_ge(bc_in.sem, bc_in.at(l, g * 16 + 16))
                    for n in range(8):
                        r, s = 2 * (n // 4) + (n % 4) // 2, n % 2
                        parts = [(0, 0, 0, 256, 0, C_MF), (1, 1, 256, 256, 0, C_MB), (1, 0, 512, 128, 0, C_MB + P),
                                 (0, 1, 640, 128, 128, C_MF)]
                        for d, si, c0, w, l0, m in parts:
                            ins = v.scalar_tensor_tensor(
                                out=E[:, n, c0:c0 + w], in0=aBC[:, d, r, s * SEQ + l0:s * SEQ + l0 + w],
                                scalar=gneg[:, 2 * s + si, d, r:r + 1], in1=cst[:, m:m + w], op0=ALU.add, op1=ALU.add)
                        ins.then_inc(arg.sem, 1)
                    for j in range(4):
                        v.wait_ge(c_acc.sem, c_acc.at(l, g * 4 + (j + 1)))
                        for q, k in enumerate((0, 1, 3, 4)):
                            o = k - CONV // 2
                            lo, w = max(0, -o), SEQ - abs(o)
                            acc = cx[j].rearrange("p (s t) -> p s t", s=NSEQ)[:, :, lo:lo + w]
                            src = pb(j).rearrange("p (s t) -> p s t", s=NSEQ)[:, :, lo + o:lo + o + w]
                            ins = v.scalar_tensor_tensor(out=acc, in0=src, scalar=gp[:, 8 * j + k:8 * j + k + 1], in1=acc,
                                                         op0=ALU.mult, op1=ALU.add)
                            if q < 3:
                                ins.then_inc(c_tap.sem, 1)
                                v.wait_ge(c_tap.sem, c_tap.at(l, g * 12 + (3 * j + q + 1)))
                            else:
                                ins.then_inc(c_ok.sem, 1)
                    for n in range(8):
                        s = n % 2
                        v.wait_ge(cb_mm.sem, cb_mm.at(l, g * 2 + 2))
                        v.wait_ge(ex.sem, ex.at(l, g * 8 + (n + 1)))
                        v.tensor_tensor(E[:, n, 0:512], E[:, n, 0:512], pb(s), ALU.mult)
                        two = pb(s)[:, 0:512].rearrange("p (a b) -> p a b", b=P)[:, 0:4:3, :]
                        v.tensor_tensor(E[:, n, 512:768].rearrange("p (a b) -> p a b", b=P),
                                        E[:, n, 512:768].rearrange("p (a b) -> p a b", b=P), two, ALU.mult).then_inc(m_ok.sem, 1)
                    v.wait_ge(xt_ok.sem, xt_ok.at(l, g * 2 + 2))
                    for d in range(2):
                        v.tensor_tensor(xdt[d].rearrange("p t (r e) -> p t r e", r=RH),
                                        xtok.rearrange("p t (r e) -> p t r e", r=RH),
                                        spread(gdt[:, :, d, :], 3, HD), ALU.mult).then_inc(xd_ok.sem, 1)
                    for i in range(2):
                        v.wait_ge(y_mm.sem, y_mm.at(l, g * 2 + (i + 1)))
                        q = 8 * (2 + i) + 6
                        v.scalar_tensor_tensor(out=y3[i], in0=cx[2 + i], scalar=gp[:, q:q + 1], in1=pb(2 + i),
                                               op0=ALU.mult, op1=ALU.add).then_inc(y_v.sem, 1)
                        v.wait_ge(y_v.sem, y_v.at(l, g * 2 + (i + 1)))
                        v.wait_ge(z_s.sem, z_s.at(l, g * 2 + (i + 1)))
                        v.tensor_tensor(y3[i], y3[i], zs[i], ALU.mult).then_inc(y3_ok.sem, 1)
                v.wait_ge(r_mm.sem, r_mm.at(l, 1))
                v.tensor_scalar(sqsum, pb(4), 1.0 / D_INNER, EPS, ALU.mult, ALU.add).then_inc(r_ms.sem, 1)
                v.wait_ge(r_sq.sem, r_sq.at(l, 1))
                v.wait_ge(y_ok.sem, y_ok.at(l, 2 * GROUPS))
                v.reciprocal(rstdB, sqsum).then_inc(r_ok.sem, 1)

                with v.Fori(0, 4) as hp:
                    for u in range(1, 6, 2):
                        v.wait_ge(p_mm.sem, p_mm.at(l, hp * 9 + (u + 1)))
                        v.tensor_copy(qk[u], pb(u % 4)).then_inc(p_evV.sem, 1)
                    v.wait_ge(bm_in.sem, bm_in.at(l, hp * 16 + 16))
                    for c in range(8):
                        j, qt = c // 4, c % 2
                        wait_alone(v, s_mm, l, hp * 8 + (c + 1))
                        for g in range(NG):
                            ins = v.tensor_tensor_reduce(
                                Pm[:, c, g, :], pb(2 * (c % 2) + g // 2)[:, (g % 2) * SEQ:(g % 2 + 1) * SEQ],
                                BM[:, qt, 3 * j + g, :], 1.0, -3e38, ALU.add, ALU.max, mx[:, c, g:g + 1])
                        ins.then_inc(s_v.sem, 1)
                        v.wait_ge(s_v.sem, s_v.at(l, hp * 8 + (c + 1)))
                        v.tensor_scalar(nm[:, c, :], mx[:, c, :], -1.0, None, ALU.mult).then_inc(s_nm.sem, 1)
                        if c == 3:
                            v.wait_ge(p_mm.sem, p_mm.at(l, hp * 9 + 8))
                            v.tensor_copy(vraw[1], pb(5)).then_inc(p_evV.sem, 1)
                    st = [0]

                    def link(ins):
                        st[0] += 1
                        ins.then_inc(a_v.sem, 1)
                        v.wait_ge(a_v.sem, a_v.at(l, hp * 6 + st[0]))

                    link(v.tensor_reduce(m1, mx, AX, ALU.max))
                    link(v.tensor_tensor(wg, mx, spread(m1, 2, NG), ALU.subtract))
                    v.wait_ge(a_w.sem, a_w.at(l, hp + 1))
                    v.wait_ge(p_x.sem, p_x.at(l, hp * 8 + 8))
                    link(v.tensor_tensor(fw, wg, den, ALU.mult))
                    link(v.tensor_reduce(s1, fw, AX, ALU.add))
                    link(v.reciprocal(r1, s1))
                    link(v.tensor_tensor(fw, wg, spread(r1, 2, NG), ALU.mult))
                    assert st[0] == 6
                    for c in range(8):
                        for g in range(NG):
                            ins = v.tensor_scalar(Pm[:, c, g, :], Pm[:, c, g, :], fw[:, c, g:g + 1], None, ALU.mult)
                        ins.then_inc(p_f.sem, 1)
                    for n in range(1, 12, 2):
                        v.wait_ge(t_mm.sem, t_mm.at(l, hp * 12 + (n + 1)))
                        js, m = n // 3, n % 3
                        if js >= 2:
                            v.wait_ge(o_mm.sem, o_mm.at(l, hp * 4 + js - 1))
                        v.tensor_copy(PTt[js % 2][:, m * 512:(m + 1) * 512], pb(4 + n % 4)).then_inc(t_evV.sem, 1)
                for k in range(16):
                    v.wait_ge(yh_ok.sem, yh_ok.at(l, k + 1))
                    v.tensor_tensor(y_lo[:, k, :], yT[:, k, :], y_hi[:, k, :], ALU.subtract).then_inc(yl_ok.sem, 1)

                with v.Fori(0, 4) as c2:
                    for h in range(2):
                        c, b = c2 * 2 + h, 4 * h
                        v.wait_ge(mT_ok.sem, mT_ok.at(l, c))
                        v.wait_ge(pa_mm.sem, pa_mm.at(l, c + 1))
                        v.tensor_tensor(t1, pb(b + 2), rstdB, ALU.mult).then_inc(m_v.sem, 1)
                        v.wait_ge(m_v.sem, m_v.at(l, c * 3 + 1))
                        v.wait_ge(sg_ok.sem, sg_ok.at(l, c * 2 + 2))
                        v.tensor_tensor(t1, t1, sg[2 * h], ALU.mult).then_inc(m_v.sem, 1)
                        v.wait_ge(pb_mm.sem, pb_mm.at(l, c + 1))
                        v.tensor_tensor(t2, pb(b + 3), sg[2 * h + 1], ALU.mult).then_inc(m_v.sem, 1)
                        v.wait_ge(m_v.sem, m_v.at(l, c * 3 + 3))
                        v.tensor_tensor(mT[:, c, :], t1, t2, ALU.add).then_inc(mT_ok.sem, 1)

                for k in range(KD):
                    v.wait_ge(mh_ok.sem, mh_ok.at(l, k + 1))
                    v.tensor_tensor(m_lo[:, k, :], mT[:, k, :], m_hi[:, k, :], ALU.subtract).then_inc(ml_ok.sem, 1)
                for n in range(8):
                    tt, nh = n // 2, n % 2
                    xo = x[:, tt, nh * 512:(nh + 1) * 512]
                    v.wait_ge(out_mm.sem, out_mm.at(l, n + 1))
                    v.tensor_tensor(xo, xo, pb(n), ALU.add).then_inc(x_mid.sem, 1)

                norm(l, 1)
                low_h(l, 1)
                with v.Fori(0, PH // 2) as h2:
                    for hh in range(2):
                        h = h2 * 2 + hh
                        st = [0]

                        def link(ins):
                            st[0] += 1
                            ins.then_inc(k_v.sem, 1)
                            wait_alone(v, k_v, l, h * TK + st[0])

                        def top16(src, tmp, val, idx, n):
                            for step in range(4):
                                for half in range(2):
                                    if step:
                                        wait_alone(v, k_v, l, h * TK + st[0] - 1)
                                    for i in range(half * n // 2, (half + 1) * n // 2):
                                        if step == 0:
                                            ins = v.max(val(i)[:, 0:8], src(i))
                                        elif step == 1:
                                            v.max_index(idx(i)[:, 0:8], val(i)[:, 0:8], src(i))
                                            ins = v.match_replace(out=tmp(i), in_to_replace=val(i)[:, 0:8], in_values=src(i),
                                                                  imm_value=-3e38)
                                        elif step == 2:
                                            ins = v.max(val(i)[:, 8:16], tmp(i))
                                        else:
                                            ins = v.max_index(idx(i)[:, 8:16], val(i)[:, 8:16], tmp(i))
                                    ins.then_inc(k_v.sem, 1)
                                    st[0] += 1
                            wait_alone(v, k_v, l, h * TK + st[0])

                        wait_alone(v, q_sv, l, h * 2 + 2)
                        top16(lambda i: sc[hh][:, i // NT, i % NT, :], lambda i: sc2[:, i // NT, i % NT, :],
                              lambda i: v16[:, i // NT, i % NT, :], lambda i: x16[:, i // NT, i % NT, :], 2 * NT)
                        v.tensor_copy(b16, x16)
                        wide = cand[:, :, 0:ROWS * TOPK].rearrange("p t (i j) -> p t i j", i=ROWS)
                        narrow = cand[:, :, ROWS * TOPK:].rearrange("p t (i j) -> p t i j", j=COLS)
                        v.tensor_tensor(wide, spread(v16[:, 0, :, 0:ROWS], 3, TOPK), spread(v16[:, 1], 2, ROWS), ALU.add)
                        link(v.tensor_tensor(narrow, spread(v16[:, 0, :, ROWS:], 3, COLS),
                                             spread(v16[:, 1, :, 0:COLS], 2, TOPK - ROWS), ALU.add))
                        top16(lambda i: cand[:, i, :], lambda i: cand2[:, i, :], lambda i: cvh[:, i, :],
                              lambda i: ci.rearrange("p (t k) -> p t k", t=NT)[:, i, :], NT)
                        v.tensor_scalar(pij[:, 0, :], ci, 4, None, ALU.logical_shift_right)
                        v.tensor_scalar(pij[:, 1, :], ci, 2, None, ALU.logical_shift_right)
                        v.tensor_scalar(pij[:, 2, :], ci, 15, None, ALU.bitwise_and)
                        link(v.tensor_scalar(pij[:, 3, :], ci, 12, None, ALU.bitwise_and))
                        link(v.tensor_copy(pf, pij))
                        v.scalar_tensor_tensor(out=ij[:, 0, :], in0=pf[:, 1, :], scalar=float(ROWS - ROWS * TOPK // COLS),
                                               in1=pf[:, 0, :], op0=ALU.add, op1=ALU.max)
                        link(v.scalar_tensor_tensor(out=over, in0=pf[:, 0, :], scalar=float(ROWS), in1=pf[:, 3, :],
                                                    op0=ALU.is_ge, op1=ALU.mult))
                        link(v.tensor_tensor(ij[:, 1, :], pf[:, 2, :], over, ALU.subtract))
                        flat = hot.rearrange("p t k j -> p (t k) j")
                        link(v.tensor_tensor(flat, spread(ij.rearrange("p q n -> p (q n)"), 2, 16),
                                             spread(iota16[:, :], 1, 2 * NT * TOPK), ALU.is_equal))
                        link(v.tensor_tensor(hot, hot, spread(b16.rearrange("p q t k -> p (q t) k"), 2, TOPK), ALU.mult))
                        v.tensor_reduce(idh.rearrange("p q n -> p (q n)"), flat, AX, ALU.add).then_inc(k_done.sem, 1)
                        assert st[0] == TK, st[0]
                        v.wait_ge(k_done.sem, k_done.at(l, h + 1))
                        v.tensor_copy(CV[:, :, h, :], cvh)
                        v.tensor_copy(ID.rearrange("p q t h k -> p (q t) h k")[:, :, h, :],
                                      idh.rearrange("p q (t k) -> p (q t) k", t=NT))
                v.wait_ge(k_done.sem, k_done.at(l, PH))
                flat = [a.rearrange("p t h k -> p (t h) k") for a in (CV, Ge)]
                v.memset(gsum, 0.0).then_inc(g_fence.sem, 1)
                v.wait_ge(g_fence.sem, g_fence.at(l, 1))
                v.tensor_tensor(flat[1], flat[0], spread(flat[0][:, :, 0], 2, TOPK), ALU.subtract).then_inc(g_v.sem, 1)
                v.wait_ge(g_e.sem, g_e.at(l, 1))
                v.tensor_reduce(gsum, flat[1], AX, ALU.add).then_inc(g_v.sem, 1)
                v.wait_ge(g_v.sem, g_v.at(l, 2))
                v.reciprocal(grec, gsum).then_inc(g_v.sem, 1)
                v.wait_ge(g_v.sem, g_v.at(l, 3))
                v.tensor_tensor(flat[1], flat[1], spread(grec, 2, TOPK), ALU.mult).then_inc(g_ok.sem, 1)
                for q in range(2):
                    v.wait_ge(gt_mm.sem, gt_mm.at(l, q + 1))
                    v.tensor_copy(idT[q], pb(q)).then_inc(gt_ok.sem, 1)
                v.wait_ge(gt_mm.sem, gt_mm.at(l, 3))
                v.tensor_copy(gP[:, 0, :], pb(2)).then_inc(gt_ok.sem, 1)
                v.wait_ge(gt_ok.sem, gt_ok.at(l, 3))
                v.tensor_tensor(gr[0], pb(2), gP[:, 0, :], ALU.subtract).then_inc(gt_ok.sem, 1)
                v.wait_ge(gt_ok.sem, gt_ok.at(l, 4))
                v.tensor_copy(gP[:, 1, :], gr[0]).then_inc(gt_ok.sem, 1)
                v.wait_ge(gt_ok.sem, gt_ok.at(l, 5))
                v.tensor_tensor(gr[1], gr[0], gP[:, 1, :], ALU.subtract).then_inc(gt_ok.sem, 1)
                v.wait_ge(gt_ok.sem, gt_ok.at(l, 6))
                v.tensor_copy(gP[:, 2, :], gr[1]).then_inc(gt_ok.sem, 1)
                wait_alone(v, gt_ok, l, 7)

                def one_hots(l, base, stripe, tok, c):
                    n0 = base + (c + 1)
                    o = tok + 16 * c
                    v.tensor_tensor(eq[c % 2], spread(idT[0][:, bass.ds(o, 16)], 1, 16),
                                    iota_b[:, bass.ds(stripe * 16, 16), :], ALU.is_equal).then_inc(h_eq.sem, 1)
                    v.tensor_tensor(Bh[c % 2], spread(idT[1][:, bass.ds(o, 16)], 1, P), iota_b[:, 0:P, :], ALU.is_equal)
                    v.wait_ge(h_eq.sem, h_eq.at(l, n0))
                    v.tensor_tensor(A3[c % 2], spread(eq[c % 2], 1, 3), spread(gP[:, :, bass.ds(o, 16)], 2, 16),
                                    ALU.mult).then_inc(h_ok.sem, 1)

                def collect(l, base, G, tok, c):
                    v.wait_ge(h_mm.sem, h_mm.at(l, base + (c + 1)))
                    src = routes[:, 2 * (c % 2):2 * (c % 2) + 2, :].rearrange("p a (t x) -> p (a t) x", x=64)
                    src = src[:, :, 0:48].rearrange("p t (q n) -> p n t q", q=3)
                    v.tensor_reduce(G[:, :, bass.ds(tok + 16 * c, 16)], src, AX, ALU.add).then_inc(G_ok.sem, 1)

                with v.Fori(0, BLOCKS) as b:
                    one_hots(l, b * 8, 0, b * P, 0)
                    for c in range(1, 8):
                        one_hots(l, b * 8, 0, b * P, c)
                        collect(l, b * 8, Gs[1], b * P, c - 1)
                    collect(l, b * 8, Gs[1], b * P, 7)
                v.wait_ge(hid_ok.sem, hid_ok.at(l, 16))
                v.wait_ge(G_ok.sem, G_ok.at(l, 8 * BLOCKS))
                for t in range(16):
                    v.tensor_tensor(Gs[1][:, t, :], Gs[1][:, t, :], yT[:, t, :], ALU.mult).then_inc(gh0_m.sem, 1)

                def add_values(blk, n):
                    xo = x[:, n // 2, n % 2 * 512:(n % 2 + 1) * 512]
                    v.wait_ge(v_mm.sem, v_mm.at(l, blk * 8 + (n + 1)))
                    v.tensor_tensor(xo, xo, pb(2 + n % 2), ALU.add).then_inc(v_add.sem, 1)

                wait_alone(v, gh0_m, l, 16)
                with v.Fori(0, BLOCKS) as b:
                    base = b * 8 + BLOCKS * 8
                    one_hots(l, base, 1, b * P, 0)
                    for j in range(4):
                        v.wait_ge(gh_hi.sem, gh_hi.at(l, b * 4 + (j + 1)))
                        v.tensor_tensor(gh_l[j][:, :], Gs[1][:, b * 4 + j, :], gh_h[j][:, :], ALU.subtract).then_inc(gh_ok.sem, 1)
                    for n in range(1, 3):
                        one_hots(l, base, 1, b * P, n)
                        collect(l, base, Gs[0], b * P, n - 1)
                    for n in range(8):
                        if n >= 2:
                            if n < 7:
                                one_hots(l, base, 1, b * P, n + 1)
                            collect(l, base, Gs[0], b * P, n)
                        add_values(b, n)

                def block(stripe, b, G, G_next):
                    blk = stripe * BLOCKS + b
                    base = blk * 8 + BLOCKS * 8
                    i = (stripe - 1) * BLOCKS + b

                    def routed(j):
                        v.wait_ge(u_ge.sem, u_ge.at(l, i * 4 + (j + 1)))
                        v.wait_ge(G_ok.sem, G_ok.at(l, stripe * (8 * BLOCKS) + 8 * BLOCKS))
                        v.tensor_tensor(gh[j], gh[j], G[:, b * 4 + j, :], ALU.mult).then_inc(gh_m.sem, 1)

                    def routed_low(j):
                        v.wait_ge(gh_hi.sem, gh_hi.at(l, blk * 4 + (j + 1)))
                        v.tensor_tensor(gh_l[j][:, :], gh[j], gh_h[j][:, :], ALU.subtract).then_inc(gh_ok.sem, 1)

                    for j in range(4):
                        if G_next is not None:
                            one_hots(l, base, stripe + 1, b * P, j)
                            if j:
                                collect(l, base, G_next, b * P, j - 1)
                        if j:
                            routed_low(j - 1)
                        routed(j)
                    routed_low(3)
                    for n in range(8):
                        if n % 2 == 0 and G_next is not None:
                            collect(l, base, G_next, b * P, 3 + n // 2)
                            one_hots(l, base, stripe + 1, b * P, 4 + n // 2)
                        add_values(blk, n)
                    if G_next is not None:
                        collect(l, base, G_next, b * P, 7)

                with v.Fori(0, STRIPES // 2 - 1) as sp2:
                    for odd in range(2):
                        with v.Fori(0, BLOCKS) as b:
                            block(sp2 * 2 + (odd + 1), b, Gs[odd], Gs[1 - odd])
                with v.Fori(0, BLOCKS) as b:
                    block(STRIPES - 1, b, Gs[0], None)

            v.wait_ge(f_w, 16)
            v.wait_ge(f_ss, 4)
            v.tensor_scalar(stat[:, 4:8], stat[:, 0:4], 1.0 / D, EPS, ALU.mult, ALU.add).then_inc(f_v, 1)
            v.wait_ge(f_sq, 1)
            v.reciprocal(stat[:, 12:16], stat[:, 8:12]).then_inc(f_v, 1)
            v.wait_ge(f_v, 2)
            for tt in range(NT):
                if tt >= 2:
                    v.wait_ge(f_out, 16 * (tt - 1))
                v.scalar_tensor_tensor(out=fin[tt % 2], in0=x[:, tt, :], scalar=stat[:, 12 + tt:13 + tt], in1=wfin,
                                       op0=ALU.mult, op1=ALU.mult).then_inc(f_ok, 1)


def unit_tiles(w, cols):
    k = w.shape[0] // P
    r = w.reshape(k, P, -1)
    return np.stack([np.ascontiguousarray(r[:, :, c:c + P].transpose(1, 0, 2)).reshape(P, k * P) for c in cols])


def lay_out(i):
    w_in = i["w_in"]
    w_ssd, w_att, w_mrg, w_qry, w_u, par = [], [], [], [], [], []
    for l in range(DEPTH):
        w = w_in[l]
        r = range(GROUPS)
        cols = [[OFF_XBC + D_INNER + g * P, OFF_XBC + D_INNER + (GROUPS + g) * P, OFF_XBC + 2 * g * P,
                 OFF_XBC + (2 * g + 1) * P, 2 * g * P, (2 * g + 1) * P] for g in r]
        w_ssd.append(np.stack([unit_tiles(w, c) for c in cols]))
        cols = [[o + g * 512 + hp * P for g in range(NG) for o in (OFF_Q, OFF_K)]
                + [OFF_V + g * 512 + hp * P for g in range(NG)] for hp in range(4)]
        w_att.append(np.stack([unit_tiles(w, c) for c in cols]))
        m = np.zeros((8, 5, P, UNIT), np.float32)
        for c in range(8):
            m[c, 0:2] = unit_tiles(w, [OFF_GATE + c * P, OFF_GATE + D + c * P])
            m[c, 2] = unit_tiles(i["w_ssd_out"][l][:D], [c * P])[0]
            m[c, 3] = unit_tiles(i["w_ssd_out"][l][D:], [c * P])[0]
            m[c, 4, :, 0:512] = unit_tiles(i["w_attn_out"][l], [c * P])[0]
        w_mrg.append(m)
        w_qry.append(unit_tiles(i["w_query"][l], [n * P for n in range(2 * PH)]).reshape(PH // 2, 4, P, UNIT))
        u = i["expert_u"][l].reshape(EXPERT_TILES, P, KD, P)
        w_u.append(u.transpose(0, 3, 2, 1).reshape(STRIPES * BLOCKS, 4, P, UNIT))
        q = np.zeros((P, PW), np.float32)
        q[:, PW_N1:PW_N1 + KD] = i["norm1_w"][l].reshape(KD, P).T
        q[:, PW_N2:PW_N2 + KD] = i["norm2_w"][l].reshape(KD, P).T
        skip = np.repeat(i["D_skip"][l], HD)
        for g in r:
            for t, ch in enumerate((D_INNER + g * P, D_INNER + (GROUPS + g) * P, 2 * g * P, (2 * g + 1) * P)):
                o = PW_CONV + g * 32 + t * 8
                q[:, o:o + CONV] = i["conv_w"][l][:, ch:ch + P].T
                q[:, o + 5] = i["conv_b"][l][ch:ch + P]
                if t >= 2:
                    q[:, o + 6] = skip[ch:ch + P]
                    q[:, o + 7] = i["ssd_norm_w"][l][ch:ch + P]
        q[:, PW_DTB:PW_DTB + 64] = i["dt_bias"][l].reshape(1, 64)
        q[:, PW_ALOG:PW_ALOG + 64] = i["A_log"][l].reshape(1, 64)
        q[:, PW_KEYS:PW_KEYS + 256] = i["sub_keys"][l].transpose(2, 0, 1).reshape(P, 256)
        q[:, PW_WDT:PW] = w[:, OFF_DT:OFF_Q].reshape(KD, P, 64).transpose(1, 0, 2).reshape(P, KD * 64)
        par.append(q)
    par.append(par[0])
    return {
        "x_prompt": i["x_prompt"], "x_sample": i["x_sample"], "consts": constants(), "biases": bias_constants(),
        "rel": i["rel_bias"], "par": np.stack(par), "w_ssd": np.stack(w_ssd), "w_att": np.stack(w_att),
        "w_mrg": np.stack(w_mrg), "w_out": i["w_out"].reshape(DEPTH, KD, P, D), "w_qry": np.stack(w_qry),
        "w_u": np.stack(w_u), "w_v": i["expert_v"].reshape(DEPTH, STRIPES * BLOCKS, 4, P, D),
        "w_final": i["final_norm_w"],
    }


def kernel(**inputs):
    import numpy as _np
    import concourse.bacc as _bacc
    from concourse.bass_utils import run_bass_kernel_spmd as _run

    nc = _bacc.Bacc("TRN2", target_bir_lowering=False, num_devices=1)
    arrays, args = {}, {}
    for name, a in lay_out({k: _np.asarray(v) for k, v in inputs.items()}).items():
        a = _np.ascontiguousarray(a)
        arrays[f"in_{name}"] = a
        args[name] = nc.dram_tensor(f"in_{name}", a.shape, F32, kind="ExternalInput").ap()
    for name in ("y_prompt", "y_sample"):
        args[name] = nc.dram_tensor(f"out_{name}", (1, SEQ, D), F32, kind="ExternalOutput").ap()
    build(nc, **args)
    r = _run(nc, [arrays], core_ids=[0])
    return tuple(r.results[0][f"out_{n}"] for n in ("y_prompt", "y_sample"))
```
